# Optimizing a Trainium2 kernel written in Bass

```python
import jax, jax.numpy as jnp
from jax import lax
import numpy as np

D_MODEL = 1024
BATCH = 1
SEQ = 256
DEPTH = 2

HEAD_DIM = 64
A_Q_HEADS = 8
A_KV_HEADS = 2
A_GROUP = A_Q_HEADS // A_KV_HEADS
A_WINDOW = 128
A_BLOCK = 128
B_HEADS = 8
GRID_W = 64
NA_KH = 8
NA_KW = 16
RET_HEADS = 8
RET_DK = D_MODEL // RET_HEADS
RET_DV = 2 * D_MODEL // RET_HEADS
RET_CHUNK = 128
D_FF = 4 * D_MODEL
N_EVEN = (DEPTH + 1) // 2
N_ODD = DEPTH // 2
EVEN_SPLITS = (A_Q_HEADS * HEAD_DIM, A_KV_HEADS * HEAD_DIM, A_KV_HEADS * HEAD_DIM,
               B_HEADS * HEAD_DIM, B_HEADS * HEAD_DIM, B_HEADS * HEAD_DIM)
EVEN_IN = sum(EVEN_SPLITS)
EVEN_MIX = (A_Q_HEADS + B_HEADS) * HEAD_DIM
ODD_SPLITS = (RET_HEADS * RET_DK, RET_HEADS * RET_DK, RET_HEADS * RET_DV, RET_HEADS * RET_DV)
ODD_IN = sum(ODD_SPLITS)
ODD_MIX = RET_HEADS * RET_DV
RMS_EPS = 1e-6
GN_EPS = 1e-5


def _split(t, sizes):
    idx = np.cumsum(sizes)[:-1].tolist()
    return jnp.split(t, idx, axis=-1)

def _rmsnorm(x, g):
    xf = x.astype(jnp.float32)
    y = xf * lax.rsqrt(jnp.mean(xf * xf, axis=-1, keepdims=True) + RMS_EPS)
    return (y * g.astype(jnp.float32)).astype(x.dtype)

def _alibi_slopes(n):
    return 2.0 ** (-(8.0 / n) * (jnp.arange(n, dtype=jnp.float32) + 1.0))

def _window_gqa(q, k, v, sink):
    B, S = q.shape[0], q.shape[1]
    nb = S // A_BLOCK
    qb = q.reshape(B, nb, A_BLOCK, A_KV_HEADS, A_GROUP, HEAD_DIM)
    pad = ((0, 0), (A_BLOCK, A_BLOCK), (0, 0), (0, 0))
    kp = jnp.pad(k, pad).reshape(B, nb + 2, A_BLOCK, A_KV_HEADS, HEAD_DIM)
    vp = jnp.pad(v, pad).reshape(B, nb + 2, A_BLOCK, A_KV_HEADS, HEAD_DIM)
    kb = jnp.concatenate([kp[:, :-2], kp[:, 1:-1], kp[:, 2:]], axis=2)
    vb = jnp.concatenate([vp[:, :-2], vp[:, 1:-1], vp[:, 2:]], axis=2)
    s = jnp.einsum('bnqhgd,bnkhd->bnhgqk', qb, kb).astype(jnp.float32) * (HEAD_DIM ** -0.5)
    qi = jnp.arange(A_BLOCK)[:, None]
    kj = jnp.arange(3 * A_BLOCK)[None, :]
    rel = kj - A_BLOCK - qi
    kpos = jnp.arange(nb)[:, None, None] * A_BLOCK + kj[None] - A_BLOCK
    valid = (jnp.abs(rel) <= A_WINDOW)[None] & (kpos >= 0) & (kpos < S)
    slopes = _alibi_slopes(A_Q_HEADS).reshape(A_KV_HEADS, A_GROUP, 1, 1)
    s = s - slopes * jnp.abs(rel).astype(jnp.float32)
    s = jnp.where(valid[None, :, None, None], s, -jnp.inf)
    sk = sink.astype(jnp.float32).reshape(A_KV_HEADS, A_GROUP)[None, None, :, :, None, None]
    m = jnp.maximum(jnp.max(s, axis=-1, keepdims=True), sk)
    p = jnp.exp(s - m)
    p = p / (jnp.sum(p, axis=-1, keepdims=True) + jnp.exp(sk - m))
    o = jnp.einsum('bnhgqk,bnkhd->bnqhgd', p.astype(v.dtype), vb)
    return o.reshape(B, S, A_Q_HEADS * HEAD_DIM)

def _neighbourhood_attn(q, k, v, rpb):
    B, S = q.shape[0], q.shape[1]
    rows = S // GRID_W
    kh = min(NA_KH, rows)
    kw = NA_KW
    qg = q.reshape(B, rows, GRID_W, B_HEADS, HEAD_DIM)
    kg = k.reshape(B, rows, GRID_W, B_HEADS, HEAD_DIM)
    vg = v.reshape(B, rows, GRID_W, B_HEADS, HEAD_DIM)
    qc = jnp.arange(GRID_W)
    cstart = jnp.clip(qc - kw // 2, 0, GRID_W - kw)
    kc = jnp.arange(GRID_W)
    col_valid = (kc[None, :] >= cstart[:, None]) & (kc[None, :] < cstart[:, None] + kw)
    col_idx = jnp.clip(kc[None, :] - qc[:, None] + NA_KW - 1, 0, 2 * NA_KW - 2)
    rpb_f = rpb.astype(jnp.float32)
    scale = HEAD_DIM ** -0.5

    def row_fn(r):
        rstart = jnp.clip(r - kh // 2, 0, rows - kh)
        qr = lax.dynamic_index_in_dim(qg, r, axis=1, keepdims=False)
        kr = lax.dynamic_slice_in_dim(kg, rstart, kh, axis=1)
        vr = lax.dynamic_slice_in_dim(vg, rstart, kh, axis=1)
        s = jnp.einsum('bqhd,brkhd->bhqrk', qr, kr).astype(jnp.float32) * scale
        row_idx = rstart + jnp.arange(kh) - r + NA_KH - 1
        bias = rpb_f[:, row_idx[None, :, None], col_idx[:, None, :]]
        s = jnp.where(col_valid[:, None, :], s + bias, -jnp.inf)
        p = jax.nn.softmax(s.reshape(B, B_HEADS, GRID_W, kh * GRID_W), axis=-1)
        p = p.reshape(B, B_HEADS, GRID_W, kh, GRID_W).astype(v.dtype)
        return jnp.einsum('bhqrk,brkhd->bqhd', p, vr)

    out = lax.map(row_fn, jnp.arange(rows))
    return out.transpose(1, 0, 2, 3, 4).reshape(B, S, B_HEADS * HEAD_DIM)

def _retention_dir(q, k, v, log_gamma, strict):
    B, S, H, dk = q.shape
    dv = v.shape[-1]
    nc = S // RET_CHUNK
    dt = q.dtype

    def chunks(t):
        return t.reshape(B, nc, RET_CHUNK, H, t.shape[-1]).transpose(1, 0, 3, 2, 4)

    lg = log_gamma[:, None]
    pos = jnp.arange(RET_CHUNK, dtype=jnp.float32)
    diff = pos[:, None] - pos[None, :]
    allowed = (diff > 0) if strict else (diff >= 0)
    dmask = jnp.where(allowed[None], jnp.exp(lg[:, :, None] * jnp.maximum(diff, 0.0)[None]), 0.0).astype(dt)
    cross = jnp.exp(lg * (pos + 1.0)).astype(dt)
    zeta = jnp.exp(lg * (RET_CHUNK - 1.0 - pos)).astype(dt)
    chunk_decay = jnp.exp(log_gamma * RET_CHUNK).astype(dt)

    def step(R, inp):
        qc, kc, vc = inp
        a = jnp.einsum('bhid,bhjd->bhij', qc, kc) * dmask
        o = jnp.einsum('bhij,bhjv->bhiv', a, vc) + jnp.einsum('bhid,bhdv->bhiv', qc, R) * cross[:, :, None]
        R = R * chunk_decay[:, None, None] + jnp.einsum('bhjd,bhjv->bhdv', kc * zeta[:, :, None], vc)
        return R, o

    R0 = jnp.zeros((B, H, dk, dv), dt)
    _, o = lax.scan(step, R0, (chunks(q), chunks(k), chunks(v)))
    return o.transpose(1, 0, 3, 2, 4).reshape(B, S, H, dv)

def _even_mixer(x, norm_g, w_in, qn_a, kn_a, sink_a, qn_b, kn_b, rpb_b, w_out):
    B, S, _ = x.shape
    h = _rmsnorm(x, norm_g)
    qa, ka, va, qb, kb, vb = _split(h @ w_in, EVEN_SPLITS)
    qa = _rmsnorm(qa.reshape(B, S, A_KV_HEADS, A_GROUP, HEAD_DIM), qn_a)
    ka = _rmsnorm(ka.reshape(B, S, A_KV_HEADS, HEAD_DIM), kn_a)
    va = va.reshape(B, S, A_KV_HEADS, HEAD_DIM)
    oa = _window_gqa(qa, ka, va, sink_a)
    qb = _rmsnorm(qb.reshape(B, S, B_HEADS, HEAD_DIM), qn_b)
    kb = _rmsnorm(kb.reshape(B, S, B_HEADS, HEAD_DIM), kn_b)
    vb = vb.reshape(B, S, B_HEADS, HEAD_DIM)
    ob = _neighbourhood_attn(qb, kb, vb, rpb_b)
    return jnp.concatenate([oa, ob], axis=-1) @ w_out

def _odd_mixer(x, norm_g, w_in, dec_f, dec_b, gn_g, w_out):
    B, S, _ = x.shape
    h = _rmsnorm(x, norm_g)
    q, k, v, g = _split(h @ w_in, ODD_SPLITS)
    q = q.reshape(B, S, RET_HEADS, RET_DK)
    k = k.reshape(B, S, RET_HEADS, RET_DK) * (RET_DK ** -0.5)
    v = v.reshape(B, S, RET_HEADS, RET_DV)
    lgf = jax.nn.log_sigmoid(dec_f.astype(jnp.float32))
    lgb = jax.nn.log_sigmoid(dec_b.astype(jnp.float32))
    y_f = _retention_dir(q, k, v, lgf, False)
    y_b = jnp.flip(_retention_dir(jnp.flip(q, 1), jnp.flip(k, 1), jnp.flip(v, 1), lgb, True), 1)
    yf = (y_f + y_b).astype(jnp.float32)
    mu = jnp.mean(yf, axis=-1, keepdims=True)
    var = jnp.mean(jnp.square(yf - mu), axis=-1, keepdims=True)
    yn = (yf - mu) * lax.rsqrt(var + GN_EPS) * gn_g.astype(jnp.float32).reshape(RET_HEADS, RET_DV)
    yn = yn.astype(x.dtype).reshape(B, S, ODD_MIX)
    return (jax.nn.silu(g) * yn) @ w_out

def _mlp(x, norm_g, w1, w2):
    h = _rmsnorm(x, norm_g)
    return jnp.square(jax.nn.relu(h @ w1)) @ w2

def first_inputs(seed: int = 0) -> dict:
    key = jax.random.key(seed)
    ks = jax.random.split(key, 20)
    f32 = jnp.float32

    def nrm(k, shape, scale):
        return jax.random.normal(k, shape, f32) * scale

    def gain(k, shape):
        return 1.0 + 0.02 * jax.random.normal(k, shape, f32)

    hr = jnp.arange(RET_HEADS, dtype=f32)
    gamma = 1.0 - 2.0 ** (-5.0 - hr)
    base_logit = jnp.log(gamma) - jnp.log1p(-gamma)
    return {
        'x': nrm(ks[0], (BATCH, SEQ, D_MODEL), 1.0),
        'attn_norm_e': gain(ks[1], (N_EVEN, D_MODEL)),
        'w_in_e': nrm(ks[2], (N_EVEN, D_MODEL, EVEN_IN), D_MODEL ** -0.5),
        'q_norm_a': gain(ks[3], (N_EVEN, HEAD_DIM)),
        'k_norm_a': gain(ks[4], (N_EVEN, HEAD_DIM)),
        'sink_a': nrm(ks[5], (N_EVEN, A_Q_HEADS), 0.5),
        'q_norm_b': gain(ks[6], (N_EVEN, HEAD_DIM)),
        'k_norm_b': gain(ks[7], (N_EVEN, HEAD_DIM)),
        'rpb_b': nrm(ks[8], (N_EVEN, B_HEADS, 2 * NA_KH - 1, 2 * NA_KW - 1), 0.02),
        'w_out_e': nrm(ks[9], (N_EVEN, EVEN_MIX, D_MODEL), EVEN_MIX ** -0.5),
        'ret_norm_o': gain(ks[10], (N_ODD, D_MODEL)),
        'w_in_o': nrm(ks[11], (N_ODD, D_MODEL, ODD_IN), D_MODEL ** -0.5),
        'decay_fwd_o': base_logit[None] + nrm(ks[12], (N_ODD, RET_HEADS), 0.05),
        'decay_bwd_o': base_logit[None] + nrm(ks[13], (N_ODD, RET_HEADS), 0.05),
        'ret_gn_o': gain(ks[14], (N_ODD, ODD_MIX)),
        'w_out_o': nrm(ks[15], (N_ODD, ODD_MIX, D_MODEL), ODD_MIX ** -0.5),
        'mlp_norm': gain(ks[16], (DEPTH, D_MODEL)),
        'w_mlp_in': nrm(ks[17], (DEPTH, D_MODEL, D_FF), D_MODEL ** -0.5),
        'w_mlp_out': nrm(ks[18], (DEPTH, D_FF, D_MODEL), D_FF ** -0.5),
    }

def first_block(x, attn_norm_e, w_in_e, q_norm_a, k_norm_a, sink_a, q_norm_b, k_norm_b, rpb_b, w_out_e,
              ret_norm_o, w_in_o, decay_fwd_o, decay_bwd_o, ret_gn_o, w_out_o,
              mlp_norm, w_mlp_in, w_mlp_out):
    for layer in range(DEPTH):
        i = layer // 2
        if layer % 2 == 0:
            x = x + _even_mixer(x, attn_norm_e[i], w_in_e[i], q_norm_a[i], k_norm_a[i], sink_a[i],
                                q_norm_b[i], k_norm_b[i], rpb_b[i], w_out_e[i])
        else:
            x = x + _odd_mixer(x, ret_norm_o[i], w_in_o[i], decay_fwd_o[i], decay_bwd_o[i],
                               ret_gn_o[i], w_out_o[i])
        x = x + _mlp(x, mlp_norm[layer], w_mlp_in[layer], w_mlp_out[layer])
    return x


DEPTH_2 = 1

MOBA_HEADS = 8
MOBA_BLOCK = 256
MOBA_TOPK = 3
MOBA_Q_CHUNK = 8
DSA_HEADS = 8
DSA_TOPK = 256
DSA_Q_CHUNK = 16
IDX_HEADS = 8
IDX_DIM = 64
MEM_LEN = 256
X_HEADS = 4
X_HEAD_DIM = 128
ROPE_THETA = 10000.0
N_BRANCH = 3
MOBA_W = MOBA_HEADS * HEAD_DIM
DSA_W = DSA_HEADS * HEAD_DIM
X_W = X_HEADS * X_HEAD_DIM
IN_SIZES = (MOBA_W, MOBA_W, MOBA_W, MOBA_W, DSA_W, DSA_W, DSA_W, DSA_W,
            IDX_HEADS * IDX_DIM, IDX_DIM, IDX_HEADS, X_W, X_W, N_BRANCH * D_MODEL)
IN_WIDTH = 4 * MOBA_W + 4 * DSA_W + IDX_HEADS * IDX_DIM + IDX_DIM + IDX_HEADS + 2 * X_W + N_BRANCH * D_MODEL


NEG_INF = -jnp.inf

def rmsnorm(x, g):
    xf = x.astype(jnp.float32)
    y = xf * lax.rsqrt(jnp.mean(xf * xf, axis=-1, keepdims=True) + RMS_EPS)
    return (y * g.astype(jnp.float32)).astype(x.dtype)

def rope(x, pos):
    d = x.shape[-1]
    half = d // 2
    inv = jnp.power(ROPE_THETA, -jnp.arange(half, dtype=jnp.float32) * 2.0 / d)
    ang = pos.astype(jnp.float32)[:, None] * inv[None, :]
    cos = jnp.cos(ang)[None, :, None, :]
    sin = jnp.sin(ang)[None, :, None, :]
    xf = x.astype(jnp.float32)
    x1, x2 = xf[..., :half], xf[..., half:]
    return jnp.concatenate([x1 * cos - x2 * sin, x2 * cos + x1 * sin], axis=-1).astype(x.dtype)

def moba_attention(q, k, v):
    B, S, H, D = q.shape
    nb = -(-S // MOBA_BLOCK)
    sp = nb * MOBA_BLOCK
    padw = ((0, 0), (0, sp - S), (0, 0), (0, 0))
    qp, kp, vp = jnp.pad(q, padw), jnp.pad(k, padw), jnp.pad(v, padw)
    scale = D ** -0.5
    kbh = kp.reshape(B, nb, MOBA_BLOCK, H, D).transpose(0, 3, 1, 2, 4)
    vbh = vp.reshape(B, nb, MOBA_BLOCK, H, D).transpose(0, 3, 1, 2, 4)
    kmean = jnp.mean(kbh.astype(jnp.float32), axis=3)
    gate = jnp.einsum('bshd,bhnd->bshn', qp.astype(jnp.float32), kmean)
    qblk = jnp.arange(sp) // MOBA_BLOCK
    past = jnp.arange(nb)[None, :] < qblk[:, None]
    gate = jnp.where(past[None, :, None, :], gate, NEG_INF)
    n_sel = max(min(MOBA_TOPK, nb - 1), 1)
    top_val, top_idx = lax.top_k(gate, n_sel)
    top_ok = jnp.isfinite(top_val)
    nc = sp // MOBA_Q_CHUNK
    b_ix = jnp.arange(B)[:, None, None, None]
    h_ix = jnp.arange(H)[None, None, :, None]

    def to_chunks(a):
        return a.reshape((B, nc, MOBA_Q_CHUNK) + a.shape[2:]).swapaxes(0, 1)

    def step(args):
        ci, q_c, idx_c, ok_c = args
        t0 = ci * MOBA_Q_CHUNK
        blk_start = (t0 // MOBA_BLOCK) * MOBA_BLOCK
        k_own = lax.dynamic_slice_in_dim(kp, blk_start, MOBA_BLOCK, axis=1)
        v_own = lax.dynamic_slice_in_dim(vp, blk_start, MOBA_BLOCK, axis=1)
        qpos = t0 + jnp.arange(MOBA_Q_CHUNK)
        kpos = blk_start + jnp.arange(MOBA_BLOCK)
        s_own = jnp.einsum('bqhd,bkhd->bhqk', q_c, k_own).astype(jnp.float32) * scale
        s_own = jnp.where((kpos[None, :] <= qpos[:, None])[None, None], s_own, NEG_INF)
        k_sel = kbh[b_ix, h_ix, idx_c]
        v_sel = vbh[b_ix, h_ix, idx_c]
        s_past = jnp.einsum('bqhd,bqhnkd->bhqnk', q_c, k_sel).astype(jnp.float32) * scale
        s_past = jnp.where(ok_c.transpose(0, 2, 1, 3)[..., None], s_past, NEG_INF)
        n_past = n_sel * MOBA_BLOCK
        s_all = jnp.concatenate([s_past.reshape(B, H, MOBA_Q_CHUNK, n_past), s_own], axis=-1)
        p = jax.nn.softmax(s_all, axis=-1).astype(q.dtype)
        p_past = p[..., :n_past].reshape(B, H, MOBA_Q_CHUNK, n_sel, MOBA_BLOCK)
        p_own = p[..., n_past:]
        return (jnp.einsum('bhqnk,bqhnkd->bqhd', p_past, v_sel)
                + jnp.einsum('bhqk,bkhd->bqhd', p_own, v_own))

    outs = lax.map(step, (jnp.arange(nc), to_chunks(qp), to_chunks(top_idx), to_chunks(top_ok)))
    return outs.swapaxes(0, 1).reshape(B, sp, H, D)[:, :S]

def dsa_attention(q, k, v, iq, ik, iw):
    B, S, H, D = q.shape
    k_top = min(DSA_TOPK, S // 4)
    nc = S // DSA_Q_CHUNK
    scale = D ** -0.5
    iscale = IDX_DIM ** -0.5
    wscale = IDX_HEADS ** -0.5
    b_ix = jnp.arange(B)[:, None, None]
    kpos = jnp.arange(S)

    def to_chunks(a):
        return a.reshape((B, nc, DSA_Q_CHUNK) + a.shape[2:]).swapaxes(0, 1)

    def step(args):
        ci, q_c, iq_c, iw_c = args
        qpos = ci * DSA_Q_CHUNK + jnp.arange(DSA_Q_CHUNK)
        logits = jnp.einsum('bqgd,bsd->bqgs', iq_c, ik).astype(jnp.float32) * iscale
        score = jnp.einsum('bqgs,bqg->bqs', jax.nn.relu(logits), iw_c.astype(jnp.float32) * wscale)
        score = jnp.where((kpos[None, :] <= qpos[:, None])[None], score, NEG_INF)
        top_val, top_idx = lax.top_k(score, k_top)
        ok = jnp.isfinite(top_val)
        k_sel = k[b_ix, top_idx]
        v_sel = v[b_ix, top_idx]
        s = jnp.einsum('bqhd,bqkhd->bhqk', q_c, k_sel).astype(jnp.float32) * scale
        s = jnp.where(ok[:, None], s, NEG_INF)
        p = jax.nn.softmax(s, axis=-1).astype(q.dtype)
        return jnp.einsum('bhqk,bqkhd->bqhd', p, v_sel)

    outs = lax.map(step, (jnp.arange(nc), to_chunks(q), to_chunks(iq), to_chunks(iw)))
    return outs.swapaxes(0, 1).reshape(B, S, H, D)

def cross_attention(q, mk, mv):
    scale = q.shape[-1] ** -0.5
    s = jnp.einsum('bshd,bmhd->bhsm', q, mk).astype(jnp.float32) * scale
    p = jax.nn.softmax(s, axis=-1).astype(q.dtype)
    return jnp.einsum('bhsm,bmhd->bshd', p, mv)

def hybrid_layer(x, mem, g_in, w_in, b_merge, g_mem, w_mem_kv, w_up_moba, w_up_dsa, w_up_cross, w_out):
    B, S, _ = x.shape
    pos = jnp.arange(S)
    h = rmsnorm(x, g_in)
    z = h @ w_in
    offs = np.cumsum(IN_SIZES)[:-1].tolist()
    (mq, mk, mv, mg, dq, dk, dv, dg, iq, ik, iw, xq, xg, glog) = jnp.split(z, offs, axis=-1)
    heads = lambda a, n, d: a.reshape(B, S, n, d)
    mq = rope(heads(mq, MOBA_HEADS, HEAD_DIM), pos)
    mk = rope(heads(mk, MOBA_HEADS, HEAD_DIM), pos)
    ya = moba_attention(mq, mk, heads(mv, MOBA_HEADS, HEAD_DIM)).reshape(B, S, MOBA_W)
    ya = (ya * jax.nn.silu(mg)) @ w_up_moba
    dq = rope(heads(dq, DSA_HEADS, HEAD_DIM), pos)
    dk = rope(heads(dk, DSA_HEADS, HEAD_DIM), pos)
    iq = rope(heads(iq, IDX_HEADS, IDX_DIM), pos)
    ik = rope(ik[:, :, None, :], pos)[:, :, 0, :]
    yb = dsa_attention(dq, dk, heads(dv, DSA_HEADS, HEAD_DIM), iq, ik, iw).reshape(B, S, DSA_W)
    yb = (yb * jax.nn.silu(dg)) @ w_up_dsa
    M = mem.shape[1]
    kv = rmsnorm(mem, g_mem) @ w_mem_kv
    xk = kv[..., :X_W].reshape(B, M, X_HEADS, X_HEAD_DIM)
    xv = kv[..., X_W:].reshape(B, M, X_HEADS, X_HEAD_DIM)
    yc = cross_attention(heads(xq, X_HEADS, X_HEAD_DIM), xk, xv).reshape(B, S, X_W)
    yc = (yc * jax.nn.silu(xg)) @ w_up_cross
    gates = jax.nn.sigmoid(glog + b_merge).reshape(B, S, N_BRANCH, D_MODEL)
    u = gates[:, :, 0] * ya + gates[:, :, 1] * yb + gates[:, :, 2] * yc
    return x + u @ w_out

def second_inputs(seed: int = 0) -> dict:
    key = jax.random.key(seed)
    ks = jax.random.split(key, 12)
    f32 = jnp.float32
    nrm = lambda k, shape, s: jax.random.normal(k, shape, f32) * s
    return {
        'x': nrm(ks[0], (BATCH, SEQ, D_MODEL), 1.0),
        'mem': nrm(ks[1], (BATCH, MEM_LEN, D_MODEL), 1.0),
        'g_in': 1.0 + nrm(ks[2], (DEPTH_2, D_MODEL), 0.02),
        'w_in': nrm(ks[3], (DEPTH_2, D_MODEL, IN_WIDTH), D_MODEL ** -0.5),
        'b_merge': nrm(ks[4], (DEPTH_2, N_BRANCH * D_MODEL), 0.1),
        'g_mem': 1.0 + nrm(ks[5], (DEPTH_2, D_MODEL), 0.02),
        'w_mem_kv': nrm(ks[6], (DEPTH_2, D_MODEL, 2 * X_W), D_MODEL ** -0.5),
        'w_up_moba': nrm(ks[7], (DEPTH_2, MOBA_W, D_MODEL), MOBA_W ** -0.5),
        'w_up_dsa': nrm(ks[8], (DEPTH_2, DSA_W, D_MODEL), DSA_W ** -0.5),
        'w_up_cross': nrm(ks[9], (DEPTH_2, X_W, D_MODEL), X_W ** -0.5),
        'w_out': nrm(ks[10], (DEPTH_2, D_MODEL, D_MODEL), D_MODEL ** -0.5),
        'g_final': 1.0 + nrm(ks[11], (D_MODEL,), 0.02),
    }

def second_block(x, mem, g_in, w_in, b_merge, g_mem, w_mem_kv, w_up_moba, w_up_dsa, w_up_cross, w_out, g_final):
    for l in range(DEPTH_2):
        x = hybrid_layer(x, mem, g_in[l], w_in[l], b_merge[l], g_mem[l], w_mem_kv[l],
                         w_up_moba[l], w_up_dsa[l], w_up_cross[l], w_out[l])
    return rmsnorm(x, g_final)


def setup_inputs(seed=0):
    out = dict(first_inputs(seed))
    for name, value in second_inputs(seed + 1).items():
        if name != "x":
            out[name + "_2"] = value
    return out


def reference(
    x, attn_norm_e, w_in_e, q_norm_a, k_norm_a, sink_a, q_norm_b, k_norm_b, rpb_b, w_out_e,
    ret_norm_o, w_in_o, decay_fwd_o, decay_bwd_o, ret_gn_o, w_out_o, mlp_norm, w_mlp_in,
    w_mlp_out, mem_2, g_in_2, w_in_2, b_merge_2, g_mem_2, w_mem_kv_2, w_up_moba_2, w_up_dsa_2,
    w_up_cross_2, w_out_2, g_final_2,
):
    x = first_block(
        x, attn_norm_e, w_in_e, q_norm_a, k_norm_a, sink_a, q_norm_b, k_norm_b, rpb_b, w_out_e,
        ret_norm_o, w_in_o, decay_fwd_o, decay_bwd_o, ret_gn_o, w_out_o, mlp_norm, w_mlp_in,
        w_mlp_out,
    )
    return second_block(
        x, mem_2, g_in_2, w_in_2, b_merge_2, g_mem_2, w_mem_kv_2, w_up_moba_2, w_up_dsa_2,
        w_up_cross_2, w_out_2, g_final_2,
    )


_drawn_inputs = setup_inputs


def setup_inputs(seed=0):
    import zlib

    import numpy as np

    out = dict(_drawn_inputs(seed))
    spreads = {}
    factors = {'attn_norm_e': 5.679,
     'q_norm_a': 8.0,
     'k_norm_a': 8.0,
     'sink_a': 8.0,
     'q_norm_b': 8.0,
     'k_norm_b': 8.0,
     'rpb_b': 8.0,
     'ret_norm_o': 3.434,
     'ret_gn_o': 7.131,
     'mem_2': 3.498,
     'g_in_2': 8.0,
     'b_merge_2': 8.0,
     'g_mem_2': 8.0,
     'w_mem_kv_2': 3.345,
     'w_up_cross_2': 3.334}
    for name, (base, spread) in spreads.items():
        noise = np.random.default_rng([zlib.crc32(name.encode()), seed]).standard_normal(out[name].shape)
        drawn = base * np.exp(spread * noise) if base else spread * noise
        out[name] = __import__('jax').numpy.asarray(drawn.astype(out[name].dtype))
    for name, factor in factors.items():
        out[name] = (out[name] * factor).astype(out[name].dtype)
    return out
```

```python
from contextlib import ExitStack
from collections import deque

import concourse.bass as bass
from concourse import mybir

F32 = mybir.dt.float32
F32R = mybir.dt.float32r
ALU = mybir.AluOpType
ACT = mybir.ActivationFunctionType
AXX = mybir.AxisListType.X

NEG = -1.0e30
LOW = -3.0e38
MARK = -3.3e38
EPS = 1e-6
GN_EPS = 1e-5

G_ATT, G_MLP0, G_RET, G_MLP1, G_IN, G_MEM, G_GN, G_BM, G_QA, G_KA, G_QB, G_KB = (
    0, 8, 16, 24, 32, 40, 48, 64, 88, 89, 90, 91)
NGAIN = 92
R_FIN, R_SINK, R_DF, R_DB = 0, 1024, 1032, 1040
NROW = 1048
C_ID, C_NA, C_MB, C_CA, C_COS, C_SIN, C_U, C_L, C_IS, C_NS = (
    0, 128, 640, 704, 960, 1088, 1216, 1600, 1984, 1992)
NCONST = 2000

NRAW = 4
NSPL = 3
ARENA = 18176


class Eng:

    def __init__(self, sem):
        self.sem, self.ops, self.count, self.seen = sem, [], 0, {}

    def wait(self, *tokens):
        for t in tokens:
            if t is None:
                continue
            if isinstance(t, list):
                self.wait(*t)
                continue
            sem, value = t
            if self.seen.get(sem, 0) < value:
                self.seen[sem] = value
                self.ops.append(lambda e, s=sem, v=value: e.wait_ge(s, v))

    def do(self, fn, *tokens, sig=True):
        self.wait(*tokens)
        if not sig:
            self.ops.append(fn)
            return None
        self.count += 1
        self.ops.append(lambda e: fn(e).then_inc(self.sem, 1))
        return (self.sem, self.count)

    def last(self):
        return (self.sem, self.count) if self.count else None

    def run(self, e):
        for op in self.ops:
            op(e)


class Buf:

    def __init__(self, ap):
        self.ap, self.free, self.ready = ap, [], None

    def part(self, k):
        return self.ready[k] if isinstance(self.ready, dict) else self.ready


def program(nc, A, out):
    with ExitStack() as st:
        def sb(name, n, dt=F32):
            return st.enter_context(nc.sbuf_tensor(name, [128, n], dt))

        raw = [sb(f"raw{i}", 2048) for i in range(NRAW)]
        whi = [sb(f"whi{i}", 2048, F32R) for i in range(NSPL)]
        wlo = [sb(f"wlo{i}", 2048, F32R) for i in range(NSPL)]
        xs = sb("xs", 2048)
        hTh, hTl = sb("hTh", 2048, F32R), sb("hTl", 2048, F32R)
        urh = [sb(f"urh{i}", 1024, F32R) for i in range(2)]
        url = [sb(f"url{i}", 1024, F32R) for i in range(2)]
        arena = sb("arena", ARENA)
        gain = sb("gain", NGAIN)
        rows = sb("rows", NROW)
        cst = sb("cst", NCONST)
        stat = sb("stat", 640)
        lgt = sb("lgt", 128)
        psum = [st.enter_context(nc.psum_tensor(f"ps{i}", [128, 512], F32)) for i in range(8)]
        sems = {n: st.enter_context(nc.semaphore(n)) for n in
                ["s_pe", "s_act", "s_dve", "s_pool", "s_c", "s_id", "s_x0", "s_x1", "s_b", "s_m", "s_out"]
                + [f"s_raw{i}" for i in range(NRAW)]}
        mem = dict(raw=raw, whi=whi, wlo=wlo, xs=xs, hTh=hTh, hTl=hTl, urh=urh, url=url, arena=arena,
                   gain=gain, rows=rows, cst=cst, stat=stat, lgt=lgt, psum=psum)
        order = emit(A, out, mem, sems, None)[0]
        engines = emit(A, out, mem, sems, order)[1]
        block = st.enter_context(nc.Block())
        for name, deco in (("sp", block.sync), ("act", block.scalar), ("dve", block.vector),
                           ("pe", block.tensor), ("pool", block.gpsimd)):
            deco(lambda e, n=name: engines[n].run(e))


def emit(A, out, mem, sems, order):
    S = sems
    sp = Eng(None)
    act, dve, pe, pool = (Eng(S[n]) for n in ("s_act", "s_dve", "s_pe", "s_pool"))
    raw, whi, wlo, xs = mem["raw"], mem["whi"], mem["wlo"], mem["xs"]
    arena, gain, rows, cst, stat, lgt = (mem[n] for n in ("arena", "gain", "rows", "cst", "stat", "lgt"))

    def v3(t, a, off=0, n=None):
        n = n or 2048
        return t[:, off:off + n].rearrange("p (a b) -> p a b", a=a)

    def av(off, n, a=None):
        assert off + n <= ARENA, (off, n)
        r = arena[:, off:off + n]
        return r if a is None else r.rearrange("p (a b) -> p a b", a=a)

    def bc(ap, *shape):
        return ap.broadcast_to(list(shape))

    banks = deque(Buf(t[:, :]) for t in mem["psum"])

    def give(b, *tokens):
        b.free = list(tokens)
        banks.append(b)

    dma_n = {}

    def dma(q, dst, src, sem, *waits):
        dma_n[sem] = dma_n.get(sem, 0) + 16
        q.do(lambda e: e.dma_start(dst, src).then_inc(S[sem], 16), *waits, sig=False)

    used, tiles, done = [], [], []
    state = dict(dma=0, split=0)

    def issue_dma(m):
        name, k0, nk, c0, n = order[m]
        src = A[name][k0:k0 + nk * 128, c0:c0 + n].rearrange("(t p) n -> p t n", p=128)
        dst = raw[m % NRAW][:, 0:nk * n].rearrange("p (t n) -> p t n", t=nk)
        waits = [tiles[m - NRAW]["lo"]] if m >= NRAW else []
        sp.do(lambda e: e.dma_start(dst, src).then_inc(S[f"s_raw{m % NRAW}"], 16), *waits, sig=False)

    def issue_split(m):
        name, k0, nk, c0, n = order[m]
        w = nk * n
        r, h, l = raw[m % NRAW][:, 0:w], whi[m % NSPL][:, 0:w], wlo[m % NSPL][:, 0:w]
        arrived = (S[f"s_raw{m % NRAW}"], 16 * (m // NRAW + 1))
        free = done[m - NSPL] if m >= NSPL else None
        th = act.do(lambda e: e.activation(h, r, ACT.Copy), arrived, free)
        tl = dve.do(lambda e: e.tensor_tensor(l, r, h.bitcast(F32), ALU.subtract), arrived, th, free)
        tiles.append(dict(hi=th, lo=tl, h=h.rearrange("p (t n) -> p t n", t=nk),
                          l=l.rearrange("p (t n) -> p t n", t=nk)))

    def next_tile(*desc):
        n = len(used)
        used.append(desc)
        if order is None:
            z = whi[0][:, 0:desc[2] * desc[4]].rearrange("p (t n) -> p t n", t=desc[2])
            return dict(hi=None, lo=None, h=z, l=z)
        assert order[n] == desc
        while state["split"] < min(n + NSPL, len(order)):
            m = state["split"]
            while state["dma"] < min(m + NRAW, len(order)):
                issue_dma(state["dma"])
                state["dma"] += 1
            issue_split(m)
            state["split"] += 1
        return tiles[n]

    def tile_done(tok):
        done.append(tok)

    def mm3(o, pairs, start, stop, *waits, sig=False):
        t = None
        for i, (a, b) in enumerate(pairs):
            last = i == len(pairs) - 1
            t = pe.do(lambda e, a=a, b=b, s=start and i == 0, p=stop and last:
                      e.matmul(o, a, b, start=s, stop=p), *(waits if i == 0 else ()), sig=sig and last)
        return t

    hT = Buf((v3(mem["hTh"], 8), v3(mem["hTl"], 8)))
    ur = [Buf((v3(h, 4, 0, 1024), v3(l, 4, 0, 1024))) for h, l in zip(mem["urh"], mem["url"])]
    urn = [0]

    def gemm_n(name, c0, n, xT=None):
        xT = xT or hT
        bk = [banks.popleft() for _ in range(2)]
        nk = 4 if n > 256 else 8
        tok = [None, None]
        for k0 in range(0, 8, nk):
            t = next_tile(name, k0 * 128, nk, c0, n)
            for tb in range(2):
                for k in range(nk):
                    kk = k0 + k
                    xh = xT.ap[0][:, kk, tb * 128:tb * 128 + 128]
                    xl = xT.ap[1][:, kk, tb * 128:tb * 128 + 128]
                    end = k == nk - 1
                    w = (bk[tb].free, xT.part(kk), t["hi"], t["lo"])
                    tok[tb] = mm3(bk[tb].ap[:, 0:n], [(xh, t["h"][:, k, :]), (xh, t["l"][:, k, :]), (xl, t["h"][:, k, :])],
                                  kk == 0, kk == 7, *w, sig=end)
            tile_done(tok[1])
        for b, t in zip(bk, tok):
            b.ready = t
        return bk

    def gemm_t(name, c0, n, nk=8, xT=None):
        xT = xT or hT
        t = next_tile(name, 0, nk, c0, n)
        res = []
        for m in range(n // 128):
            if m % 2 == 0:
                b = banks.popleft()
                res.append(b)
            o = b.ap[:, (m % 2) * 256:(m % 2) * 256 + 256]
            for k in range(nk):
                wh, wl = t["h"][:, k, m * 128:m * 128 + 128], t["l"][:, k, m * 128:m * 128 + 128]
                xh, xl = xT.ap[0][:, k, :], xT.ap[1][:, k, :]
                tok = mm3(o, [(wh, xh), (wh, xl), (wl, xh)], k == 0, k == nk - 1,
                          b.free, xT.part(k), t["hi"], t["lo"], sig=k == nk - 1)
            b.ready = tok
        tile_done(tok)
        return res

    def acc_open():
        return [banks.popleft() for _ in range(4)]

    def gemm_acc(acc, name, k0, u, j, first, last):
        t = next_tile(name, k0, 2, 0, 1024)
        for tb in range(2):
            for k in range(2):
                uh = u.ap[0][:, j + k, tb * 128:tb * 128 + 128]
                ul = u.ap[1][:, j + k, tb * 128:tb * 128 + 128]
                s, p = first and k == 0, last and k == 1
                b0, b1 = acc[2 * tb], acc[2 * tb + 1]
                h = [t["h"][:, k, 512 * i:512 * i + 512] for i in range(2)]
                l = [t["l"][:, k, 512 * i:512 * i + 512] for i in range(2)]
                w = (b0.free, b1.free, u.part(j + k), t["hi"], t["lo"])
                mm3(b0.ap, [(uh, h[0])], s, False, *w)
                mm3(b1.ap, [(uh, h[1])], s, False)
                mm3(b0.ap, [(uh, l[0])], False, False)
                mm3(b1.ap, [(uh, l[1])], False, False)
                mm3(b0.ap, [(ul, h[0])], False, p)
                tok = mm3(b1.ap, [(ul, h[1])], False, p, sig=k == 1)
            b0.ready = b1.ready = tok
        tile_done(tok)
        u.free = [tok]
        return tok

    def acc_close(acc, scale=None):
        toks = []
        for tb in range(2):
            for i in range(2):
                b = acc[2 * tb + i]
                o = xs[:, tb * 1024 + i * 512:tb * 1024 + i * 512 + 512]
                if scale:
                    sc, ts = scale[tb]
                    t = dve.do(lambda e, o=o, b=b, sc=sc: e.scalar_tensor_tensor(o, b.ap, sc, o, ALU.mult, ALU.add),
                               b.ready, ts)
                else:
                    t = dve.do(lambda e, o=o, b=b: e.tensor_tensor(o, o, b.ap, ALU.add), b.ready)
                give(b, t)
            toks.append(t)
        return toks

    ident = cst[:, C_ID:C_ID + 128]
    half = stat[:, 0:32]
    stn = [32]

    def stats(n):
        if stn[0] + n > 640:
            stn[0] = 32
        stn[0] += n
        return stat[:, stn[0] - n:stn[0]]

    def boundary():
        ts = [q.last() for q in (act, dve, pe, pool)]
        for q in (act, dve, pe, pool):
            q.wait(*ts)
        stn[0] = 32

    def rstd(ss, n, scale, eps, *waits):
        t = pool.do(lambda e: e.tensor_scalar(ss, ss, scale, eps, ALU.mult, ALU.add), *waits)
        return pool.do(lambda e: e.tensor_tensor(ss, ss, half[:, 0:n], ALU.pow), t)

    def rms_rows(src, dst, ready):
        toks = []
        for tb in range(2):
            ss = stats(1)
            s, d = src[:, tb, :], dst[:, tb, :]
            t = act.do(lambda e, s=s, d=d, ss=ss: e.activation(d, s, ACT.Square, accum_out=ss), ready[tb])
            t = rstd(ss, 1, 1.0 / 1024, EPS, t)
            toks.append(dve.do(lambda e, s=s, d=d, ss=ss: e.tensor_scalar(d, s, ss, None, ALU.mult), t, ready[tb]))
        return toks

    def split_evac(dh, dl, src, scales, *waits):
        for h, s, g in zip(dh, src, scales):
            kw = {} if g is None else dict(scale=g)
            th = act.do(lambda e, h=h, s=s, kw=kw: e.activation(h, s, ACT.Copy, **kw), *waits)
        for h, l, s, g in zip(dh, dl, src, scales):
            if g is None:
                tl = dve.do(lambda e, h=h, l=l, s=s: e.tensor_tensor(l, s, h.bitcast(F32), ALU.subtract), th)
            else:
                tl = dve.do(lambda e, h=h, l=l, s=s, g=g: e.scalar_tensor_tensor(
                    l, s, g, h.bitcast(F32), ALU.mult, ALU.subtract), th)
        return tl

    def to_T(src, dst, kts, d0, gcol, ready, *waits):
        if not isinstance(dst.ready, dict):
            dst.ready = {}
        for i in range(0, len(kts), 2):
            b = banks.popleft()
            for j in range(2):
                for tb in range(2):
                    k = kts[i + j]
                    o = b.ap[:, j * 256 + tb * 128:j * 256 + tb * 128 + 128]
                    s = src[:, tb, k * 128:k * 128 + 128]
                    t = pe.do(lambda e, o=o, s=s: e.transpose(o, s, ident), b.free, ready, s_ident,
                              sig=(j == 1 and tb == 1))
            k, d = kts[i], d0 + i
            if gcol is None:
                tok = split_evac([dst.ap[0][:, d:d + 2, :]], [dst.ap[1][:, d:d + 2, :]],
                                 [b.ap.rearrange("p (a b) -> p a b", a=2)], [None], t, dst.free, *waits)
            else:
                tok = split_evac([dst.ap[0][:, d + j, :] for j in range(2)], [dst.ap[1][:, d + j, :] for j in range(2)],
                                 [b.ap[:, j * 256:j * 256 + 256] for j in range(2)],
                                 [gain[:, gcol + k + j:gcol + k + j + 1] for j in range(2)], t, dst.free, *waits)
            give(b, tok)
            dst.ready[d] = dst.ready[d + 1] = tok
        return tok

    pool.do(lambda e: e.memset(half, -0.5))
    for tb in range(2):
        dma((sp, act)[tb], xs[:, tb * 1024:tb * 1024 + 1024], A["x"][0, tb * 128:tb * 128 + 128, :], f"s_x{tb}")
    dma(act, cst[:, 0:128], A["consts"][:, 0:128], "s_id")
    dma(act, gain[:, :], A["gains"], "s_id")
    s_ident = (S["s_id"], 32)
    s_const = (S["s_c"], 32)
    x3 = v3(xs, 2)

    def norm_to_hT(gcol, ready, hn):
        toks = rms_rows(x3, hn, ready)
        to_T(hn, hT, list(range(8)), 0, gcol, toks)

    NBUF = 2
    scr = {}

    def scratch(off):
        scr["S"] = [Buf(av(off + 512 * i, 512, 2)) for i in range(NBUF)]
        scr["P"] = [Buf(av(off + 512 * (NBUF + i), 512, 2)) for i in range(NBUF)]
        scr["T"] = [Buf(av(off + 512 * (2 * NBUF + i), 512)) for i in range(NBUF)]
        return off + 512 * 3 * NBUF

    def attention(units, kmax, q_of, k_of, v_of, score, hd, per_q, finish, ready):
        n = len(units)
        st2 = {}
        ob = {}
        sums = {}

        def stage1(i):
            qb, hs = units[i]
            nk = kmax[qb]
            if qb not in sums:
                sums[qb] = stats(8)
            b = banks.popleft()
            for j, h in enumerate(hs):
                o = b.ap[:, j * 256:j * 256 + nk]
                t = pe.do(lambda e, o=o, h=h: e.matmul(o, q_of(h, qb), k_of(h, nk), start=True, stop=True),
                          b.free, ready, sig=j == 1)
            Sb, Pb = scr["S"][i % NBUF], scr["P"][i % NBUF]
            src, par, t2, freed = score(qb, hs, b.ap.rearrange("p (a b) -> p a b", a=2)[:, :, 0:nk],
                                        Sb.ap[:, :, 0:nk], (t, Sb.free))
            for j, h in enumerate(hs):
                scl, nm = par[j]
                po, si, ac = Pb.ap[:, j, 0:nk], src[:, j, :], sums[qb][:, h:h + 1]
                t3 = act.do(lambda e, po=po, si=si, ac=ac, scl=scl, nm=nm: e.activation(
                    po, si, ACT.Exp, bias=nm, scale=scl, accum_out=ac), t2, Pb.free)
            if freed is None:
                give(b, t3)
            else:
                give(b, freed)
                Sb.free = [t3]
            Pb.ready = t3

        def stage2(i):
            qb, hs = units[i]
            nk = kmax[qb]
            Pb, Tb = scr["P"][i % NBUF], scr["T"][i % NBUF]
            b = banks.popleft()
            nb = nk // 128
            for j in range(2):
                for kb in range(nb):
                    o = b.ap[:, (j * nb + kb) * 128:(j * nb + kb) * 128 + 128]
                    s = Pb.ap[:, j, kb * 128:kb * 128 + 128]
                    t = pe.do(lambda e, o=o, s=s: e.transpose(o, s, ident), b.free, Pb.ready, s_ident,
                              sig=(j == 1 and kb == nb - 1))
            Pb.free = [t]
            q = act if i % 2 else dve
            w = 2 * nk
            if i % 2:
                t = act.do(lambda e: e.activation(Tb.ap[:, 0:w], b.ap[:, 0:w], ACT.Copy), t, Tb.free)
            else:
                t = dve.do(lambda e: e.tensor_copy(Tb.ap[:, 0:w], b.ap[:, 0:w]), t, Tb.free)
            give(b, t)
            Tb.ready = t

        def stage3(i):
            qb, hs = units[i]
            nb = kmax[qb] // 128
            Tb = scr["T"][i % NBUF]
            if qb not in ob:
                ob[qb] = banks.popleft()
            b = ob[qb]
            for j, h in enumerate(hs):
                for kb in range(nb):
                    o = b.ap[:, h * hd:h * hd + hd]
                    s = Tb.ap[:, (j * nb + kb) * 128:(j * nb + kb) * 128 + 128]
                    t = pe.do(lambda e, o=o, s=s, kb=kb, h=h: e.matmul(o, s, v_of(h, kb), start=kb == 0, stop=kb == nb - 1),
                              b.free, Tb.ready, ready, sig=(j == 1 and kb == nb - 1))
            Tb.free = [t]
            b.ready = t
            if i == n - 1 or units[i + 1][0] != qb:
                finish(qb, b, sums[qb])

        for i in range(n + 2):
            if i < n:
                stage1(i)
            if 0 <= i - 1 < n:
                stage2(i - 1)
            if 0 <= i - 2 < n:
                stage3(i - 2)
            yield

    PAIRS = [(0, 2), (1, 3), (4, 6), (5, 7)]
    U8 = [(qb, hs) for qb in range(2) for hs in PAIRS]
    U4 = [(qb, hs) for qb in range(2) for hs in ((0, 1), (2, 3))]

    def qT_of(qT):
        return lambda h, qb: qT[(h % 2) * 64:(h % 2) * 64 + 64, h // 2, qb * 128:qb * 128 + 128]

    def kT_of(kT):
        return lambda h, nk: kT[(h % 2) * 64:(h % 2) * 64 + 64, h // 2, 0:nk]

    def soft_common(biased):
        def score(qb, hs, bank, Sb, waits):
            nm = stats(2)
            tab = biased["tab"](qb, hs) if biased["tab"] else None
            c = biased["scale"]
            if tab is None:
                t = dve.do(lambda e: e.tensor_reduce(nm, bank, AXX, ALU.max, negate=True), waits[0])
                t = dve.do(lambda e: e.tensor_scalar(nm, nm, c, None, ALU.mult), t)
                return bank, [(c, nm[:, 0:1]), (c, nm[:, 1:2])], t, None
            t = dve.do(lambda e: e.scalar_tensor_tensor(Sb, bank, c, tab, ALU.mult, ALU.add),
                       *waits, biased["ready"])
            f = t
            t = dve.do(lambda e: e.tensor_reduce(nm, Sb, AXX, ALU.max, negate=True), t)
            return Sb, [(1.0, nm[:, 0:1]), (1.0, nm[:, 1:2])], t, f
        return score

    def norm_out(dst_of, nh=8, extra=None, mul=None):
        toks = {}

        def finish(qb, b, sm):
            r = stats(8)
            t = act.last()
            if extra:
                t = extra(qb, sm, t)
            t = dve.do(lambda e: e.reciprocal(r[:, 0:nh], sm[:, 0:nh]), t)
            hd = 512 // nh
            o3 = b.ap.rearrange("p (h d) -> p h d", h=nh)
            d = dst_of(qb)
            d3 = d.rearrange("p (h d) -> p h d", h=nh)
            rb = bc(r[:, 0:nh].unsqueeze(2), 128, nh, hd)
            t = dve.do(lambda e: e.tensor_tensor(d3, o3, rb, ALU.mult), t, b.ready)
            give(b, t)
            if mul:
                m, mr = mul(qb)
                t = dve.do(lambda e: e.tensor_tensor(d, d, m, ALU.mult), t, mr)
            toks[qb] = t
        return finish, toks

    def drive(*gens):
        gens = list(gens)
        while gens:
            for g in list(gens):
                try:
                    next(g)
                except StopIteration:
                    gens.remove(g)

    AQT, AKT, BQT, BKT, AV, BV, BB, OS = 0, 1024, 1536, 2560, 3584, 3840, 4864, 8960
    o = scratch(11008)
    SQ = [Buf(av(o + 512 * i, 512)) for i in range(2)]
    QN = [Buf(av(o + 1024 + 512 * i, 512)) for i in range(2)]
    aqT, akT, bqT, bkT = av(AQT, 1024, 4), av(AKT, 512, 2), av(BQT, 1024, 4), av(BKT, 1024, 4)
    avv, bvv = av(AV, 256, 2), av(BV, 1024, 2)
    biasB = av(BB, 4096)
    osb = av(OS, 2048, 2)

    norm_to_hT(G_ATT, [(S["s_x0"], 16), (S["s_x1"], 16)], osb)
    dma(act, cst[:, 128:NCONST], A["consts"][:, 128:NCONST], "s_c")
    dma(act, rows[:, :], bass.AP(A["rowvec"].tensor, 0, [[0, 128], [1, NROW]]), "s_c")
    for qr in range(4):
        dst = biasB[(qr % 2) * 64:(qr % 2) * 64 + 64, (qr // 2) * 2048:(qr // 2) * 2048 + 2048]
        src = A["rpb"].rearrange("q (h r) k -> q h (r k)", h=8)[:, :, (3 - qr) * 64:(7 - qr) * 64]
        dma(act, dst.rearrange("p (h c) -> p h c", h=8), src, "s_b")
    m3 = biasB.rearrange("p (a c) -> p a c", c=64)
    invs, negs = cst[:, C_IS:C_IS + 8], cst[:, C_NS:C_NS + 8]
    skp = lgt[:, 0:8]
    t_skp = pool.do(lambda e: e.tensor_tensor(skp, rows[:, R_SINK:R_SINK + 8], invs, ALU.mult), s_const)


    pend = []

    def run_pend():
        for f in pend:
            f()
        pend.clear()

    cnt = [0]

    def head_norm(b, tb, c0, nh, gcol, dst, dup=False):
        w = nh * 64
        i = cnt[0] % 2
        cnt[0] += 1
        sq, qn = SQ[i], QN[i]
        src = b.ap[:, c0:c0 + w]
        ss = stats(nh)
        t0 = act.do(lambda e, w=w: e.activation(sq.ap[:, 0:w], src, ACT.Square), b.ready, sq.free)
        t1 = dve.do(lambda e, w=w: e.tensor_reduce(ss, sq.ap[:, 0:w].rearrange("p (h d) -> p h d", d=64), AXX, ALU.add), t0)
        sq.free = [t1]
        t2 = rstd(ss, nh, 1.0 / 64, EPS, t1)
        s3 = src.rearrange("p (h d) -> p h d", d=64)
        if dup:
            q4 = qn.ap[:, 0:2 * w].rearrange("p (h r d) -> p h r d", h=nh, r=2)
            for r in range(2):
                t3 = dve.do(lambda e, r=r: e.tensor_tensor(q4[:, :, r, :], s3, bc(ss.unsqueeze(2), 128, nh, 64), ALU.mult),
                            t2, b.ready, qn.free)
            w *= 2
        else:
            q3 = qn.ap[:, 0:w].rearrange("p (h d) -> p h d", d=64)
            t3 = dve.do(lambda e: e.tensor_tensor(q3, s3, bc(ss.unsqueeze(2), 128, nh, 64), ALU.mult),
                        t2, b.ready, qn.free)
        nb = w // 128

        def later():
            tbk = banks.popleft()
            for j in range(nb):
                t = pe.do(lambda e, j=j: e.transpose(tbk.ap[:, j * 128:j * 128 + 128], qn.ap[:, j * 128:j * 128 + 128], ident),
                          tbk.free, t3, s_ident, sig=j == nb - 1)
            qn.free = [t]
            d = dst[:, 0:nb, tb * 128:tb * 128 + 128]
            s = tbk.ap[:, 0:nb * 128].rearrange("p (a b) -> p a b", a=nb)
            t = act.do(lambda e: e.activation(d, s, ACT.Copy, scale=gain[:, gcol:gcol + 1]), t)
            give(tbk, t)
        pend.append(later)
        return t3

    def plain_evac(b, c0, w, d, which):
        s = b.ap[:, c0:c0 + w]
        if which:
            return act.do(lambda e: e.activation(d, s, ACT.Copy), b.ready)
        return dve.do(lambda e: e.tensor_copy(d, s), b.ready)

    W = "w_in_e"

    def g_heads(c0, gc, dst):
        bk = gemm_n(W, c0, 512)
        run_pend()
        for tb in range(2):
            give(bk[tb], head_norm(bk[tb], tb, 0, 8, gc, dst))

    g_heads(0, G_QA, aqT)
    bk = gemm_n(W, 512, 256)
    run_pend()
    for tb in range(2):
        t = head_norm(bk[tb], tb, 0, 2, G_KA, akT, dup=True)
        t = dve.do(lambda e, tb=tb, b=bk[tb]: e.tensor_copy(avv[:, tb, :], b.ap[:, 128:256]), t)
        give(bk[tb], t)
    g_heads(768, G_QB, bqT)
    readyA = [act.last(), dve.last()]
    bT = {}

    def rest_b():
        g_heads(1280, G_KB, bkT)
        bT["bias"] = pool.do(lambda e: e.tensor_tensor(m3, m3, bc(cst[:, C_MB:C_MB + 64].unsqueeze(1), 128, 64, 64), ALU.add),
                             (S["s_b"], dma_n["s_b"]), s_const)
        yield
        yield
        bk = gemm_n(W, 1792, 512)
        run_pend()
        for tb in range(2):
            t = plain_evac(bk[tb], 0, 512, bvv[:, tb, :], tb)
            give(bk[tb], t)
        bT["ready"] = [act.last(), dve.last()]
        yield

    slope = [2.0 ** -(h + 1) for h in range(8)]
    negabs = v3(cst, 2, C_NA, 512)
    nmA = [stats(8), stats(8)]

    def scoreA(qb, hs, bank, Sb, waits):
        mx = stats(2)
        for j, h in enumerate(hs):
            t = dve.do(lambda e, j=j, h=h: e.scalar_tensor_tensor(
                Sb[:, j, :], bank[:, j, :], 0.125 / slope[h], negabs[:, qb, :], ALU.mult, ALU.add), *waits, s_const)
        f = t
        t = dve.do(lambda e: e.tensor_reduce(mx, Sb, AXX, ALU.max), t)
        hsl = slice(hs[0], hs[1] + 1, hs[1] - hs[0])
        nm = nmA[qb][:, hsl]
        t = dve.do(lambda e: e.tensor_tensor(mx, mx, skp[:, hsl], ALU.max), t, t_skp)
        t = dve.do(lambda e: e.tensor_tensor(nm, mx, negs[:, hsl], ALU.mult), t)
        return Sb, [(slope[h], nmA[qb][:, h:h + 1]) for h in hs], t, f

    def extraA(qb, sm, t):
        es = stats(8)
        t1 = dve.do(lambda e: e.tensor_tensor(es, rows[:, R_SINK:R_SINK + 8], nmA[qb], ALU.add), t)
        t1 = act.do(lambda e: e.activation(es, es, ACT.Exp), t1)
        return dve.do(lambda e: e.tensor_tensor(sm, sm, es, ALU.add), t1, t)

    finA, tokA = norm_out(lambda qb: osb[:, qb, 0:512], extra=extraA)
    finB, tokB = norm_out(lambda qb: osb[:, qb, 512:1024])
    bias5 = biasB.rearrange("p (q h k) -> p q h k", q=2, h=8)
    kAT = lambda h, nk: akT[(h % 2) * 64:(h % 2) * 64 + 64, h // 4, 0:nk]
    drive(attention(U8, [256, 256], qT_of(aqT), kAT, lambda h, kb: avv[:, kb, (h // 4) * 64:(h // 4) * 64 + 64],
                    scoreA, 64, None, finA, readyA), rest_b())
    cfgB = dict(scale=0.125, tab=lambda qb, hs: bias5[:, qb, hs[0]:hs[1] + 1:hs[1] - hs[0], :], ready=bT["bias"])

    def out_half(acc, name, src, g, ready):
        u = ur[urn[0] % 2]
        urn[0] += 1
        to_T(src, u, list(range(4 * g, 4 * g + 4)), 0, None, ready)
        for j in range(2):
            yield
            gemm_acc(acc, name, (4 * g + 2 * j) * 128, u, 2 * j, g == 0 and j == 0, g == 1 and j == 1)

    acc = acc_open()
    drive(attention(U8, [256, 256], qT_of(bqT), kT_of(bkT), lambda h, kb: bvv[:, kb, h * 64:h * 64 + 64],
                    soft_common(cfgB), 64, None, finB, bT["ready"]),
          out_half(acc, "w_out_e", osb, 0, list(tokA.values())))
    drive(out_half(acc, "w_out_e", osb, 1, list(tokB.values())))
    xr = acc_close(acc)

    def mlp(layer, gcol, xr, during=None):
        boundary()
        hn = av(0, 2048, 2)
        RL = [Buf(av(2048 + 512 * i, 512)) for i in range(2)]
        SQ2 = [Buf(av(3072 + 512 * i, 512)) for i in range(2)]
        to_T(x3, hT, list(range(8)), 0, gcol, xr)
        inv = []
        for tb in range(2):
            ss = stats(1)
            t = act.do(lambda e, tb=tb, ss=ss: e.activation(hn[:, tb, :], x3[:, tb, :], ACT.Square, accum_out=ss), xr[tb])
            t = pool.do(lambda e, ss=ss: e.tensor_scalar(ss, ss, 1.0 / 1024, EPS, ALU.mult, ALU.add), t)
            inv.append((ss, dve.do(lambda e, ss=ss: e.reciprocal(ss, ss), t)))
        if during:
            during = during()
        acc = acc_open()
        w1, w2 = f"w1_{layer}", f"w2_{layer}"
        slots = []
        for j in range(17):
            if j < 16:
                b, = gemm_t(w1, j * 256, 256)
                rl, sq = RL[j % 2], SQ2[j % 2]
                u, off = ur[(j // 2) % 2], 2 * (j % 2)
                t = act.do(lambda e, b=b, rl=rl: e.activation(rl.ap, b.ap, ACT.Relu), b.ready, rl.free)
                give(b, t)
                t = dve.do(lambda e, rl=rl, sq=sq: e.tensor_tensor(sq.ap, rl.ap, rl.ap, ALU.mult), t, sq.free)
                rl.free = [t]
                s3 = sq.ap.rearrange("p (a b) -> p a b", a=2)
                dh, dl = u.ap[0][:, off:off + 2, :], u.ap[1][:, off:off + 2, :]
                th = act.do(lambda e, dh=dh, s3=s3: e.activation(dh, s3, ACT.Copy), t, u.free)
                t = dve.do(lambda e, dl=dl, dh=dh, s3=s3: e.tensor_tensor(dl, s3, dh.bitcast(F32), ALU.subtract), th, u.free)
                sq.free = [t]
                if not isinstance(u.ready, dict):
                    u.ready = {}
                u.ready[off] = u.ready[off + 1] = t
                slots.append((u, off))
            if j >= 1:
                u, off = slots[j - 1]
                gemm_acc(acc, w2, (j - 1) * 256, u, off, j == 1, j == 16)
            if during and j > 2:
                next(during, None)
        return acc_close(acc, inv)

    DT = 15104
    dtab = av(DT, 3072, 8)

    def decays():
        d = rows[:, R_DF:R_DF + 16]
        a = [lgt[:, 16 * i:16 * i + 16] for i in range(1, 8)]
        ad, e_, s_, s2, pl, lo, t1 = a
        p = pool
        t = p.do(lambda e: e.tensor_scalar(ad, d, -1.0, None, ALU.mult), s_const)
        t = dve.do(lambda e: e.tensor_tensor(ad, ad, d, ALU.min), t)
        t = act.do(lambda e: e.activation(e_, ad, ACT.Exp), t)
        t = p.do(lambda e: e.tensor_scalar(t1, e_, 2.0, None, ALU.add), t)
        t = dve.do(lambda e: e.reciprocal(t1, t1), t)
        t = p.do(lambda e: e.tensor_tensor(s_, e_, t1, ALU.mult), t)
        t = p.do(lambda e: e.tensor_tensor(s2, s_, s_, ALU.mult), t)
        t = p.do(lambda e: e.tensor_scalar(pl, s2, 1.0 / 19, 1.0 / 17, ALU.mult, ALU.add), t)
        for n in (15, 13, 11, 9, 7, 5, 3, 1):
            t = p.do(lambda e: e.tensor_tensor(pl, pl, s2, ALU.mult), t)
            t = p.do(lambda e, n=n: e.tensor_scalar(pl, pl, 1.0 / n, None, ALU.add), t)
        t = p.do(lambda e: e.tensor_tensor(pl, pl, s_, ALU.mult), t)
        t = p.do(lambda e: e.tensor_scalar(pl, pl, 2.0, None, ALU.mult), t)
        t = p.do(lambda e: e.tensor_scalar(lo, d, 0.0, None, ALU.min), t)
        t = p.do(lambda e: e.tensor_tensor(lo, lo, pl, ALU.subtract), t)
        uu, ll = cst[:, C_U:C_U + 384], cst[:, C_L:C_L + 384]
        tmp = av(4096, 3072, 8)
        for h in range(8):
            p.do(lambda e, h=h: e.tensor_scalar(dtab[:, h, :], uu, lo[:, h:h + 1], None, ALU.mult), t)
            t2 = p.do(lambda e, h=h: e.tensor_scalar(tmp[:, h, :], ll, lo[:, 8 + h:9 + h], None, ALU.mult), t)
        t2 = p.do(lambda e: e.tensor_tensor(dtab, dtab, tmp, ALU.add), t2)
        for _ in range(10):
            yield
        for h in range(4):
            dd = dtab[:, 2 * h:2 * h + 2, :]
            td.append(act.do(lambda e, dd=dd: e.activation(dd, dd, ACT.Exp), t2))
            yield

    td = []
    xr = mlp(0, G_MLP0, xr, decays)
    t_dtab = td[-1]
    assert len(td) == 4

    boundary()
    OQ, OK_, OV, OY, OX = 0, 2048, 4096, 8192, 12288
    oqT, okT = av(OQ, 2048, 8), av(OK_, 2048, 8)
    ov, oy = av(OV, 4096, 2), av(OY, 4096, 2)
    ATs = [Buf(av(OX + 512 * i, 512, 2)) for i in range(2)]
    GT = [Buf(av(OX + 1024 + 512 * i, 512)) for i in range(2)]
    norm_to_hT(G_RET, xr, av(OY, 2048, 2))
    W = "w_in_o"
    for base, dst in ((0, oqT), (1024, okT)):
        for c in range(4):
            b, = gemm_t(W, base + c * 256, 256)
            d = dst[:, 2 * c:2 * c + 2, :]
            s = b.ap.rearrange("p (a b) -> p a b", a=2)
            if c % 2:
                t = act.do(lambda e, d=d, s=s: e.activation(d, s, ACT.Copy), b.ready)
            else:
                t = dve.do(lambda e, d=d, s=s: e.tensor_copy(d, s), b.ready)
            give(b, t)
    vtok = []
    for c in range(4):
        bk = gemm_n(W, 2048 + 512 * c, 512)
        for tb in range(2):
            t = plain_evac(bk[tb], 0, 512, ov[:, tb, 512 * c:512 * c + 512], tb)
            give(bk[tb], t)
        vtok.append([act.last(), dve.last()])
    ytok = {}

    def retention():
        kscale = float(128 ** -0.5)

        def sc(h):
            b = banks.popleft()
            for jb in range(2):
                o = b.ap[:, jb * 256:jb * 256 + 256]
                t = pe.do(lambda e, o=o, jb=jb, h=h: e.matmul(o, okT[:, h, jb * 128:jb * 128 + 128], oqT[:, h, :],
                                                             start=True, stop=True), b.free, vtok[0], sig=jb == 1)
            a = ATs[h % 2]
            for jb in range(2):
                dd = dtab[:, h, 128 - jb * 128:128 - jb * 128 + 256]
                t2 = dve.do(lambda e, jb=jb, a=a, b=b, dd=dd: e.scalar_tensor_tensor(
                    a.ap[:, jb, :], b.ap[:, jb * 256:jb * 256 + 256], kscale, dd, ALU.mult, ALU.mult), t, a.free, t_dtab)
            a.ready = t2
            give(b, t2)

        def pv(h):
            a = ATs[h % 2]
            b = banks.popleft()
            for ib in range(2):
                for jb in range(2):
                    o = b.ap[:, ib * 256:ib * 256 + 256]
                    t = pe.do(lambda e, o=o, ib=ib, jb=jb, h=h, a=a: e.matmul(
                        o, a.ap[:, jb, ib * 128:ib * 128 + 128], ov[:, jb, h * 256:h * 256 + 256],
                        start=jb == 0, stop=jb == 1), b.free, a.ready, vtok[h // 2], sig=(ib == 1 and jb == 1))
            a.free = [t]
            st6, mv = stats(12), stats(4)
            for ib in range(2):
                t1 = dve.do(lambda e, ib=ib, st6=st6, b=b: e.bn_stats(st6[:, ib * 6:ib * 6 + 6], b.ap[:, ib * 256:ib * 256 + 256]), t)
            for ib in range(2):
                t1 = dve.do(lambda e, ib=ib, st6=st6, mv=mv: e.bn_aggr(mv[:, 2 * ib:2 * ib + 2], st6[:, ib * 6:ib * 6 + 6]), t1)
            t1 = rstd(mv[:, 1:4:2], 2, 1.0, GN_EPS, t1)
            for ib in range(2):
                t1 = dve.do(lambda e, ib=ib, mv=mv, b=b, h=h: e.tensor_scalar(
                    oy[:, ib, h * 256:h * 256 + 256], b.ap[:, ib * 256:ib * 256 + 256],
                    mv[:, 2 * ib:2 * ib + 1], mv[:, 2 * ib + 1:2 * ib + 2], ALU.subtract, ALU.mult), t1)
            give(b, t1)
            ytok[h] = t1

        for h in range(9):
            if h < 8:
                sc(h)
            if h >= 1:
                pv(h - 1)
            yield

    acc = acc_open()
    gen = retention()
    for _ in range(3):
        next(gen)
    utok = {}
    for c in range(5):
        if c < 4:
            bk = gemm_n(W, 4096 + 512 * c, 512)
            for tb in range(2):
                g = GT[tb]
                b = bk[tb]
                t = act.do(lambda e, g=g, b=b: e.activation(g.ap, b.ap, ACT.Tanh, scale=0.5), b.ready, g.free)
                t = dve.do(lambda e, g=g, b=b: e.scalar_tensor_tensor(g.ap, g.ap, 1.0, b.ap, ALU.add, ALU.mult), t)
                give(b, t)
                y = oy[:, tb, 512 * c:512 * c + 512]
                t = dve.do(lambda e, g=g, y=y: e.scalar_tensor_tensor(y, g.ap, 0.5, y, ALU.mult, ALU.mult), t,
                           ytok[2 * c], ytok[2 * c + 1])
                g.free = [t]
                utok[(c, tb)] = t
            for _ in range(2):
                next(gen, None)
        if c >= 1:
            k = c - 1
            u = ur[k % 2]
            to_T(oy, u, list(range(4 * k, 4 * k + 4)), 0, G_GN, [utok[(k, 0)], utok[(k, 1)]])
            for j in range(2):
                gemm_acc(acc, "w_out_o", (4 * k + 2 * j) * 128, u, 2 * j, k == 0 and j == 0, k == 3 and j == 1)
    for _ in gen:
        pass
    xr = acc_close(acc)

    DQ, DK, DV, MQ, MK, MV, XQ, XK, XV, SG, DM, IQ, UU, TT = (
        0, 1024, 2048, 3072, 4096, 5120, 6144, 7168, 8192, 9216, 12288, 3072, 0, 1024)
    MEMN = 6144
    memn = av(MEMN, 2048, 2)
    mr = []

    def mem_rows():
        dma(sp, memn, A["mem"].rearrange("a (t p) n -> p (a t) n", p=128), "s_m", act.last(), dve.last(), pe.last(), pool.last())
        sqb = av(8192, 2048, 2)
        yield
        for tb in range(2):
            ss = lgt[:, 8 + tb:9 + tb]
            t = act.do(lambda e, tb=tb, ss=ss: e.activation(sqb[:, tb, :], memn[:, tb, :], ACT.Square, accum_out=ss), (S["s_m"], 16))
            t = rstd(ss, 1, 1.0 / 1024, EPS, t)
            yield
            mr.append(dve.do(lambda e, tb=tb, ss=ss: e.tensor_scalar(memn[:, tb, :], memn[:, tb, :], ss, None, ALU.mult), t))

    xr = mlp(1, G_MLP1, xr, mem_rows)

    boundary()
    dqT, dkT, dv = av(DQ, 1024, 4), av(DK, 1024, 4), av(DV, 1024, 2)
    mqT, mkT, mvv = av(MQ, 1024, 4), av(MK, 1024, 4), av(MV, 1024, 2)
    iqT, ikT = av(MQ, 1024, 4), av(MK, 256)
    xqT, xkT, xv = av(XQ, 1024, 4), av(XK, 1024, 4), av(XV, 1024, 2)
    sg = [av(SG + 1024 * i, 1024, 2) for i in range(3)]
    msk = av(DM, 512, 2)
    o = scratch(12800)
    R1 = [Buf(av(o + 512 * i, 512)) for i in range(2)]
    R2 = [Buf(av(o + 1024 + 512 * i, 512)) for i in range(2)]
    o += 2048
    iwt = av(o, 16, 2)
    hnx = av(SG, 2048, 2)
    to_T(memn, hT, list(range(8)), 0, G_MEM, mr)
    for c in range(2):
        b, = gemm_t("w_mem", c * 256, 256)
        t = act.do(lambda e, b=b, c=c: e.activation(xkT[:, 2 * c:2 * c + 2, :], b.ap.rearrange("p (a b) -> p a b", a=2), ACT.Copy),
                   b.ready, list(hT.ready.values()))
        give(b, t)
    bk = gemm_n("w_mem", 512, 512)
    for tb in range(2):
        give(bk[tb], plain_evac(bk[tb], 0, 512, xv[:, tb, :], tb))
    hT.free = [bk[1].ready]
    norm_to_hT(G_IN, xr, hnx)

    cos, sin = v3(cst, 2, C_COS, 128), v3(cst, 2, C_SIN, 128)
    rc = [0]

    def rope(b, tb, c0, nh, dst, dup=False):
        i = rc[0] % 2
        rc[0] += 1
        r1, r2 = R1[i], R2[i]
        w = nh * 64
        src = b.ap[:, c0:c0 + w].rearrange("p (h d) -> p h d", d=64)
        a = r1.ap[:, 0:w].rearrange("p (h d) -> p h d", d=64)
        c = r2.ap[:, 0:w].rearrange("p (h d) -> p h d", d=64)
        ct, s_t = cos[:, tb, :], sin[:, tb, :]
        t1 = dve.do(lambda e: e.tensor_tensor(a, src, bc(ct.unsqueeze(1), 128, nh, 64), ALU.mult), b.ready, r1.free)
        for q in range(2):
            t2 = dve.do(lambda e, q=q: e.tensor_tensor(c[:, :, q * 32:q * 32 + 32], src[:, :, 32 - q * 32:64 - q * 32],
                                                      bc(s_t[:, q * 32:q * 32 + 32].unsqueeze(1), 128, nh, 32), ALU.mult),
                        b.ready, r2.free)
        if dup:
            pool.do(lambda e: e.tensor_tensor(r2.ap[:, 64:128], r1.ap[:, 0:64], r2.ap[:, 0:64], ALU.add), t1, t2)
            t3 = pool.do(lambda e: e.tensor_tensor(r1.ap[:, 0:64], r1.ap[:, 0:64], r2.ap[:, 0:64], ALU.add), t1, t2)
            t3 = pool.do(lambda e: e.tensor_copy(r1.ap[:, 64:128], r2.ap[:, 64:128]), t3)
            w = 128
        else:
            t3 = pool.do(lambda e: e.tensor_tensor(r1.ap[:, 0:w], r1.ap[:, 0:w], r2.ap[:, 0:w], ALU.add), t1, t2)
        r2.free = [t3]
        nb = w // 128

        def later():
            tbk = banks.popleft()
            for j in range(nb):
                t = pe.do(lambda e, j=j: e.transpose(tbk.ap[:, j * 128:j * 128 + 128], r1.ap[:, j * 128:j * 128 + 128], ident),
                          tbk.free, t3, s_ident, sig=j == nb - 1)
            r1.free = [t]
            d = dst[:, 0:nb, tb * 128:tb * 128 + 128]
            s = tbk.ap[:, 0:nb * 128].rearrange("p (a b) -> p a b", a=nb)
            give(tbk, act.do(lambda e: e.activation(d, s, ACT.Copy), t))
        pend.append(later)
        return t2

    W = "w_in_2"

    def g_rope(c0, dst):
        bk = gemm_n(W, c0, 512)
        run_pend()
        for tb in range(2):
            give(bk[tb], rope(bk[tb], tb, 0, 8, dst))

    def g_plain(c0, dst):
        bk = gemm_n(W, c0, 512)
        run_pend()
        for tb in range(2):
            give(bk[tb], plain_evac(bk[tb], 0, 512, dst[:, tb, :], tb))

    def g_silu(c0, dst):
        bk = gemm_n(W, c0, 512)
        run_pend()
        for tb in range(2):
            b, d = bk[tb], dst[:, tb, :]
            t = act.do(lambda e, b=b, d=d: e.activation(d, b.ap, ACT.Tanh, scale=0.5), b.ready, list(hT.ready.values()))
            t = dve.do(lambda e, b=b, d=d: e.scalar_tensor_tensor(d, d, 1.0, b.ap, ALU.add, ALU.mult), t)
            give(b, t)
            t = dve.do(lambda e, d=d: e.tensor_scalar(d, d, 0.5, None, ALU.mult), t)
        return t

    g_rope(4096, iqT)
    bk = gemm_n(W, 4608, 72)
    run_pend()
    for tb in range(2):
        t = rope(bk[tb], tb, 0, 1, ikT.rearrange("p (a b) -> p a b", a=1), dup=True)
        t = dve.do(lambda e, tb=tb, b=bk[tb]: e.tensor_scalar(iwt[:, tb, :], b.ap[:, 64:72], float(8 ** -0.5), 0.125, ALU.mult, ALU.mult), t)
        give(bk[tb], t)
    t_iw = t
    caus = cst[:, C_CA:C_CA + 256]
    mtok = {}

    def index():
        ready = [act.last(), t_iw]
        for qb in range(2):
            nk = 128 + 128 * qb
            m = msk[:, qb, 0:nk]
            ca = caus[:, 256 - nk:256]
            t = dve.do(lambda e, m=m, ca=ca: e.tensor_copy(m, ca), s_const)
            for i, hs in enumerate(PAIRS):
                b = banks.popleft()
                for j, h in enumerate(hs):
                    o = b.ap[:, j * 256:j * 256 + nk]
                    hf = (h % 2) * 64
                    tp = pe.do(lambda e, o=o, h=h, hf=hf, qb=qb, nk=nk: e.matmul(
                        o, iqT[hf:hf + 64, h // 2, qb * 128:qb * 128 + 128], ikT[hf:hf + 64, 0:nk],
                        start=True, stop=True), b.free, ready, sig=j == 1)
                Sb = scr["S"][i % NBUF]
                s = Sb.ap[:, :, 0:nk]
                bb = b.ap.rearrange("p (a b) -> p a b", a=2)[:, :, 0:nk]
                tr = act.do(lambda e, s=s, bb=bb: e.activation(s, bb, ACT.Relu), tp, Sb.free)
                give(b, tr)
                for j, h in enumerate(hs):
                    t = dve.do(lambda e, s=s, j=j, h=h, m=m, qb=qb: e.scalar_tensor_tensor(
                        m, s[:, j, :], iwt[:, qb, h:h + 1], m, ALU.mult, ALU.add), tr, t, t_iw)
                Sb.free = [t]
                if i % 2:
                    yield
            m8 = stats(8)
            for r in range(8):
                t = dve.do(lambda e, m=m, m8=m8: e.max(m8, m), t)
                t = dve.do(lambda e, m=m, m8=m8: e.match_replace(m, m8, m, MARK), t)
                if r % 4 == 3:
                    yield
            t = dve.do(lambda e, m=m: e.tensor_scalar(m, m, -3.2e38, NEG, ALU.is_gt, ALU.mult), t)
            t = dve.do(lambda e, m=m, ca=ca: e.tensor_tensor(m, m, ca, ALU.add), t)
            mtok[qb] = t

    def gemms(*fs):
        for f in fs:
            f()
            yield

    def skip(g, n):
        for _ in range(n):
            yield
        yield from g

    drive(gemms(lambda: g_rope(2048, dqT), lambda: g_rope(2560, dkT), lambda: g_plain(3072, dv),
                lambda: run_pend()), skip(index(), 1))
    d_ready = [act.last(), dve.last()]
    tsg = {}

    def f_silu(c0, i):
        def f():
            tsg[i] = g_silu(c0, sg[i])
        return f

    tkd = []

    def f_xq():
        for c in range(2):
            b, = gemm_t(W, 4680 + c * 256, 256)
            t = act.do(lambda e, b=b, c=c: e.activation(xqT[:, 2 * c:2 * c + 2, :], b.ap.rearrange("p (a b) -> p a b", a=2), ACT.Copy),
                       b.ready)
            give(b, t)

    f_silu(3584, 1)()
    cfgD = dict(scale=0.125, ready=[mtok[0], mtok[1]],
                tab=lambda qb, hs: bc(msk[:, qb, 0:128 + 128 * qb].unsqueeze(1), 128, 2, 128 + 128 * qb))
    def mul_of(i):
        return lambda qb: (sg[i][:, qb, :], tsg[i])

    def gated_out(i):
        toks = {}
        def finish(qb, b, sm):
            nh = 4 if i == 2 else 8
            r = stats(8)
            t = dve.do(lambda e: e.reciprocal(r[:, 0:nh], sm[:, 0:nh]), act.last())
            d = sg[i][:, qb, :]
            hd = 512 // nh
            t1 = dve.do(lambda e: e.tensor_tensor(d, b.ap, d, ALU.mult), b.ready, tsg[i])
            give(b, t1)
            d3 = d.rearrange("p (h d) -> p h d", h=nh)
            toks[qb] = dve.do(lambda e: e.tensor_tensor(d3, d3, bc(r[:, 0:nh].unsqueeze(2), 128, nh, hd), ALU.mult), t, t1)
        return finish, toks

    finD, tokD = gated_out(1)
    drive(attention(U8, [128, 256], qT_of(dqT), kT_of(dkT), lambda h, kb: dv[:, kb, h * 64:h * 64 + 64],
                    soft_common(cfgD), 64, None, finD, d_ready),
          gemms(lambda: g_rope(0, mqT), lambda: g_rope(512, mkT), lambda: g_plain(1024, mvv),
                lambda: run_pend(), f_silu(1536, 0), f_xq, f_silu(5192, 2)))
    m_ready = [act.last(), dve.last()]

    uT, tT = av(UU, 2048, 8), av(TT + 1024, 1024, 4)
    hb = lgt[:, 8:32]
    t_hb = pool.do(lambda e: e.tensor_scalar(hb, gain[:, G_BM:G_BM + 24], 0.5, None, ALU.mult), m_ready, s_const)
    state_u = dict(first=True, tfree=[], uw=None)

    names = {0: "w_up_moba", 1: "w_up_dsa", 2: "w_up_cross"}
    finM, tokM = gated_out(0)
    finX, tokX = gated_out(2)
    cfgM = dict(scale=0.125, ready=s_const,
                tab=lambda qb, hs: bc(caus[:, 128 - 128 * qb:256].unsqueeze(1), 128, 2, 128 + 128 * qb))
    cfgX = dict(scale=float(128 ** -0.5), ready=None, tab=None)

    def merge_any(i, toks, first):
        u = ur[urn[0] % 2]
        urn[0] += 1
        for g in range(2):
            tl = []
            for c in range(2):
                b, = gemm_t(W, 5704 + 1024 * i + 512 * g + 256 * c, 256)
                for m in range(2):
                    k = 4 * g + 2 * c + m
                    t = act.do(lambda e, b=b, m=m, c=c, k=k: e.activation(
                        tT[:, 2 * c + m, :], b.ap[:, 256 * m:256 * m + 256], ACT.Tanh,
                        bias=hb[:, 8 * i + k:8 * i + k + 1], scale=0.5), b.ready, t_hb, state_u["tfree"])
                give(b, t)
                yield
            if g == 0:
                to_T(sg[i], u, [0, 1, 2, 3], 0, None, [toks[0], toks[1]])
            bks = gemm_t(names[i], 512 * g, 512, nk=4, xT=u)
            for n, b in enumerate(bks):
                tt = tT[:, 2 * n:2 * n + 2, :]
                dd = uT[:, 4 * g + 2 * n:4 * g + 2 * n + 2, :]
                b3 = b.ap.rearrange("p (a b) -> p a b", a=2)
                dst = dd if first else tt
                t1 = dve.do(lambda e, tt=tt, b3=b3, dst=dst: e.scalar_tensor_tensor(dst, tt, 1.0, b3, ALU.add, ALU.mult),
                            b.ready, t, m_ready)
                give(b, t1)
                if not first:
                    t1 = dve.do(lambda e, dd=dd, tt=tt: e.tensor_tensor(dd, dd, tt, ALU.add), t1)
            state_u["tfree"] = [t1]
            if g == 1:
                u.free = [bks[-1].ready]
            yield
        state_u["uw"] = t1

    for q in (act, dve, pe, pool):
        q.wait(tokD[0], tokD[1])
    drive(attention(U8, [128, 256], qT_of(mqT), kT_of(mkT), lambda h, kb: mvv[:, kb, h * 64:h * 64 + 64],
                    soft_common(cfgM), 64, None, finM, m_ready),
          merge_any(1, tokD, True))
    drive(attention(U4, [256, 256], lambda h, qb: xqT[:, h, qb * 128:qb * 128 + 128], lambda h, nk: xkT[:, h, 0:nk],
                    lambda h, kb: xv[:, kb, h * 128:h * 128 + 128], soft_common(cfgX), 128, None, finX, m_ready),
          merge_any(0, tokM, False))
    drive(merge_any(2, tokX, False))

    acc = acc_open()
    for g in range(2):
        u = ur[urn[0] % 2]
        urn[0] += 1
        src = uT[:, 4 * g:4 * g + 4, :]
        dh, dl = u.ap
        t = act.do(lambda e, dh=dh, src=src: e.activation(dh, src, ACT.Copy, scale=0.5), state_u["uw"], u.free)
        u.ready = dve.do(lambda e, dh=dh, dl=dl, src=src: e.scalar_tensor_tensor(
            dl, src, 0.5, dh.bitcast(F32), ALU.mult, ALU.subtract), t, u.free)
        for j in range(2):
            gemm_acc(acc, "w_out_2", (4 * g + 2 * j) * 128, u, 2 * j, g == 0 and j == 0, g == 1 and j == 1)
    xr = acc_close(acc)
    fin = av(3072, 2048, 2)
    toks = rms_rows(x3, fin, [[xr[tb], act.last(), pe.last()] for tb in range(2)])
    for tb in range(2):
        f = fin[:, tb, :]
        t = dve.do(lambda e, f=f: e.tensor_tensor(f, f, rows[:, R_FIN:R_FIN + 1024], ALU.mult), toks[tb])
        dma(sp, out[0, tb * 128:tb * 128 + 128, :], f, "s_out", t)
    sp.wait((S["s_out"], dma_n["s_out"]))
    return used, dict(sp=sp, act=act, dve=dve, pe=pe, pool=pool)


def shape_constants():
    import numpy as np
    c = np.zeros((128, NCONST), np.float32)
    p = np.arange(128)
    c[:, C_ID:C_ID + 128] = np.eye(128)
    for qb in range(2):
        rel = np.abs(np.arange(256)[None, :] - (p[:, None] + 128 * qb))
        c[:, C_NA + 256 * qb:C_NA + 256 * qb + 256] = np.where(rel <= 128, -rel, NEG)
    qc, kc = (p % 64)[:, None], np.arange(64)[None, :]
    cs = np.clip(qc - 8, 0, 48)
    c[:, C_MB:C_MB + 64] = np.where((kc >= cs) & (kc < cs + 16), 0.0, NEG)
    c[:, C_CA + 128:C_CA + 256] = np.where(p[None, :] <= p[:, None], 0.0, LOW)
    inv = np.power(np.float32(10000.0), -np.arange(32, dtype=np.float32) * np.float32(2.0) / np.float32(64)).astype(np.float32)
    for tb in range(2):
        ang = ((p + 128 * tb).astype(np.float32)[:, None] * inv[None, :]).astype(np.float32).astype(np.float64)
        co, si = np.cos(ang), np.sin(ang)
        c[:, C_COS + 64 * tb:C_COS + 64 * tb + 64] = np.concatenate([co, co], 1)
        c[:, C_SIN + 64 * tb:C_SIN + 64 * tb + 64] = np.concatenate([-si, si], 1)
    d = np.arange(384)[None, :] - 128 - p[:, None]
    c[:, C_U:C_U + 384] = np.maximum(d, 0)
    c[:, C_L:C_L + 384] = np.maximum(-d, 0)
    h = np.arange(8)
    c[:, C_IS:C_IS + 8] = 2.0 ** (h + 1)
    c[:, C_NS:C_NS + 8] = -(2.0 ** -(h + 1.0))
    return c


def layout(inputs):
    import numpy as np
    a = {k: np.asarray(v) for k, v in inputs.items()}

    def cols(v):
        return v.reshape(-1, 128).T

    def twice(v):
        return np.concatenate([v, v])[:, None]

    gains = np.concatenate([
        cols(a["attn_norm_e"][0]), cols(a["mlp_norm"][0]), cols(a["ret_norm_o"][0]), cols(a["mlp_norm"][1]),
        cols(a["g_in_2"][0]), cols(a["g_mem_2"][0]), cols(a["ret_gn_o"][0]), cols(a["b_merge_2"][0]),
        twice(a["q_norm_a"][0]), twice(a["k_norm_a"][0]), twice(a["q_norm_b"][0]), twice(a["k_norm_b"][0])], 1)
    rowvec = np.concatenate([a["g_final_2"], a["sink_a"][0], a["decay_fwd_o"][0], a["decay_bwd_o"][0]])[None, :]
    wide = np.zeros((8, 7, 127), np.float32)
    wide[:, :, 48:79] = a["rpb_b"][0][:, 4:11]
    rpb = np.stack([wide[:, :, 63 - q:127 - q] for q in range(64)]).reshape(64, 56, 64)
    return dict(
        x=a["x"], mem=a["mem_2"], gains=gains, rowvec=rowvec, rpb=rpb, consts=shape_constants(),
        w_in_e=a["w_in_e"][0], w_out_e=a["w_out_e"][0], w_in_o=a["w_in_o"][0], w_out_o=a["w_out_o"][0],
        w1_0=a["w_mlp_in"][0], w1_1=a["w_mlp_in"][1], w2_0=a["w_mlp_out"][0], w2_1=a["w_mlp_out"][1],
        w_in_2=a["w_in_2"][0], w_mem=a["w_mem_kv_2"][0], w_up_moba=a["w_up_moba_2"][0],
        w_up_dsa=a["w_up_dsa_2"][0], w_up_cross=a["w_up_cross_2"][0], w_out_2=a["w_out_2"][0])


def kernel(**inputs):
    import numpy as np
    import concourse.bacc as bacc
    from concourse.bass_utils import run_bass_kernel_spmd

    nc = bacc.Bacc("TRN2", target_bir_lowering=False, num_devices=1)
    arrays, args = {}, {}
    for name, a in layout(inputs).items():
        a = np.ascontiguousarray(a)
        arrays[f"in_{name}"] = a
        args[name] = nc.dram_tensor(f"in_{name}", a.shape, mybir.dt.from_np(a.dtype), kind="ExternalInput").ap()
    out = nc.dram_tensor("out", (1, 256, 1024), F32, kind="ExternalOutput").ap()
    program(nc, args, out)
    r = run_bass_kernel_spmd(nc, [arrays], core_ids=[0])
    return r.results[0]["out"]
```

```python
from contextlib import ExitStack
from collections import deque

import concourse.bass as bass
from concourse import mybir

F32 = mybir.dt.float32
F32R = mybir.dt.float32r
ALU = mybir.AluOpType
ACT = mybir.ActivationFunctionType
AXX = mybir.AxisListType.X

NEG = -1.0e30
LOW = -3.0e38
MARK = -3.3e38
EPS = 1e-6
GN_EPS = 1e-5

G_ATT, G_MLP0, G_RET, G_MLP1, G_IN, G_MEM, G_GN, G_BM, G_QA, G_KA, G_QB, G_KB = (
    0, 8, 16, 24, 32, 40, 48, 64, 88, 89, 90, 91)
NGAIN = 92
R_FIN, R_SINK, R_DF, R_DB = 0, 1024, 1032, 1040
NROW = 1048
C_ID, C_NA, C_MB, C_CA, C_COS, C_SIN, C_U, C_L, C_IS, C_NS = (
    0, 128, 640, 704, 960, 1088, 1216, 1600, 1984, 1992)
NCONST = 2000

NRAW = 4
NSPL = 5
LOOK = 4
ARENA = 18176


class Eng:

    def __init__(self, sem):
        self.sem, self.ops, self.count, self.seen = sem, [], 0, {}

    def wait(self, *tokens):
        for t in tokens:
            if t is None:
                continue
            if isinstance(t, list):
                self.wait(*t)
                continue
            sem, value = t
            if self.seen.get(sem, 0) < value:
                self.seen[sem] = value
                self.ops.append(lambda e, s=sem, v=value: e.wait_ge(s, v))

    def do(self, fn, *tokens, sig=True):
        self.wait(*tokens)
        if not sig:
            self.ops.append(fn)
            return None
        self.count += 1
        self.ops.append(lambda e: fn(e).then_inc(self.sem, 1))
        return (self.sem, self.count)

    def last(self):
        return (self.sem, self.count) if self.count else None

    def run(self, e):
        for op in self.ops:
            op(e)


class Buf:

    def __init__(self, ap):
        self.ap, self.free, self.ready = ap, [], None

    def part(self, k):
        return self.ready[k] if isinstance(self.ready, dict) else self.ready


def program(nc, A, out):
    with ExitStack() as st:
        def sb(name, n, dt=F32):
            return st.enter_context(nc.sbuf_tensor(name, [128, n], dt))

        raw = [sb(f"raw{i}", 2048) for i in range(NRAW)]
        whi = [sb(f"whi{i}", 1024, F32R) for i in range(NSPL)]
        wlo = [sb(f"wlo{i}", 1024, F32R) for i in range(NSPL)]
        xs = sb("xs", 2048)
        hTh, hTl = sb("hTh", 2048, F32R), sb("hTl", 2048, F32R)
        urh = [sb(f"urh{i}", 1024, F32R) for i in range(2)]
        url = [sb(f"url{i}", 1024, F32R) for i in range(2)]
        arena = sb("arena", ARENA)
        gain = sb("gain", NGAIN)
        rows = sb("rows", NROW)
        cst = sb("cst", NCONST)
        stat = sb("stat", 640)
        lgt = sb("lgt", 128)
        psum = [st.enter_context(nc.psum_tensor(f"ps{i}", [128, 512], F32)) for i in range(8)]
        sems = {n: st.enter_context(nc.semaphore(n)) for n in
                ["s_pe", "s_act", "s_dve", "s_pool", "s_c", "s_id", "s_x0", "s_x1", "s_t0", "s_t1", "s_g", "s_b", "s_m", "s_out"]
                + [f"s_raw{i}" for i in range(NRAW)]}
        mem = dict(raw=raw, whi=whi, wlo=wlo, xs=xs, hTh=hTh, hTl=hTl, urh=urh, url=url, arena=arena,
                   gain=gain, rows=rows, cst=cst, stat=stat, lgt=lgt, psum=psum)
        order = emit(A, out, mem, sems, None)[0]
        engines = emit(A, out, mem, sems, order)[1]
        block = st.enter_context(nc.Block())
        for name, deco in (("sp", block.sync), ("act", block.scalar), ("dve", block.vector),
                           ("pe", block.tensor), ("pool", block.gpsimd)):
            deco(lambda e, n=name: engines[n].run(e))


def emit(A, out, mem, sems, order):
    S = sems
    sp = Eng(None)
    act, dve, pe, pool = (Eng(S[n]) for n in ("s_act", "s_dve", "s_pe", "s_pool"))
    raw, whi, wlo, xs = mem["raw"], mem["whi"], mem["wlo"], mem["xs"]
    arena, gain, rows, cst, stat, lgt = (mem[n] for n in ("arena", "gain", "rows", "cst", "stat", "lgt"))

    def v3(t, a, off=0, n=None):
        n = n or 2048
        return t[:, off:off + n].rearrange("p (a b) -> p a b", a=a)

    def av(off, n, a=None):
        assert off + n <= ARENA, (off, n)
        r = arena[:, off:off + n]
        return r if a is None else r.rearrange("p (a b) -> p a b", a=a)

    def bc(ap, *shape):
        return ap.broadcast_to(list(shape))

    banks = deque(Buf(t[:, :]) for t in mem["psum"])

    def give(b, *tokens):
        b.free = list(tokens)
        banks.append(b)

    dma_n = {}

    def dma(q, dst, src, sem, *waits):
        dma_n[sem] = dma_n.get(sem, 0) + 16
        q.do(lambda e: e.dma_start(dst, src).then_inc(S[sem], 16), *waits, sig=False)

    used, halves, done = [], [], []
    state = dict(dma=0)
    after_dma = {}

    def issue_dma(m):
        name, k0, nk, c0, n, _ = order[2 * m]
        src = A[name][k0:k0 + nk * 128, c0:c0 + n].rearrange("(t p) n -> p t n", p=128)
        dst = raw[m % NRAW][:, 0:nk * n].rearrange("p (t n) -> p t n", t=nk)
        waits = [halves[2 * (m - NRAW) + 1]["lo"]] if m >= NRAW else []
        sp.do(lambda e: e.dma_start(dst, src).then_inc(S[f"s_raw{m % NRAW}"], 16), *waits, sig=False)
        if m in after_dma:
            after_dma[m]()

    def issue_split(i):
        m, x = i // 2, i % 2
        name, k0, nk, c0, n, by = order[i]
        r = raw[m % NRAW][:, 0:nk * n].rearrange("p (t n) -> p t n", t=nk)
        if by == "k":
            nk //= 2
            r = r[:, x * nk:x * nk + nk, :]
        else:
            n //= 2
            r = r[:, :, x * n:x * n + n]
        h, l = (t[i % NSPL][:, 0:nk * n].rearrange("p (t n) -> p t n", t=nk) for t in (whi, wlo))
        arrived = (S[f"s_raw{m % NRAW}"], 16 * (m // NRAW + 1))
        free = done[i - NSPL] if i >= NSPL else None
        th = act.do(lambda e: e.activation(h, r, ACT.Copy), arrived, free)
        tl = dve.do(lambda e: e.tensor_tensor(l, r, h.bitcast(F32), ALU.subtract), arrived, th, free)
        halves.append(dict(hi=th, lo=tl, h=h, l=l))

    def next_half(name, k0, nk, c0, n, by):
        i = len(used)
        used.append((name, k0, nk, c0, n, by))
        if order is None:
            a, b = (nk // 2, n) if by == "k" else (nk, n // 2)
            z = whi[0][:, 0:a * b].rearrange("p (t n) -> p t n", t=a)
            return dict(hi=None, lo=None, h=z, l=z)
        assert order[i] == used[i]
        while len(halves) < min(i + LOOK, len(order)):
            while 2 * state["dma"] < min(len(halves) + 2 * NRAW, len(order)):
                if state["dma"] >= NRAW and len(halves) < 2 * (state["dma"] - NRAW) + 2:
                    break
                issue_dma(state["dma"])
                state["dma"] += 1
            issue_split(len(halves))
        return halves[i]

    def half_done(tok):
        done.append(tok)

    def mm3(o, pairs, start, stop, *waits, sig=False):
        t = None
        for i, (a, b) in enumerate(pairs):
            last = i == len(pairs) - 1
            t = pe.do(lambda e, a=a, b=b, s=start and i == 0, p=stop and last:
                      e.matmul(o, a, b, start=s, stop=p), *(waits if i == 0 else ()), sig=sig and last)
        return t

    hT = Buf((v3(mem["hTh"], 8), v3(mem["hTl"], 8)))
    ur = [Buf((v3(h, 4, 0, 1024), v3(l, 4, 0, 1024))) for h, l in zip(mem["urh"], mem["url"])]
    urn = [0]

    def finish_gen(g):
        while True:
            try:
                next(g)
            except StopIteration as e:
                return e.value

    def gemm_n(*a, **k):
        return finish_gen(gemm_ng(*a, **k))

    def gemm_ng(name, c0, n, xT=None, mid=None):
        xT = xT or hT
        bk = [banks.popleft() for _ in range(2)]
        nk = 4 if n > 256 else 8
        tok = [None, None]
        for k0 in range(0, 8, nk):
            for x in range(2):
                t = next_half(name, k0 * 128, nk, c0, n, "k")
                for tb in range(2):
                    for k in range(nk // 2):
                        kk = k0 + x * nk // 2 + k
                        xh = xT.ap[0][:, kk, tb * 128:tb * 128 + 128]
                        xl = xT.ap[1][:, kk, tb * 128:tb * 128 + 128]
                        end = k == nk // 2 - 1
                        w = (bk[tb].free, xT.part(kk), t["hi"], t["lo"])
                        tok[tb] = mm3(bk[tb].ap[:, 0:n], [(xh, t["h"][:, k, :]), (xh, t["l"][:, k, :]), (xl, t["h"][:, k, :])],
                                      kk == 0, kk == 7, *w, sig=end)
                half_done(tok[1])
            if mid and k0 == 0:
                mid()
            if k0 + nk < 8:
                yield
        for b, t in zip(bk, tok):
            b.ready = t
        return bk

    def gemm_t(name, c0, n, nk=8, xT=None):
        xT = xT or hT
        res = []
        for m in range(n // 128):
            if m % (n // 256) == 0:
                t, m0 = next_half(name, 0, nk, c0, n, "n"), m
            if m % 2 == 0:
                b = banks.popleft()
                res.append(b)
            o = b.ap[:, (m % 2) * 256:(m % 2) * 256 + 256]
            for k in range(nk):
                c = (m - m0) * 128
                wh, wl = t["h"][:, k, c:c + 128], t["l"][:, k, c:c + 128]
                xh, xl = xT.ap[0][:, k, :], xT.ap[1][:, k, :]
                tok = mm3(o, [(wh, xh), (wh, xl), (wl, xh)], k == 0, k == nk - 1,
                          b.free, xT.part(k), t["hi"], t["lo"], sig=k == nk - 1)
            b.ready = tok
            if (m + 1) % (n // 256) == 0:
                half_done(tok)
        return res

    def acc_open():
        return [banks.popleft() for _ in range(4)]

    def gemm_acc(acc, name, k0, u, j, first, last):
        for k in range(2):
            t = next_half(name, k0, 2, 0, 1024, "k")
            for tb in range(2):
                uh = u.ap[0][:, j + k, tb * 128:tb * 128 + 128]
                ul = u.ap[1][:, j + k, tb * 128:tb * 128 + 128]
                s, p = first and k == 0, last and k == 1
                b0, b1 = acc[2 * tb], acc[2 * tb + 1]
                h = [t["h"][:, 0, 512 * i:512 * i + 512] for i in range(2)]
                l = [t["l"][:, 0, 512 * i:512 * i + 512] for i in range(2)]
                w = (b0.free, b1.free, u.part(j + k), t["hi"], t["lo"])
                mm3(b0.ap, [(uh, h[0])], s, False, *w)
                mm3(b1.ap, [(uh, h[1])], s, False)
                mm3(b0.ap, [(uh, l[0])], False, False)
                mm3(b1.ap, [(uh, l[1])], False, False)
                mm3(b0.ap, [(ul, h[0])], False, p)
                tok = mm3(b1.ap, [(ul, h[1])], False, p, sig=True)
                b0.ready = b1.ready = tok
            half_done(tok)
        u.free = [tok]
        return tok

    def acc_close(acc, scale=None):
        toks = []
        for tb in range(2):
            for i in range(2):
                b = acc[2 * tb + i]
                o = xs[:, tb * 1024 + i * 512:tb * 1024 + i * 512 + 512]
                if scale:
                    sc, ts = scale[tb]
                    t = dve.do(lambda e, o=o, b=b, sc=sc: e.scalar_tensor_tensor(o, b.ap, sc, o, ALU.mult, ALU.add),
                               b.ready, ts)
                else:
                    t = dve.do(lambda e, o=o, b=b: e.tensor_tensor(o, o, b.ap, ALU.add), b.ready)
                give(b, t)
            toks.append(t)
        return toks

    ident = cst[:, C_ID:C_ID + 128]
    half = stat[:, 0:33]
    stn = [34]

    def stats(n):
        if stn[0] + n > 640:
            stn[0] = 34
        stn[0] += n
        return stat[:, stn[0] - n:stn[0]]

    def boundary():
        ts = [q.last() for q in (act, dve, pe, pool)]
        for q in (act, dve, pe, pool):
            q.wait(*ts)
        stn[0] = 34

    def rstd(ss, n, scale, eps, *waits):
        t = pool.do(lambda e: e.tensor_scalar(ss, ss, scale, eps, ALU.mult, ALU.add), *waits)
        return pool.do(lambda e: e.tensor_tensor(ss, ss, half[:, 0:n], ALU.pow), t)

    def row_scales(src, junk, ready):
        res = []
        for tb in range(2):
            i, rr, hh, i64 = (stats(1) for _ in range(4))
            t = act.do(lambda e, tb=tb, i=i: e.activation(junk[:, tb, :], src[:, tb, :], ACT.Square, accum_out=i), ready[tb])
            t = pool.do(lambda e, i=i: e.tensor_scalar(i, i, 1.0 / 1024, EPS, ALU.mult, ALU.add), t)
            ti = dve.do(lambda e, i=i: e.reciprocal(i, i), t)
            t = pool.do(lambda e, i=i, rr=rr: e.tensor_tensor(rr, i, half[:, 32:33], ALU.pow), ti)
            t64 = pool.do(lambda e, i=i, i64=i64: e.tensor_scalar(i64, i, 1.0 / 64, None, ALU.mult), ti)
            th = pool.do(lambda e, rr=rr, hh=hh: e.tensor_scalar(hh, rr, 0.5, None, ALU.mult), t)
            res.append(dict(i=i, r=rr, h=hh, i64=i64, t=th, ti=ti))
        return res

    ones, diag, rbc = cst[:, C_U:C_U + 128], cst[:, C_U + 128:C_U + 384], cst[:, C_L:C_L + 256]

    def row_broadcast(sc, *waits):
        for tb in range(2):
            t = dve.do(lambda e, tb=tb: e.tensor_scalar(diag[:, tb * 128:tb * 128 + 128], ident, sc[tb]["r"], None, ALU.mult),
                       sc[tb]["t"], *waits)
        b = banks.popleft()
        t = pe.do(lambda e: e.matmul(b.ap[:, 0:256], ones, diag, start=True, stop=True), b.free, t, t_ones)
        t = dve.do(lambda e: e.tensor_copy(rbc, b.ap[:, 0:256]), t, *waits)
        give(b, t)
        return t

    def split_x(srcT, gcol, dst, ready, *waits):
        dst.ready = {}
        for k in range(8):
            g = gain[:, gcol + k:gcol + k + 1]
            dh, dl = dst.ap[0][:, k, :], dst.ap[1][:, k, :]
            t = act.do(lambda e, k=k, dh=dh, g=g: e.activation(dh, srcT[:, k, :], ACT.Copy, scale=g), ready[k // 4], *waits)
            dst.ready[k] = dve.do(lambda e, k=k, dh=dh, dl=dl, g=g: e.scalar_tensor_tensor(
                dl, srcT[:, k, :], g, dh.bitcast(F32), ALU.mult, ALU.subtract), t)

    def split_evac(dh, dl, src, scales, *waits):
        for h, s, g in zip(dh, src, scales):
            kw = {} if g is None else dict(scale=g)
            th = act.do(lambda e, h=h, s=s, kw=kw: e.activation(h, s, ACT.Copy, **kw), *waits)
        for h, l, s, g in zip(dh, dl, src, scales):
            if g is None:
                tl = dve.do(lambda e, h=h, l=l, s=s: e.tensor_tensor(l, s, h.bitcast(F32), ALU.subtract), th)
            else:
                tl = dve.do(lambda e, h=h, l=l, s=s, g=g: e.scalar_tensor_tensor(
                    l, s, g, h.bitcast(F32), ALU.mult, ALU.subtract), th)
        return tl

    def to_T(src, dst, kts, d0, gcol, ready, *waits):
        if not isinstance(dst.ready, dict):
            dst.ready = {}
        for i in range(0, len(kts), 2):
            b = banks.popleft()
            for j in range(2):
                for tb in range(2):
                    k = kts[i + j]
                    o = b.ap[:, j * 256 + tb * 128:j * 256 + tb * 128 + 128]
                    s = src[:, tb, k * 128:k * 128 + 128]
                    t = pe.do(lambda e, o=o, s=s: e.transpose(o, s, ident), b.free, ready, s_ident,
                              sig=(j == 1 and tb == 1))
            k, d = kts[i], d0 + i
            if gcol is None:
                tok = split_evac([dst.ap[0][:, d:d + 2, :]], [dst.ap[1][:, d:d + 2, :]],
                                 [b.ap.rearrange("p (a b) -> p a b", a=2)], [None], t, dst.free, *waits)
            else:
                tok = split_evac([dst.ap[0][:, d + j, :] for j in range(2)], [dst.ap[1][:, d + j, :] for j in range(2)],
                                 [b.ap[:, j * 256:j * 256 + 256] for j in range(2)],
                                 [gain[:, gcol + k + j:gcol + k + j + 1] for j in range(2)], t, dst.free, *waits)
            give(b, tok)
            dst.ready[d] = dst.ready[d + 1] = tok
        return tok

    pool.do(lambda e: e.memset(half[:, 0:32], -0.5))
    pool.do(lambda e: e.memset(half[:, 32:33], 0.5))
    dma(act, gain[:, :], A["gains"], "s_g")
    XT = 14080
    xT0 = av(XT, 2048, 8)
    for i in range(2):
        dma(act, xT0[:, 4 * i:4 * i + 4, :], A["xT"][i * 512:i * 512 + 512, :].rearrange("(t p) n -> p t n", p=128), f"s_t{i}")
    s_ident = (S["s_id"], 16)
    s_const = (S["s_c"], 32)
    x3 = v3(xs, 2)

    NBUF = 2
    scr = {}

    def scratch(off):
        scr["S"] = [Buf(av(off + 512 * i, 512, 2)) for i in range(NBUF)]
        scr["P"] = [Buf(av(off + 512 * (NBUF + i), 512, 2)) for i in range(NBUF)]
        scr["T"] = [Buf(av(off + 512 * (2 * NBUF + i), 512)) for i in range(NBUF)]
        return off + 512 * 3 * NBUF

    def attention(units, kmax, q_of, k_of, v_of, score, hd, per_q, finish, ready):
        n = len(units)
        st2 = {}
        ob = {}
        sums = {}

        def stage1(i):
            qb, hs = units[i]
            nk = kmax[qb]
            if qb not in sums:
                sums[qb] = stats(8)
            b = banks.popleft()
            for j, h in enumerate(hs):
                o = b.ap[:, j * 256:j * 256 + nk]
                t = pe.do(lambda e, o=o, h=h: e.matmul(o, q_of(h, qb), k_of(h, nk), start=True, stop=True),
                          b.free, ready, sig=j == 1)
            Sb, Pb = scr["S"][i % NBUF], scr["P"][i % NBUF]
            src, par, t2, freed = score(qb, hs, b.ap.rearrange("p (a b) -> p a b", a=2)[:, :, 0:nk],
                                        Sb.ap[:, :, 0:nk], (t, Sb.free))
            for j, h in enumerate(hs):
                scl, nm = par[j]
                po, si, ac = Pb.ap[:, j, 0:nk], src[:, j, :], sums[qb][:, h:h + 1]
                t3 = act.do(lambda e, po=po, si=si, ac=ac, scl=scl, nm=nm: e.activation(
                    po, si, ACT.Exp, bias=nm, scale=scl, accum_out=ac), t2, Pb.free)
            if freed is None:
                give(b, t3)
            else:
                give(b, freed)
                Sb.free = [t3]
            Pb.ready = t3

        def stage2(i):
            qb, hs = units[i]
            nk = kmax[qb]
            Pb, Tb = scr["P"][i % NBUF], scr["T"][i % NBUF]
            b = banks.popleft()
            nb = nk // 128
            for j in range(2):
                for kb in range(nb):
                    o = b.ap[:, (j * nb + kb) * 128:(j * nb + kb) * 128 + 128]
                    s = Pb.ap[:, j, kb * 128:kb * 128 + 128]
                    t = pe.do(lambda e, o=o, s=s: e.transpose(o, s, ident), b.free, Pb.ready, s_ident,
                              sig=(j == 1 and kb == nb - 1))
            Pb.free = [t]
            q = act if i % 2 else dve
            w = 2 * nk
            if i % 2:
                t = act.do(lambda e: e.activation(Tb.ap[:, 0:w], b.ap[:, 0:w], ACT.Copy), t, Tb.free)
            else:
                t = dve.do(lambda e: e.tensor_copy(Tb.ap[:, 0:w], b.ap[:, 0:w]), t, Tb.free)
            give(b, t)
            Tb.ready = t

        def stage3(i):
            qb, hs = units[i]
            nb = kmax[qb] // 128
            Tb = scr["T"][i % NBUF]
            if qb not in ob:
                ob[qb] = banks.popleft()
            b = ob[qb]
            for j, h in enumerate(hs):
                for kb in range(nb):
                    o = b.ap[:, h * hd:h * hd + hd]
                    s = Tb.ap[:, (j * nb + kb) * 128:(j * nb + kb) * 128 + 128]
                    t = pe.do(lambda e, o=o, s=s, kb=kb, h=h: e.matmul(o, s, v_of(h, kb), start=kb == 0, stop=kb == nb - 1),
                              b.free, Tb.ready, ready, sig=(j == 1 and kb == nb - 1))
            Tb.free = [t]
            b.ready = t
            if i == n - 1 or units[i + 1][0] != qb:
                finish(qb, b, sums[qb])

        for i in range(n + 2):
            if i < n:
                stage1(i)
            if 0 <= i - 1 < n:
                stage2(i - 1)
            if 0 <= i - 2 < n:
                stage3(i - 2)
            yield

    PAIRS = [(0, 2), (1, 3), (4, 6), (5, 7)]
    U8 = [(qb, hs) for qb in range(2) for hs in PAIRS]
    U4 = [(qb, hs) for qb in range(2) for hs in ((0, 1), (2, 3))]

    def qT_of(qT):
        return lambda h, qb: qT[(h % 2) * 64:(h % 2) * 64 + 64, h // 2, qb * 128:qb * 128 + 128]

    def kT_of(kT):
        return lambda h, nk: kT[(h % 2) * 64:(h % 2) * 64 + 64, h // 2, 0:nk]

    def soft_common(biased):
        def score(qb, hs, bank, Sb, waits):
            nm = stats(2)
            tab = biased["tab"](qb, hs) if biased["tab"] else None
            c = biased["scale"]
            if tab is None:
                t = dve.do(lambda e: e.tensor_reduce(nm, bank, AXX, ALU.max, negate=True), waits[0])
                t = dve.do(lambda e: e.tensor_scalar(nm, nm, c, None, ALU.mult), t)
                return bank, [(c, nm[:, 0:1]), (c, nm[:, 1:2])], t, None
            t = dve.do(lambda e: e.scalar_tensor_tensor(Sb, bank, c, tab, ALU.mult, ALU.add),
                       *waits, biased["ready"])
            f = t
            t = dve.do(lambda e: e.tensor_reduce(nm, Sb, AXX, ALU.max, negate=True), t)
            return Sb, [(1.0, nm[:, 0:1]), (1.0, nm[:, 1:2])], t, f
        return score

    def norm_out(dst_of, nh=8, extra=None, mul=None):
        toks = {}

        def finish(qb, b, sm):
            r = stats(8)
            t = act.last()
            if extra:
                t = extra(qb, sm, t)
            t = dve.do(lambda e: e.reciprocal(r[:, 0:nh], sm[:, 0:nh]), t)
            hd = 512 // nh
            o3 = b.ap.rearrange("p (h d) -> p h d", h=nh)
            d = dst_of(qb)
            d3 = d.rearrange("p (h d) -> p h d", h=nh)
            rb = bc(r[:, 0:nh].unsqueeze(2), 128, nh, hd)
            t = dve.do(lambda e: e.tensor_tensor(d3, o3, rb, ALU.mult), t, b.ready)
            give(b, t)
            if mul:
                m, mr = mul(qb)
                t = dve.do(lambda e: e.tensor_tensor(d, d, m, ALU.mult), t, mr)
            toks[qb] = t
        return finish, toks

    def drive(*gens):
        gens = list(gens)
        while gens:
            for g in list(gens):
                try:
                    next(g)
                except StopIteration:
                    gens.remove(g)

    AQT, AKT, BQT, BKT, AV, BV, BB, OS = 0, 1024, 1536, 2560, 3584, 3840, 4864, 8960
    o = scratch(11008)
    SQ = [Buf(av(o + 512 * i, 512)) for i in range(2)]
    QN = [Buf(av(o + 1024 + 512 * i, 512)) for i in range(2)]
    aqT, akT, bqT, bkT = av(AQT, 1024, 4), av(AKT, 512, 2), av(BQT, 1024, 4), av(BKT, 1024, 4)
    avv, bvv = av(AV, 256, 2), av(BV, 1024, 2)
    biasB = av(BB, 4096)
    osb = av(OS, 2048, 2)

    split_x(xT0, G_ATT, hT, [(S["s_t0"], 16), (S["s_t1"], 16)], (S["s_g"], 16))

    def load_x():
        for tb in range(2):
            dma(sp, xs[:, tb * 1024:tb * 1024 + 1024], A["x"][0, tb * 128:tb * 128 + 128, :], f"s_x{tb}")
        dma(sp, cst[:, 0:128], A["consts"][:, 0:128], "s_id")

    def load_consts():
        dma(sp, cst[:, 128:NCONST], A["consts"][:, 128:NCONST], "s_c")
        dma(sp, rows[:, :], bass.AP(A["rowvec"].tensor, 0, [[0, 128], [1, NROW]]), "s_c")

    def load_bias():
        for qr in range(4):
            dst = biasB[(qr % 2) * 64:(qr % 2) * 64 + 64, (qr // 2) * 2048:(qr // 2) * 2048 + 2048]
            src = A["rpb"].rearrange("q (h r) k -> q h (r k)", h=8)[:, :, (3 - qr) * 64:(7 - qr) * 64]
            dma(sp, dst.rearrange("p (h c) -> p h c", h=8), src, "s_b")

    after_dma.update({1: load_x, 2: load_consts, 4: load_bias})
    invs, negs = cst[:, C_IS:C_IS + 8], cst[:, C_NS:C_NS + 8]
    skp = lgt[:, 0:8]
    t_skp = pool.do(lambda e: e.tensor_tensor(skp, rows[:, R_SINK:R_SINK + 8], invs, ALU.mult), s_const)


    pend = []

    def run_pend():
        for f in pend:
            f()
        pend.clear()

    cnt = [0]

    muls = []

    def run_muls():
        for f in muls:
            f()
        muls.clear()

    def head_norm(b, tb, c0, nh, gcol, dst, rdy, dup=False, then=None):
        w = nh * 64
        i = cnt[0] % 2
        cnt[0] += 1
        sq, qn = SQ[i], QN[i]
        src = b.ap[:, c0:c0 + w]
        ss = stats(nh)
        t0 = act.do(lambda e, w=w: e.activation(sq.ap[:, 0:w], src, ACT.Square), b.ready, sq.free)
        t1 = dve.do(lambda e, w=w: e.tensor_reduce(ss, sq.ap[:, 0:w].rearrange("p (h d) -> p h d", d=64), AXX, ALU.add), t0)
        sq.free = [t1]
        sc = xsc[tb]
        t2 = pool.do(lambda e: e.tensor_scalar(ss, ss, sc["i64"], EPS, ALU.mult, ALU.add), t1, sc["t"])
        t2 = pool.do(lambda e: e.tensor_tensor(ss, ss, half[:, 0:nh], ALU.pow), t2)
        t2 = pool.do(lambda e: e.tensor_scalar(ss, ss, sc["r"], None, ALU.mult), t2)

        def scale(w=w):
            s3 = src.rearrange("p (h d) -> p h d", d=64)
            if dup:
                q4 = qn.ap[:, 0:2 * w].rearrange("p (h r d) -> p h r d", h=nh, r=2)
                for r in range(2):
                    t3 = dve.do(lambda e, r=r: e.tensor_tensor(q4[:, :, r, :], s3, bc(ss.unsqueeze(2), 128, nh, 64), ALU.mult),
                                t2, b.ready, qn.free)
                w *= 2
            else:
                q3 = qn.ap[:, 0:w].rearrange("p (h d) -> p h d", d=64)
                t3 = dve.do(lambda e: e.tensor_tensor(q3, s3, bc(ss.unsqueeze(2), 128, nh, 64), ALU.mult),
                            t2, b.ready, qn.free)
            nb = w // 128

            def later(t3=t3):
                tbk = banks.popleft()
                for j in range(nb):
                    t = pe.do(lambda e, j=j: e.transpose(tbk.ap[:, j * 128:j * 128 + 128], qn.ap[:, j * 128:j * 128 + 128], ident),
                              tbk.free, t3, s_ident, sig=j == nb - 1)
                qn.free = [t]
                d = dst[:, 0:nb, tb * 128:tb * 128 + 128]
                s = tbk.ap[:, 0:nb * 128].rearrange("p (a b) -> p a b", a=nb)
                t = act.do(lambda e: e.activation(d, s, ACT.Copy, scale=gain[:, gcol:gcol + 1]), t)
                give(tbk, t)
                rdy.append(t)
            pend.append(later)
            if then:
                t3 = then(t3)
            give(b, t3)
        muls.append(scale)

    def plain_evac(b, c0, w, d, which, sc, *waits):
        s = b.ap[:, c0:c0 + w]
        if which:
            return act.do(lambda e: e.activation(d, s, ACT.Copy, scale=sc["r"]), b.ready, sc["t"], *waits)
        return dve.do(lambda e: e.tensor_scalar(d, s, sc["r"], None, ALU.mult), b.ready, sc["t"], *waits)

    W = "w_in_e"

    rA, rB = [], []

    def g_heads(c0, gc, dst, rdy):
        bk = yield from gemm_ng(W, c0, 512)
        run_muls()
        run_pend()
        for tb in range(2):
            head_norm(bk[tb], tb, 0, 8, gc, dst, rdy)

    bk = gemm_n(W, 0, 512)
    xsc = row_scales(x3, osb, [(S["s_x0"], 16), (S["s_x1"], 16)])
    for tb in range(2):
        head_norm(bk[tb], tb, 0, 8, G_QA, aqT, rA)
    bk = gemm_n(W, 512, 256)
    run_muls()
    run_pend()

    def ev(b, tb):
        def f(t):
            t = plain_evac(b, 128, 128, avv[:, tb, :], 0, xsc[tb], t)
            rA.append(t)
            return t
        return f

    for tb in range(2):
        head_norm(bk[tb], tb, 0, 2, G_KA, akT, rA, dup=True, then=ev(bk[tb], tb))
    finish_gen(g_heads(768, G_QB, bqT, rB))
    readyA = rA
    bT = {}

    def rest_b():
        yield
        yield from g_heads(1280, G_KB, bkT, rB)
        yield
        bk = yield from gemm_ng(W, 1792, 512)
        run_muls()
        run_pend()
        for tb in range(2):
            t = plain_evac(bk[tb], 0, 512, bvv[:, tb, :], tb, xsc[tb])
            rB.append(t)
            give(bk[tb], t)
        bT["ready"] = rB
        yield

    slope = [2.0 ** -(h + 1) for h in range(8)]
    negabs = v3(cst, 2, C_NA, 512)
    nmA = [stats(8), stats(8)]

    def scoreA(qb, hs, bank, Sb, waits):
        mx = stats(2)
        for j, h in enumerate(hs):
            t = dve.do(lambda e, j=j, h=h: e.scalar_tensor_tensor(
                Sb[:, j, :], bank[:, j, :], 0.125 / slope[h], negabs[:, qb, :], ALU.mult, ALU.add), *waits, s_const)
        f = t
        t = dve.do(lambda e: e.tensor_reduce(mx, Sb, AXX, ALU.max), t)
        hsl = slice(hs[0], hs[1] + 1, hs[1] - hs[0])
        nm = nmA[qb][:, hsl]
        t = dve.do(lambda e: e.tensor_tensor(mx, mx, skp[:, hsl], ALU.max), t, t_skp)
        t = dve.do(lambda e: e.tensor_tensor(nm, mx, negs[:, hsl], ALU.mult), t)
        return Sb, [(slope[h], nmA[qb][:, h:h + 1]) for h in hs], t, f

    def extraA(qb, sm, t):
        es = stats(8)
        t1 = dve.do(lambda e: e.tensor_tensor(es, rows[:, R_SINK:R_SINK + 8], nmA[qb], ALU.add), t)
        t1 = act.do(lambda e: e.activation(es, es, ACT.Exp), t1)
        return dve.do(lambda e: e.tensor_tensor(sm, sm, es, ALU.add), t1, t)

    finA, tokA = norm_out(lambda qb: osb[:, qb, 0:512], extra=extraA)
    finB, tokB = norm_out(lambda qb: osb[:, qb, 512:1024])
    bias5 = biasB.rearrange("p (q h k) -> p q h k", q=2, h=8)
    kAT = lambda h, nk: akT[(h % 2) * 64:(h % 2) * 64 + 64, h // 4, 0:nk]
    drive(attention(U8, [256, 256], qT_of(aqT), kAT, lambda h, kb: avv[:, kb, (h // 4) * 64:(h // 4) * 64 + 64],
                    scoreA, 64, None, finA, readyA), rest_b())
    cfgB = dict(scale=0.125, tab=lambda qb, hs: bias5[:, qb, hs[0]:hs[1] + 1:hs[1] - hs[0], :], ready=(S["s_b"], 64))

    def out_half(acc, name, src, g, ready):
        u = ur[urn[0] % 2]
        urn[0] += 1
        to_T(src, u, list(range(4 * g, 4 * g + 4)), 0, None, ready)
        for j in range(2):
            yield
            gemm_acc(acc, name, (4 * g + 2 * j) * 128, u, 2 * j, g == 0 and j == 0, g == 1 and j == 1)

    acc = acc_open()
    drive(attention(U8, [256, 256], qT_of(bqT), kT_of(bkT), lambda h, kb: bvv[:, kb, h * 64:h * 64 + 64],
                    soft_common(cfgB), 64, None, finB, bT["ready"]),
          out_half(acc, "w_out_e", osb, 0, list(tokA.values())))
    drive(out_half(acc, "w_out_e", osb, 1, list(tokB.values())))
    xr = acc_close(acc)

    def mlp(layer, gcol, xr, during=None):
        boundary()
        hn = av(0, 2048, 2)
        RL = [Buf(av(2048 + 512 * i, 512)) for i in range(2)]
        SQ2 = [Buf(av(3072 + 512 * i, 512)) for i in range(2)]
        to_T(x3, hT, list(range(8)), 0, gcol, xr)
        inv = [(c["i"], c["ti"]) for c in row_scales(x3, hn, xr)]
        acc = acc_open()
        w1, w2 = f"w1_{layer}", f"w2_{layer}"
        slots = []
        for j in range(17):
            if j < 16:
                b, = gemm_t(w1, j * 256, 256)
                rl, sq = RL[j % 2], SQ2[j % 2]
                u, off = ur[(j // 2) % 2], 2 * (j % 2)
                t = act.do(lambda e, b=b, rl=rl: e.activation(rl.ap, b.ap, ACT.Relu), b.ready, rl.free)
                give(b, t)
                t = dve.do(lambda e, rl=rl, sq=sq: e.tensor_tensor(sq.ap, rl.ap, rl.ap, ALU.mult), t, sq.free)
                rl.free = [t]
                s3 = sq.ap.rearrange("p (a b) -> p a b", a=2)
                dh, dl = u.ap[0][:, off:off + 2, :], u.ap[1][:, off:off + 2, :]
                th = act.do(lambda e, dh=dh, s3=s3: e.activation(dh, s3, ACT.Copy), t, u.free)
                t = dve.do(lambda e, dl=dl, dh=dh, s3=s3: e.tensor_tensor(dl, s3, dh.bitcast(F32), ALU.subtract), th, u.free)
                sq.free = [t]
                if not isinstance(u.ready, dict):
                    u.ready = {}
                u.ready[off] = u.ready[off + 1] = t
                slots.append((u, off))
            if j >= 1:
                u, off = slots[j - 1]
                gemm_acc(acc, w2, (j - 1) * 256, u, off, j == 1, j == 16)
            if during:
                during(j)
        return acc_close(acc, inv)

    DT = 15104
    dtab = av(DT, 3072, 8)

    td = []

    def decays(j):
        if 12 <= j < 16:
            dd = dtab[:, 2 * (j - 12):2 * (j - 12) + 2, :]
            td.append(act.do(lambda e: e.activation(dd, dd, ACT.Exp), td[0]))
        if j != 1:
            return
        d = rows[:, R_DF:R_DF + 16]
        a = [lgt[:, 16 * i:16 * i + 16] for i in range(1, 8)]
        ad, e_, s_, s2, pl, lo, t1 = a
        p = pool
        t = p.do(lambda e: e.tensor_scalar(ad, d, -1.0, None, ALU.mult), s_const)
        t = dve.do(lambda e: e.tensor_tensor(ad, ad, d, ALU.min), t)
        t = act.do(lambda e: e.activation(e_, ad, ACT.Exp), t)
        t = p.do(lambda e: e.tensor_scalar(t1, e_, 2.0, None, ALU.add), t)
        t = dve.do(lambda e: e.reciprocal(t1, t1), t)
        t = p.do(lambda e: e.tensor_tensor(s_, e_, t1, ALU.mult), t)
        t = p.do(lambda e: e.tensor_tensor(s2, s_, s_, ALU.mult), t)
        t = p.do(lambda e: e.tensor_scalar(pl, s2, 1.0 / 19, 1.0 / 17, ALU.mult, ALU.add), t)
        for n in (15, 13, 11, 9, 7, 5, 3, 1):
            t = p.do(lambda e: e.tensor_tensor(pl, pl, s2, ALU.mult), t)
            t = p.do(lambda e, n=n: e.tensor_scalar(pl, pl, 1.0 / n, None, ALU.add), t)
        t = p.do(lambda e: e.tensor_tensor(pl, pl, s_, ALU.mult), t)
        t = p.do(lambda e: e.tensor_scalar(pl, pl, 2.0, None, ALU.mult), t)
        t = p.do(lambda e: e.tensor_scalar(lo, d, 0.0, None, ALU.min), t)
        t = p.do(lambda e: e.tensor_tensor(lo, lo, pl, ALU.subtract), t)
        uu, ll = cst[:, C_U:C_U + 384], cst[:, C_L:C_L + 384]
        tmp = av(4096, 3072, 8)
        for h in range(8):
            p.do(lambda e, h=h: e.tensor_scalar(dtab[:, h, :], uu, lo[:, h:h + 1], None, ALU.mult), t)
            t2 = p.do(lambda e, h=h: e.tensor_scalar(tmp[:, h, :], ll, lo[:, 8 + h:9 + h], None, ALU.mult), t)
        t2 = p.do(lambda e: e.tensor_tensor(dtab, dtab, tmp, ALU.add), t2)
        td.append(t2)

    xr = mlp(0, G_MLP0, xr, decays)
    t_dtab = td[-1]

    boundary()
    OQ, OK_, OV, OY, OX = 0, 2048, 4096, 8192, 12288
    oqT, okT = av(OQ, 2048, 8), av(OK_, 2048, 8)
    ov, oy = av(OV, 4096, 2), av(OY, 4096, 2)
    ATs = [Buf(av(OX + 512 * i, 512, 2)) for i in range(2)]
    GT = [Buf(av(OX + 1024 + 512 * i, 512)) for i in range(2)]
    to_T(x3, hT, list(range(8)), 0, G_RET, xr)
    xsc = row_scales(x3, av(OY, 2048, 2), xr)
    t_ones = pool.do(lambda e: e.memset(ones, 1.0))
    W = "w_in_o"
    qtok = []
    for base, dst in ((0, oqT), (1024, okT)):
        for c in range(0, 4, 2):
            bks = gemm_t(W, base + c * 256, 256) + gemm_t(W, base + c * 256 + 256, 256)
            if not qtok:
                t_rb = row_broadcast(xsc)
            for i, b in enumerate(bks):
                d = dst[:, 2 * (c + i):2 * (c + i) + 2, :]
                s = b.ap.rearrange("p (a b) -> p a b", a=2)
                t = dve.do(lambda e, d=d, s=s: e.tensor_tensor(d, s, bc(rbc.unsqueeze(1), 128, 2, 256), ALU.mult), b.ready, t_rb)
                give(b, t)
                qtok.append(t)
    vtok = []

    def g_v(c):
        bk = gemm_n(W, 2048 + 512 * c, 512)
        ts = []
        for tb in range(2):
            ts.append(plain_evac(bk[tb], 0, 512, ov[:, tb, 512 * c:512 * c + 512], tb, xsc[tb]))
            give(bk[tb], ts[tb])
        vtok.append(ts)

    ytok = {}

    def retention():
        kscale = float(128 ** -0.5)

        def sc(h):
            b = banks.popleft()
            for jb in range(2):
                o = b.ap[:, jb * 256:jb * 256 + 256]
                t = pe.do(lambda e, o=o, jb=jb, h=h: e.matmul(o, okT[:, h, jb * 128:jb * 128 + 128], oqT[:, h, :],
                                                             start=True, stop=True), b.free, qtok, sig=jb == 1)
            a = ATs[h % 2]
            for jb in range(2):
                dd = dtab[:, h, 128 - jb * 128:128 - jb * 128 + 256]
                t2 = dve.do(lambda e, jb=jb, a=a, b=b, dd=dd: e.scalar_tensor_tensor(
                    a.ap[:, jb, :], b.ap[:, jb * 256:jb * 256 + 256], kscale, dd, ALU.mult, ALU.mult), t, a.free, t_dtab)
            a.ready = t2
            give(b, t2)

        def pv(h):
            a = ATs[h % 2]
            b = banks.popleft()
            for ib in range(2):
                for jb in range(2):
                    o = b.ap[:, ib * 256:ib * 256 + 256]
                    t = pe.do(lambda e, o=o, ib=ib, jb=jb, h=h, a=a: e.matmul(
                        o, a.ap[:, jb, ib * 128:ib * 128 + 128], ov[:, jb, h * 256:h * 256 + 256],
                        start=jb == 0, stop=jb == 1), b.free, a.ready, vtok[h // 2], sig=(ib == 1 and jb == 1))
            a.free = [t]
            st6, mv = stats(12), stats(4)
            for ib in range(2):
                t1 = dve.do(lambda e, ib=ib, st6=st6, b=b: e.bn_stats(st6[:, ib * 6:ib * 6 + 6], b.ap[:, ib * 256:ib * 256 + 256]), t)
            for ib in range(2):
                t1 = dve.do(lambda e, ib=ib, st6=st6, mv=mv: e.bn_aggr(mv[:, 2 * ib:2 * ib + 2], st6[:, ib * 6:ib * 6 + 6]), t1)
            t1 = rstd(mv[:, 1:4:2], 2, 1.0, GN_EPS, t1)
            for ib in range(2):
                t1 = dve.do(lambda e, ib=ib, mv=mv, b=b, h=h: e.tensor_scalar(
                    oy[:, ib, h * 256:h * 256 + 256], b.ap[:, ib * 256:ib * 256 + 256],
                    mv[:, 2 * ib:2 * ib + 1], mv[:, 2 * ib + 1:2 * ib + 2], ALU.subtract, ALU.mult), t1)
            give(b, t1)
            ytok[h] = t1

        for h in range(9):
            if h < 8:
                sc(h)
            if h >= 1:
                pv(h - 1)
            yield

    gen = retention()
    g_v(0)
    for c in range(1, 4):
        g_v(c)
        next(gen)
        next(gen)
    acc = acc_open()
    utok = {}

    def u_T(k):
        to_T(oy, ur[k % 2], list(range(4 * k, 4 * k + 4)), 0, G_GN, [utok[(k, 0)], utok[(k, 1)]])

    def u_acc(k, j):
        gemm_acc(acc, "w_out_o", (4 * k + 2 * j) * 128, ur[k % 2], 2 * j, k == 0 and j == 0, k == 3 and j == 1)

    for c in range(4):
        bk = gemm_n(W, 4096 + 512 * c, 512, mid=(lambda: u_T(c - 1)) if c else None)
        for _ in range(2):
            next(gen, None)
        for tb in range(2):
            g, b, sc = GT[tb], bk[tb], xsc[tb]
            t = act.do(lambda e, g=g, b=b, sc=sc: e.activation(g.ap, b.ap, ACT.Tanh, scale=sc["h"]), b.ready, g.free, sc["t"])
            t = dve.do(lambda e, g=g, b=b: e.scalar_tensor_tensor(g.ap, g.ap, 1.0, b.ap, ALU.add, ALU.mult), t)
            give(b, t)
            y = oy[:, tb, 512 * c:512 * c + 512]
            t = dve.do(lambda e, g=g, y=y, sc=sc: e.scalar_tensor_tensor(y, g.ap, sc["h"], y, ALU.mult, ALU.mult), t,
                       ytok[2 * c], ytok[2 * c + 1])
            g.free = [t]
            utok[(c, tb)] = t
        if c:
            u_acc(c - 1, 0)
            if c == 3:
                u_T(3)
            u_acc(c - 1, 1)
    u_acc(3, 0)
    u_acc(3, 1)
    for _ in gen:
        pass
    xr = acc_close(acc)

    MQ, MK, MV, DQ, DK, DV, XQ, XK, XV, SG, DM, IQ, UU, TT = (
        0, 1024, 2048, 3072, 4096, 5120, 6144, 7168, 8192, 9216, 12288, 3072, 0, 2048)
    MT, MR, MJ = 6144, 9216, 13184
    memT, memr = av(MT, 2048, 8), av(MR, 2048, 2)
    msc = []

    class Halves:

        def __init__(self, i):
            self.i = i

        def __getitem__(self, key):
            return ur[key[1] // 4].ap[self.i][:, key[1] % 4, key[2]]

    mT = Buf((Halves(0), Halves(1)))
    mT.ready = {}

    def split_mem(half_):
        u = ur[half_]
        for k in range(4 * half_, 4 * half_ + 4):
            g = gain[:, G_MEM + k:G_MEM + k + 1]
            dh, dl = u.ap[0][:, k % 4, :], u.ap[1][:, k % 4, :]
            t = act.do(lambda e, k=k, dh=dh, g=g: e.activation(dh, memT[:, k, :], ACT.Copy, scale=g), (S["s_m"], 32), u.free)
            mT.ready[k] = dve.do(lambda e, k=k, dh=dh, dl=dl, g=g: e.scalar_tensor_tensor(
                dl, memT[:, k, :], g, dh.bitcast(F32), ALU.mult, ALU.subtract), t, u.free)

    mrb = []

    def mem_rows(j):
        if j == 1:
            w = [q.last() for q in (act, dve, pe, pool)]
            dma(sp, memT, A["memT"].rearrange("(t p) n -> p t n", p=128), "s_m", *w)
            dma(sp, memr, A["mem"].rearrange("a (t p) n -> p (a t) n", p=128), "s_m", *w)
        if j == 5:
            msc.extend(row_scales(memr, av(MJ, 2048, 2), [(S["s_m"], 32)] * 2))
        if j == 8:
            mrb.append(row_broadcast(msc, *(q.last() for q in (act, dve, pe))))
        if j == 15:
            split_mem(0)

    xr = mlp(1, G_MLP1, xr, mem_rows)

    boundary()
    dqT, dkT, dv = av(DQ, 1024, 4), av(DK, 1024, 4), av(DV, 1024, 2)
    mqT, mkT, mvv = av(MQ, 1024, 4), av(MK, 1024, 4), av(MV, 1024, 2)
    iqT, ikT = av(IQ, 1024, 4), av(IQ + 1024, 256)
    xqT, xkT, xv = av(XQ, 1024, 4), av(XK, 1024, 4), av(XV, 1024, 2)
    sg = [av(SG + 1024 * i, 1024, 2) for i in range(3)]
    msk = av(DM, 512, 2)
    o = scratch(12800)
    R1 = [Buf(av(o + 512 * i, 512)) for i in range(2)]
    R2 = [Buf(av(o + 1024 + 512 * i, 512)) for i in range(2)]
    o += 2048
    iwt = av(o, 16, 2)
    hnx = av(SG, 2048, 2)
    split_mem(1)
    t_rb = mrb[0]
    for c in range(2):
        b, = gemm_t("w_mem", c * 256, 256, xT=mT)
        t = dve.do(lambda e, b=b, c=c: e.tensor_tensor(xkT[:, 2 * c:2 * c + 2, :], b.ap.rearrange("p (a b) -> p a b", a=2),
                                                      bc(rbc.unsqueeze(1), 128, 2, 256), ALU.mult), b.ready, t_rb, mT.ready[7])
        give(b, t)
    rX = [t]
    t_rbfree = t
    to_T(x3, hT, list(range(8)), 0, G_IN, xr)
    xsc = row_scales(x3, hnx, xr)
    bk = gemm_n("w_mem", 512, 512, xT=mT)
    for tb in range(2):
        t = plain_evac(bk[tb], 0, 512, xv[:, tb, :], tb, msc[tb], mT.ready[7])
        give(bk[tb], t)
        rX.append(t)
    for u in ur:
        u.free = [bk[1].ready]
        u.ready = None

    cos, sin = v3(cst, 2, C_COS, 128), v3(cst, 2, C_SIN, 128)
    rc = [0]

    def rope(b, tb, c0, nh, dst, rdy, dup=False):
        i = rc[0] % 2
        rc[0] += 1
        r1, r2 = R1[i], R2[i]
        w = nh * 64
        src = b.ap[:, c0:c0 + w].rearrange("p (h d) -> p h d", d=64)
        a = r1.ap[:, 0:w].rearrange("p (h d) -> p h d", d=64)
        c = r2.ap[:, 0:w].rearrange("p (h d) -> p h d", d=64)
        ct, s_t = cos[:, tb, :], sin[:, tb, :]
        sc = xsc[tb]
        t1 = dve.do(lambda e: e.scalar_tensor_tensor(a, src, sc["r"], bc(ct.unsqueeze(1), 128, nh, 64), ALU.mult, ALU.mult),
                    b.ready, r1.free, sc["t"])
        for q in range(2):
            t2 = dve.do(lambda e, q=q: e.scalar_tensor_tensor(
                c[:, :, q * 32:q * 32 + 32], src[:, :, 32 - q * 32:64 - q * 32], sc["r"],
                bc(s_t[:, q * 32:q * 32 + 32].unsqueeze(1), 128, nh, 32), ALU.mult, ALU.mult),
                        b.ready, r2.free)
        if dup:
            pool.do(lambda e: e.tensor_tensor(r2.ap[:, 64:128], r1.ap[:, 0:64], r2.ap[:, 0:64], ALU.add), t1, t2)
            t3 = pool.do(lambda e: e.tensor_tensor(r1.ap[:, 0:64], r1.ap[:, 0:64], r2.ap[:, 0:64], ALU.add), t1, t2)
            t3 = pool.do(lambda e: e.tensor_copy(r1.ap[:, 64:128], r2.ap[:, 64:128]), t3)
            w = 128
        else:
            t3 = pool.do(lambda e: e.tensor_tensor(r1.ap[:, 0:w], r1.ap[:, 0:w], r2.ap[:, 0:w], ALU.add), t1, t2)
        r2.free = [t3]
        nb = w // 128

        def later():
            tbk = banks.popleft()
            for j in range(nb):
                t = pe.do(lambda e, j=j: e.transpose(tbk.ap[:, j * 128:j * 128 + 128], r1.ap[:, j * 128:j * 128 + 128], ident),
                          tbk.free, t3, s_ident, sig=j == nb - 1)
            r1.free = [t]
            d = dst[:, 0:nb, tb * 128:tb * 128 + 128]
            s = tbk.ap[:, 0:nb * 128].rearrange("p (a b) -> p a b", a=nb)
            t = act.do(lambda e: e.activation(d, s, ACT.Copy), t)
            give(tbk, t)
            rdy.append(t)
        pend.append(later)
        return t2

    W = "w_in_2"

    def g_rope(c0, dst, rdy):
        bk = yield from gemm_ng(W, c0, 512)
        run_pend()
        for tb in range(2):
            give(bk[tb], rope(bk[tb], tb, 0, 8, dst, rdy))

    def g_plain(c0, dst, rdy):
        bk = yield from gemm_ng(W, c0, 512)
        run_pend()
        for tb in range(2):
            t = plain_evac(bk[tb], 0, 512, dst[:, tb, :], tb, xsc[tb])
            give(bk[tb], t)
            rdy.append(t)

    tsg = {}

    def g_silu(c0, i):
        bk = yield from gemm_ng(W, c0, 512)
        run_pend()
        for tb in range(2):
            b, d, sc = bk[tb], sg[i][:, tb, :], xsc[tb]
            t = act.do(lambda e, b=b, d=d, sc=sc: e.activation(d, b.ap, ACT.Tanh, scale=sc["h"]), b.ready, sc["t"])
            t = dve.do(lambda e, b=b, d=d: e.scalar_tensor_tensor(d, d, 1.0, b.ap, ALU.add, ALU.mult), t)
            give(b, t)
            t = dve.do(lambda e, d=d, sc=sc: e.tensor_scalar(d, d, sc["h"], None, ALU.mult), t)
        tsg[i] = t

    rI, rM, rD = [], [], []
    finish_gen(g_rope(4096, iqT, rI))
    t_rb = row_broadcast(xsc, t_rbfree)
    bk = gemm_n(W, 4608, 72)
    run_pend()
    for tb in range(2):
        t = rope(bk[tb], tb, 0, 1, ikT.rearrange("p (a b) -> p a b", a=1), rI, dup=True)
        t = dve.do(lambda e, tb=tb, b=bk[tb]: e.tensor_scalar(
            iwt[:, tb, :], b.ap[:, 64:72], xsc[tb]["r"], float(8 ** -0.5) * 0.125, ALU.mult, ALU.mult), t)
        give(bk[tb], t)
    t_iw = t
    caus = cst[:, C_CA:C_CA + 256]
    mtok = {}

    def index():
        for qb in range(2):
            nk = 128 + 128 * qb
            m = msk[:, qb, 0:nk]
            ca = caus[:, 256 - nk:256]
            t = dve.do(lambda e, m=m, ca=ca: e.tensor_copy(m, ca), s_const)
            for i, hs in enumerate(PAIRS):
                b = banks.popleft()
                for j, h in enumerate(hs):
                    o = b.ap[:, j * 256:j * 256 + nk]
                    hf = (h % 2) * 64
                    tp = pe.do(lambda e, o=o, h=h, hf=hf, qb=qb, nk=nk: e.matmul(
                        o, iqT[hf:hf + 64, h // 2, qb * 128:qb * 128 + 128], ikT[hf:hf + 64, 0:nk],
                        start=True, stop=True), b.free, rI, t_iw, sig=j == 1)
                Sb = scr["S"][i % NBUF]
                s = Sb.ap[:, :, 0:nk]
                bb = b.ap.rearrange("p (a b) -> p a b", a=2)[:, :, 0:nk]
                tr = act.do(lambda e, s=s, bb=bb: e.activation(s, bb, ACT.Relu), tp, Sb.free)
                give(b, tr)
                for j, h in enumerate(hs):
                    t = dve.do(lambda e, s=s, j=j, h=h, m=m, qb=qb: e.scalar_tensor_tensor(
                        m, s[:, j, :], iwt[:, qb, h:h + 1], m, ALU.mult, ALU.add), tr, t, t_iw)
                Sb.free = [t]
                if i % 2:
                    yield
            mtok[qb] = t
        ms = [(qb, msk[:, qb, 0:128 + 128 * qb], stats(8)) for qb in range(2)]
        for r in range(8):
            for qb, m, m8 in ms:
                mtok[qb] = dve.do(lambda e, m=m, m8=m8: e.max(m8, m), mtok[qb])
            for qb, m, m8 in ms:
                mtok[qb] = dve.do(lambda e, m=m, m8=m8: e.match_replace(m, m8, m, MARK), mtok[qb])
            if r % 2:
                yield
        for qb, m, m8 in ms:
            ca = caus[:, 128 - 128 * qb:256]
            t = dve.do(lambda e, m=m: e.tensor_scalar(m, m, -3.2e38, NEG, ALU.is_gt, ALU.mult), mtok[qb])
            mtok[qb] = dve.do(lambda e, m=m, ca=ca: e.tensor_tensor(m, m, ca, ALU.add), t)

    def take(g, n):
        for _ in range(n):
            next(g)
            yield

    ix = index()

    def mlist(*fs):
        for f in fs:
            g = f()
            if g is not None:
                yield from g
            yield

    def skip(g, n):
        for _ in range(n):
            yield
        yield from g

    drive(mlist(lambda: g_rope(0, mqT, rM), lambda: g_rope(512, mkT, rM), lambda: g_plain(1024, mvv, rM),
                lambda: g_silu(1536, 0)), skip(take(ix, 4), 1))

    def f_xq():
        for c in range(2):
            b, = gemm_t(W, 4680 + c * 256, 256)
            t = dve.do(lambda e, b=b, c=c: e.tensor_tensor(
                xqT[:, 2 * c:2 * c + 2, :], b.ap.rearrange("p (a b) -> p a b", a=2),
                bc(rbc.unsqueeze(1), 128, 2, 256), ALU.mult), b.ready, t_rb)
            give(b, t)
            rX.append(t)
            if c == 0:
                yield

    def gated_out(i):
        toks = {}
        def finish(qb, b, sm):
            nh = 4 if i == 2 else 8
            r = stats(8)
            t = dve.do(lambda e: e.reciprocal(r[:, 0:nh], sm[:, 0:nh]), act.last())
            d = sg[i][:, qb, :]
            hd = 512 // nh
            t1 = dve.do(lambda e: e.tensor_tensor(d, b.ap, d, ALU.mult), b.ready, tsg[i])
            give(b, t1)
            d3 = d.rearrange("p (h d) -> p h d", h=nh)
            toks[qb] = dve.do(lambda e: e.tensor_tensor(d3, d3, bc(r[:, 0:nh].unsqueeze(2), 128, nh, hd), ALU.mult), t, t1)
        return finish, toks

    uT, tT = av(UU, 2048, 8), av(TT, 1024, 4)
    hb = lgt[:, 8:32]
    t_hb = pool.do(lambda e: e.tensor_scalar(hb, gain[:, G_BM:G_BM + 24], 0.5, None, ALU.mult), s_const)
    state_u = dict(tfree=[])

    names = {0: "w_up_moba", 1: "w_up_dsa", 2: "w_up_cross"}
    finM, tokM = gated_out(0)
    finX, tokX = gated_out(2)
    cfgM = dict(scale=0.125, ready=s_const,
                tab=lambda qb, hs: bc(caus[:, 128 - 128 * qb:256].unsqueeze(1), 128, 2, 128 + 128 * qb))
    cfgX = dict(scale=float(128 ** -0.5), ready=None, tab=None)

    def merge(i, toks, first):
        u = ur[urn[0] % 2]
        urn[0] += 1
        for g in range(2):
            for c in range(2):
                b, = gemm_t(W, 5704 + 1024 * i + 512 * g + 256 * c, 256)
                d = tT[:, 2 * c:2 * c + 2, :]
                t = dve.do(lambda e, b=b, d=d: e.tensor_tensor(
                    d, b.ap.rearrange("p (a b) -> p a b", a=2), bc(rbc.unsqueeze(1), 128, 2, 256), ALU.mult),
                    b.ready, t_rb, state_u["tfree"])
                give(b, t)
                for m in range(2):
                    k = 4 * g + 2 * c + m
                    d = tT[:, 2 * c + m, :]
                    tt_ = act.do(lambda e, d=d, k=k: e.activation(
                        d, d, ACT.Tanh, bias=hb[:, 8 * i + k:8 * i + k + 1], scale=0.5), t, t_hb)
                if g == 0 and c == 0:
                    to_T(sg[i], u, [0, 1, 2, 3], 0, None, [toks[0], toks[1]])
                yield
            bks = gemm_t(names[i], 512 * g, 512, nk=4, xT=u)
            for n, b in enumerate(bks):
                tt = tT[:, 2 * n:2 * n + 2, :]
                dd = uT[:, 4 * g + 2 * n:4 * g + 2 * n + 2, :]
                b3 = b.ap.rearrange("p (a b) -> p a b", a=2)
                dst = dd if first else tt
                t1 = dve.do(lambda e, tt=tt, b3=b3, dst=dst: e.scalar_tensor_tensor(dst, tt, 1.0, b3, ALU.add, ALU.mult),
                            b.ready, tt_)
                give(b, t1)
                if not first:
                    t1 = dve.do(lambda e, dd=dd, tt=tt: e.tensor_tensor(dd, dd, tt, ALU.add), t1)
            state_u["tfree"] = [t1]
            state_u[g] = t1
            if g == 1:
                u.free = [bks[-1].ready]
            yield

    def all_of(*gs):
        for g in gs:
            yield from g

    drive(attention(U8, [128, 256], qT_of(mqT), kT_of(mkT), lambda h, kb: mvv[:, kb, h * 64:h * 64 + 64],
                    soft_common(cfgM), 64, None, finM, rM),
          mlist(lambda: g_rope(2048, dqT, rD), lambda: g_rope(2560, dkT, rD), lambda: g_plain(3072, dv, rD),
                lambda: g_silu(3584, 1)), ix)
    cfgD = dict(scale=0.125, ready=[mtok[0], mtok[1]],
                tab=lambda qb, hs: bc(msk[:, qb, 0:128 + 128 * qb].unsqueeze(1), 128, 2, 128 + 128 * qb))
    finD, tokD = gated_out(1)
    for q in (act, dve, pe, pool):
        q.wait(tokM[0], tokM[1])
    drive(attention(U8, [128, 256], qT_of(dqT), kT_of(dkT), lambda h, kb: dv[:, kb, h * 64:h * 64 + 64],
                    soft_common(cfgD), 64, None, finD, rD),
          all_of(mlist(f_xq), merge(0, tokM, True)))
    drive(attention(U4, [256, 256], lambda h, qb: xqT[:, h, qb * 128:qb * 128 + 128], lambda h, nk: xkT[:, h, 0:nk],
                    lambda h, kb: xv[:, kb, h * 128:h * 128 + 128], soft_common(cfgX), 128, None, finX, rX),
          all_of(mlist(lambda: g_silu(5192, 2)), merge(1, tokD, False)))

    def split_u(g):
        u = ur[urn[0] % 2]
        urn[0] += 1
        u.ready = {}
        for i in range(2):
            src = uT[:, 4 * g + 2 * i:4 * g + 2 * i + 2, :]
            dh, dl = u.ap[0][:, 2 * i:2 * i + 2, :], u.ap[1][:, 2 * i:2 * i + 2, :]
            t = act.do(lambda e, dh=dh, src=src: e.activation(dh, src, ACT.Copy, scale=0.5), state_u[g], u.free)
            u.ready[2 * i] = u.ready[2 * i + 1] = dve.do(lambda e, dh=dh, dl=dl, src=src: e.scalar_tensor_tensor(
                dl, src, 0.5, dh.bitcast(F32), ALU.mult, ALU.subtract), t, u.free)
        return u

    mg = merge(2, tokX, False)
    for _ in range(4):
        next(mg)
    u0 = split_u(0)
    drive(mg)
    u1 = split_u(1)
    acc = acc_open()
    for g, u in ((0, u0), (1, u1)):
        for j in range(2):
            gemm_acc(acc, "w_out_2", (4 * g + 2 * j) * 128, u, 2 * j, g == 0 and j == 0, g == 1 and j == 1)
    xr = acc_close(acc)
    fin = av(3072, 2048, 2)
    for tb in range(2):
        ss = stats(1)
        f, x = fin[:, tb, :], x3[:, tb, :]
        t = act.do(lambda e, f=f, x=x, ss=ss: e.activation(f, x, ACT.Square, accum_out=ss), xr[tb], pe.last())
        t = rstd(ss, 1, 1.0 / 1024, EPS, t)
        for i in range(2):
            c = slice(512 * i, 512 * i + 512)
            t1 = dve.do(lambda e, f=f, x=x, ss=ss, c=c: e.scalar_tensor_tensor(
                f[:, c], x[:, c], ss, rows[:, R_FIN + c.start:R_FIN + c.stop], ALU.mult, ALU.mult), t)
            dma((sp, act)[i], out[0, tb * 128:tb * 128 + 128, c], f[:, c], "s_out", t1)
    sp.wait((S["s_out"], dma_n["s_out"]))
    return used, dict(sp=sp, act=act, dve=dve, pe=pe, pool=pool)


def shape_constants():
    import numpy as np
    c = np.zeros((128, NCONST), np.float32)
    p = np.arange(128)
    c[:, C_ID:C_ID + 128] = np.eye(128)
    for qb in range(2):
        rel = np.abs(np.arange(256)[None, :] - (p[:, None] + 128 * qb))
        c[:, C_NA + 256 * qb:C_NA + 256 * qb + 256] = np.where(rel <= 128, -rel, NEG)
    qc, kc = (p % 64)[:, None], np.arange(64)[None, :]
    cs = np.clip(qc - 8, 0, 48)
    c[:, C_MB:C_MB + 64] = np.where((kc >= cs) & (kc < cs + 16), 0.0, NEG)
    c[:, C_CA + 128:C_CA + 256] = np.where(p[None, :] <= p[:, None], 0.0, LOW)
    inv = np.power(np.float32(10000.0), -np.arange(32, dtype=np.float32) * np.float32(2.0) / np.float32(64)).astype(np.float32)
    for tb in range(2):
        ang = ((p + 128 * tb).astype(np.float32)[:, None] * inv[None, :]).astype(np.float32).astype(np.float64)
        co, si = np.cos(ang), np.sin(ang)
        c[:, C_COS + 64 * tb:C_COS + 64 * tb + 64] = np.concatenate([co, co], 1)
        c[:, C_SIN + 64 * tb:C_SIN + 64 * tb + 64] = np.concatenate([-si, si], 1)
    d = np.arange(384)[None, :] - 128 - p[:, None]
    c[:, C_U:C_U + 384] = np.maximum(d, 0)
    c[:, C_L:C_L + 384] = np.maximum(-d, 0)
    h = np.arange(8)
    c[:, C_IS:C_IS + 8] = 2.0 ** (h + 1)
    c[:, C_NS:C_NS + 8] = -(2.0 ** -(h + 1.0))
    return c


def layout(inputs):
    import numpy as np
    a = {k: np.asarray(v) for k, v in inputs.items()}

    def cols(v):
        return v.reshape(-1, 128).T

    def twice(v):
        return np.concatenate([v, v])[:, None]

    gains = np.concatenate([
        cols(a["attn_norm_e"][0]), cols(a["mlp_norm"][0]), cols(a["ret_norm_o"][0]), cols(a["mlp_norm"][1]),
        cols(a["g_in_2"][0]), cols(a["g_mem_2"][0]), cols(a["ret_gn_o"][0]), cols(a["b_merge_2"][0]),
        twice(a["q_norm_a"][0]), twice(a["k_norm_a"][0]), twice(a["q_norm_b"][0]), twice(a["k_norm_b"][0])], 1)
    rowvec = np.concatenate([a["g_final_2"], a["sink_a"][0], a["decay_fwd_o"][0], a["decay_bwd_o"][0]])[None, :]
    rpb = np.full((64, 8, 7, 64), NEG, np.float32)
    for q in range(64):
        k0 = min(max(q - 8, 0), 48)
        rpb[q, :, :, k0:k0 + 16] = a["rpb_b"][0][:, 4:11, k0 - q + 15:k0 - q + 31]
    rpb = rpb.reshape(64, 56, 64)
    return dict(
        x=a["x"], xT=a["x"][0].T, mem=a["mem_2"], memT=a["mem_2"][0].T, gains=gains, rowvec=rowvec, rpb=rpb, consts=shape_constants(),
        w_in_e=a["w_in_e"][0], w_out_e=a["w_out_e"][0], w_in_o=a["w_in_o"][0], w_out_o=a["w_out_o"][0],
        w1_0=a["w_mlp_in"][0], w1_1=a["w_mlp_in"][1], w2_0=a["w_mlp_out"][0], w2_1=a["w_mlp_out"][1],
        w_in_2=a["w_in_2"][0], w_mem=a["w_mem_kv_2"][0], w_up_moba=a["w_up_moba_2"][0],
        w_up_dsa=a["w_up_dsa_2"][0], w_up_cross=a["w_up_cross_2"][0], w_out_2=a["w_out_2"][0])


def kernel(**inputs):
    import numpy as np
    import concourse.bacc as bacc
    from concourse.bass_utils import run_bass_kernel_spmd

    nc = bacc.Bacc("TRN2", target_bir_lowering=False, num_devices=1)
    arrays, args = {}, {}
    for name, a in layout(inputs).items():
        a = np.ascontiguousarray(a)
        arrays[f"in_{name}"] = a
        args[name] = nc.dram_tensor(f"in_{name}", a.shape, mybir.dt.from_np(a.dtype), kind="ExternalInput").ap()
    out = nc.dram_tensor("out", (1, 256, 1024), F32, kind="ExternalOutput").ap()
    program(nc, args, out)
    r = run_bass_kernel_spmd(nc, [arrays], core_ids=[0])
    return r.results[0]["out"]
```

```python
from contextlib import ExitStack
from collections import deque

import concourse.bass as bass
from concourse import mybir

F32 = mybir.dt.float32
F32R = mybir.dt.float32r
ALU = mybir.AluOpType
ACT = mybir.ActivationFunctionType
AXX = mybir.AxisListType.X

NEG = -1.0e30
LOW = -3.0e38
MARK = -3.3e38
EPS = 1e-6
GN_EPS = 1e-5

G_ATT, G_MLP0, G_RET, G_MLP1, G_IN, G_MEM, G_GN, G_BM, G_QA, G_KA, G_QB, G_KB = (
    0, 8, 16, 24, 32, 40, 48, 64, 88, 89, 90, 91)
NGAIN = 92
R_FIN, R_SINK, R_DF, R_DB = 0, 1024, 1032, 1040
NROW = 1048
C_ID, C_NA, C_CA, C_COS, C_SIN, C_U, C_L, C_IS, C_NS = (
    0, 128, 640, 896, 1024, 1152, 1536, 1920, 1928)
NCONST = 1936

NRAW = 4
NHI = 6
NLO = 5
LOOK = 4
ARENA = 19216


class Eng:

    def __init__(self, sem):
        self.sem, self.ops, self.count, self.seen = sem, [], 0, {}

    def wait(self, *tokens):
        for t in tokens:
            if t is None:
                continue
            if isinstance(t, list):
                self.wait(*t)
                continue
            sem, value = t
            if self.seen.get(sem, 0) < value:
                self.seen[sem] = value
                self.ops.append(lambda e, s=sem, v=value: e.wait_ge(s, v))

    def do(self, fn, *tokens, sig=True):
        self.wait(*tokens)
        if not sig:
            self.ops.append(fn)
            return None
        self.count += 1
        self.ops.append(lambda e: fn(e).then_inc(self.sem, 1))
        return (self.sem, self.count)

    def last(self):
        return (self.sem, self.count) if self.count else None

    def run(self, e):
        for op in self.ops:
            op(e)


class Buf:

    def __init__(self, ap):
        self.ap, self.free, self.ready = ap, [], None

    def part(self, k):
        return self.ready[k] if isinstance(self.ready, dict) else self.ready


def program(nc, A, out):
    with ExitStack() as st:
        def sb(name, n, dt=F32):
            return st.enter_context(nc.sbuf_tensor(name, [128, n], dt))

        raw = [sb(f"raw{i}", 2048) for i in range(NRAW)]
        whi = [sb(f"whi{i}", 1024, F32R) for i in range(NHI)]
        wlo = [sb(f"wlo{i}", 1024, F32R) for i in range(NLO)]
        xs = sb("xs", 2048)
        hTh, hTl = sb("hTh", 2048, F32R), sb("hTl", 2048, F32R)
        urh = [sb(f"urh{i}", 1024, F32R) for i in range(2)]
        url = [sb(f"url{i}", 1024, F32R) for i in range(2)]
        arena = sb("arena", ARENA)
        gain = sb("gain", NGAIN)
        rows = sb("rows", NROW)
        cst = sb("cst", NCONST)
        stat = sb("stat", 640)
        lgt = sb("lgt", 128)
        psum = [st.enter_context(nc.psum_tensor(f"ps{i}", [128, 512], F32)) for i in range(8)]
        sems = {n: st.enter_context(nc.semaphore(n)) for n in
                ["s_pe", "s_act", "s_dve", "s_pool", "s_c", "s_id", "s_x0", "s_x1", "s_w", "s_t0", "s_t1", "s_g", "s_b", "s_m", "s_out"]
                + [f"s_raw{i}" for i in range(NRAW)]}
        mem = dict(raw=raw, whi=whi, wlo=wlo, xs=xs, hTh=hTh, hTl=hTl, urh=urh, url=url, arena=arena,
                   gain=gain, rows=rows, cst=cst, stat=stat, lgt=lgt, psum=psum)
        order = emit(A, out, mem, sems, None)[0]
        engines = emit(A, out, mem, sems, order)[1]
        block = st.enter_context(nc.Block())
        for name, deco in (("sp", block.sync), ("act", block.scalar), ("dve", block.vector),
                           ("pe", block.tensor), ("pool", block.gpsimd)):
            deco(lambda e, n=name: engines[n].run(e))


def emit(A, out, mem, sems, order):
    S = sems
    sp = Eng(None)
    act, dve, pe, pool = (Eng(S[n]) for n in ("s_act", "s_dve", "s_pe", "s_pool"))
    raw, whi, wlo, xs = mem["raw"], mem["whi"], mem["wlo"], mem["xs"]
    arena, gain, rows, cst, stat, lgt = (mem[n] for n in ("arena", "gain", "rows", "cst", "stat", "lgt"))

    def v3(t, a, off=0, n=None):
        n = n or 2048
        return t[:, off:off + n].rearrange("p (a b) -> p a b", a=a)

    def av(off, n, a=None):
        assert off + n <= ARENA, (off, n)
        r = arena[:, off:off + n]
        return r if a is None else r.rearrange("p (a b) -> p a b", a=a)

    def bc(ap, *shape):
        return ap.broadcast_to(list(shape))

    banks = deque(Buf(t[:, :]) for t in mem["psum"])

    def give(b, *tokens):
        b.free = list(tokens)
        banks.append(b)

    dma_n = {}

    def dma(q, dst, src, sem, *waits):
        dma_n[sem] = dma_n.get(sem, 0) + 16
        q.do(lambda e: e.dma_start(dst, src).then_inc(S[sem], 16), *waits, sig=False)

    used, halves, done = [], [], []
    state = dict(dma=0, lo=0)
    after_dma = {}

    def issue_dma(m):
        name, k0, nk, c0, n, _ = order[2 * m]
        src = A[name][k0:k0 + nk * 128, c0:c0 + n].rearrange("(t p) n -> p t n", p=128)
        dst = raw[m % NRAW][:, 0:nk * n].rearrange("p (t n) -> p t n", t=nk)
        waits = [halves[2 * (m - NRAW) + 1]["lo"]] if m >= NRAW else []
        if m == 0:
            h = nk // 2
            d0, s0 = dst[:, 0:h, :], src[:, 0:h, :]
            sp.do(lambda e: e.dma_start(d0, s0).then_inc(S["s_w"], 16), sig=False)
            src, dst = src[:, h:nk, :], dst[:, h:nk, :]
        sp.do(lambda e: e.dma_start(dst, src).then_inc(S[f"s_raw{m % NRAW}"], 16), *waits, sig=False)
        if m in after_dma:
            after_dma[m]()

    def issue_split(i, low):
        m, x = i // 2, i % 2
        name, k0, nk, c0, n, by = order[i]
        r = raw[m % NRAW][:, 0:nk * n].rearrange("p (t n) -> p t n", t=nk)
        if by == "k":
            nk //= 2
            r = r[:, x * nk:x * nk + nk, :]
        else:
            n //= 2
            r = r[:, :, x * n:x * n + n]
        h, l = (t[i % d][:, 0:nk * n].rearrange("p (t n) -> p t n", t=nk) for t, d in ((whi, NHI), (wlo, NLO)))
        arrived = (S[f"s_raw{m % NRAW}"], 16 * (m // NRAW + 1)) if i else (S["s_w"], 16)
        if low:
            halves[i]["lo"] = dve.do(lambda e: e.tensor_tensor(l, r, h.bitcast(F32), ALU.subtract), arrived,
                                     halves[i]["hi"], done[i - NLO] if i >= NLO else None)
            return
        th = act.do(lambda e: e.activation(h, r, ACT.Copy), arrived, done[i - NHI] if i >= NHI else None)
        halves.append(dict(hi=th, h=h, l=l))

    def next_half(name, k0, nk, c0, n, by):
        i = len(used)
        used.append((name, k0, nk, c0, n, by))
        if order is None:
            a, b = (nk // 2, n) if by == "k" else (nk, n // 2)
            z = whi[0][:, 0:a * b].rearrange("p (t n) -> p t n", t=a)
            return dict(hi=None, lo=None, h=z, l=z)
        assert order[i] == used[i]
        split_until(i + LOOK)
        return halves[i]

    def split_until(end):
        n = len(order or ())
        while state["lo"] < min(end, n):
            while len(halves) < min(state["lo"] + 2, n):
                while state["dma"] < min(len(halves) // 2 + NRAW, n // 2):
                    m = state["dma"]
                    if m >= NRAW and state["lo"] < 2 * (m - NRAW) + 2:
                        break
                    issue_dma(m)
                    state["dma"] += 1
                issue_split(len(halves), False)
            issue_split(state["lo"], True)
            state["lo"] += 1

    def peek_half(desc):
        if order is None:
            return dict(hi=None, lo=None, h=whi[0][:, 0:1024].unsqueeze(1), l=whi[0][:, 0:1024].unsqueeze(1))
        assert order[len(used)] == desc
        return halves[len(used)]

    def half_done(tok):
        done.append(tok)

    def mm3(o, pairs, start, stop, *waits, sig=False):
        t = None
        for i, (a, b) in enumerate(pairs):
            last = i == len(pairs) - 1
            t = pe.do(lambda e, a=a, b=b, s=start and i == 0, p=stop and last:
                      e.matmul(o, a, b, start=s, stop=p), *(waits if i == 0 else ()), sig=sig and last)
        return t

    hT = Buf((v3(mem["hTh"], 8), v3(mem["hTl"], 8)))
    ur = [Buf((v3(h, 4, 0, 1024), v3(l, 4, 0, 1024))) for h, l in zip(mem["urh"], mem["url"])]
    urn = [0]

    def finish_gen(g):
        while True:
            try:
                next(g)
            except StopIteration as e:
                return e.value

    def gemm_n(*a, **k):
        return finish_gen(gemm_ng(*a, **k))

    def gemm_ng(name, c0, n, xT=None, mid=None):
        xT = xT or hT
        bk = [banks.popleft() for _ in range(2)]
        nk = 4 if n > 256 else 8
        tok = [None, None]
        for k0 in range(0, 8, nk):
            for x in range(2):
                t = next_half(name, k0 * 128, nk, c0, n, "k")
                for tb in range(2):
                    for k in range(nk // 2):
                        kk = k0 + x * nk // 2 + k
                        xh = xT.ap[0][:, kk, tb * 128:tb * 128 + 128]
                        xl = xT.ap[1][:, kk, tb * 128:tb * 128 + 128]
                        end = k == nk // 2 - 1
                        w = (bk[tb].free, xT.part(kk), t["hi"], t["lo"])
                        tok[tb] = mm3(bk[tb].ap[:, 0:n], [(xh, t["h"][:, k, :]), (xh, t["l"][:, k, :]), (xl, t["h"][:, k, :])],
                                      kk == 0, kk == 7, *w, sig=end)
                half_done(tok[1])
                yield
                if mid and k0 + x * nk // 2 == 8 // 2 - nk // 2:
                    mid()
        for b, t in zip(bk, tok):
            b.ready = t
        return bk

    def gemm_t(*a, **k):
        return finish_gen(gemm_tg(*a, **k))

    def gemm_tg(name, c0, n, nk=8, xT=None):
        xT = xT or hT
        res = []
        for m in range(n // 128):
            if m % (n // 256) == 0:
                t, m0 = next_half(name, 0, nk, c0, n, "n"), m
            if m % 2 == 0:
                b = banks.popleft()
                res.append(b)
            o = b.ap[:, (m % 2) * 256:(m % 2) * 256 + 256]
            for k in range(nk):
                c = (m - m0) * 128
                wh, wl = t["h"][:, k, c:c + 128], t["l"][:, k, c:c + 128]
                xh, xl = xT.ap[0][:, k, :], xT.ap[1][:, k, :]
                tok = mm3(o, [(wh, xh), (wh, xl), (wl, xh)], k == 0, k == nk - 1,
                          b.free, xT.part(k), t["hi"], t["lo"], sig=k == nk - 1)
            b.ready = tok
            if (m + 1) % (n // 256) == 0:
                half_done(tok)
                yield
        return res

    def acc_open():
        return [banks.popleft() for _ in range(4)]

    def gemm_acc(*a):
        return finish_gen(gemm_accg(*a))

    def gemm_accg(acc, name, k0, u, j, first, last):
        desc = (name, k0, 2, 0, 1024, "k")

        def part(t, k, tb, seq):
            uh = u.ap[0][:, j + k, tb * 128:tb * 128 + 128]
            ul = u.ap[1][:, j + k, tb * 128:tb * 128 + 128]
            bb = acc[2 * tb:2 * tb + 2]
            w = (bb[0].free, bb[1].free, u.part(j + k), t["hi"], t["lo"])
            passes = [(uh, "h"), (uh, "l"), (ul, "h")]
            for p, i in seq:
                x, which = passes[p]
                end = last and k == 1 and p == 2
                tok = mm3(bb[i].ap, [(x, t[which][:, 0, 512 * i:512 * i + 512])], first and k == 0 and p == 0, end, *w,
                          sig=end or (p, i) == seq[-1])
                w = ()
                if end:
                    bb[i].ready = tok
            return tok

        by_pass = [(p, i) for p in range(3) for i in range(2)]
        by_bank = [(p, i) for i in range(2) for p in range(3)]
        if last:
            t = [next_half(*desc), peek_half(desc)]
            tok = [part(t[k], k, tb, by_bank if k else by_pass) for tb in range(2) for k in range(2)]
            half_done(tok[2])
            next_half(*desc)
            half_done(tok[3])
            tok = tok[3]
        else:
            for k in range(2):
                t = next_half(*desc)
                for tb in range(2):
                    tok = part(t, k, tb, by_pass)
                half_done(tok)
                u.free = [tok]
                yield
        u.free = [tok]
        return tok

    def acc_close(acc, scale=None):
        toks = []
        for tb in range(2):
            for i in range(2):
                b = acc[2 * tb + i]
                o = xs[:, tb * 1024 + i * 512:tb * 1024 + i * 512 + 512]
                if scale:
                    sc, ts = scale[tb]
                    t = dve.do(lambda e, o=o, b=b, sc=sc: e.scalar_tensor_tensor(o, b.ap, sc, o, ALU.mult, ALU.add),
                               b.ready, ts)
                else:
                    t = dve.do(lambda e, o=o, b=b: e.tensor_tensor(o, o, b.ap, ALU.add), b.ready)
                give(b, t)
                toks.append(t)
        return toks

    ident = cst[:, C_ID:C_ID + 128]
    half = stat[:, 0:33]
    stn = [34]

    def stats(n):
        if stn[0] + n > 640:
            stn[0] = 34
        stn[0] += n
        return stat[:, stn[0] - n:stn[0]]

    def boundary():
        ts = [q.last() for q in (act, dve, pe, pool)]
        for q in (act, dve, pe, pool):
            q.wait(*ts)
        stn[0] = 34

    def rstd(ss, n, scale, eps, *waits):
        t = pool.do(lambda e: e.tensor_scalar(ss, ss, scale, eps, ALU.mult, ALU.add), *waits)
        return pool.do(lambda e: e.tensor_tensor(ss, ss, half[:, 0:n], ALU.pow), t)

    def row_scales(src, junk, ready):
        res = []
        for tb in range(2):
            i, rr, hh, i64 = (stats(1) for _ in range(4))
            t = act.do(lambda e, tb=tb, i=i: e.activation(junk[:, tb, :], src[:, tb, :], ACT.Square, accum_out=i), ready[2 * tb + 1])
            t = pool.do(lambda e, i=i: e.tensor_scalar(i, i, 1.0 / 1024, EPS, ALU.mult, ALU.add), t)
            ti = dve.do(lambda e, i=i: e.reciprocal(i, i), t)
            t = pool.do(lambda e, i=i, rr=rr: e.tensor_tensor(rr, i, half[:, 32:33], ALU.pow), ti)
            t64 = pool.do(lambda e, i=i, i64=i64: e.tensor_scalar(i64, i, 1.0 / 64, None, ALU.mult), ti)
            th = pool.do(lambda e, rr=rr, hh=hh: e.tensor_scalar(hh, rr, 0.5, None, ALU.mult), t)
            res.append(dict(i=i, r=rr, h=hh, i64=i64, t=th, ti=ti))
        return res

    ones, diag, rbc = cst[:, C_U:C_U + 128], cst[:, C_U + 128:C_U + 384], cst[:, C_L:C_L + 256]

    def row_broadcast(sc, *waits):
        for tb in range(2):
            td_ = pool.do(lambda e, tb=tb: e.tensor_scalar(diag[:, tb * 128:tb * 128 + 128], ident, sc[tb]["r"], None, ALU.mult),
                          sc[tb]["t"], *waits)

        def rest():
            b = banks.popleft()
            t = pe.do(lambda e: e.matmul(b.ap[:, 0:256], ones, diag, start=True, stop=True), b.free, td_, t_ones)
            t = act.do(lambda e: e.activation(rbc, b.ap[:, 0:256], ACT.Copy), t, *waits)
            give(b, t)
            return t
        return rest

    def split_x(srcT, gcol, dst, ready, *waits):
        dst.ready = {}
        for k in range(8):
            if k in (0, 2, 4):
                split_until(k // 2 + 1)
            g = gain[:, gcol + k:gcol + k + 1]
            dh, dl = dst.ap[0][:, k, :], dst.ap[1][:, k, :]
            t = act.do(lambda e, k=k, dh=dh, g=g: e.activation(dh, srcT[:, k, :], ACT.Copy, scale=g), ready[k // 2], *waits)
            dst.ready[k] = dve.do(lambda e, k=k, dh=dh, dl=dl, g=g: e.scalar_tensor_tensor(
                dl, srcT[:, k, :], g, dh.bitcast(F32), ALU.mult, ALU.subtract), t)

    def split_evac(dh, dl, src, scales, *waits):
        for h, s, g in zip(dh, src, scales):
            kw = {} if g is None else dict(scale=g)
            th = act.do(lambda e, h=h, s=s, kw=kw: e.activation(h, s, ACT.Copy, **kw), *waits)
        for h, l, s, g in zip(dh, dl, src, scales):
            if g is None:
                tl = dve.do(lambda e, h=h, l=l, s=s: e.tensor_tensor(l, s, h.bitcast(F32), ALU.subtract), th)
            else:
                tl = dve.do(lambda e, h=h, l=l, s=s, g=g: e.scalar_tensor_tensor(
                    l, s, g, h.bitcast(F32), ALU.mult, ALU.subtract), th)
        return tl

    def to_T(src, dst, kts, d0, gcol, ready, *waits, by_half=False):
        if not isinstance(dst.ready, dict):
            dst.ready = {}
        for i in range(0, len(kts), 2):
            b = banks.popleft()
            for j in range(2):
                for tb in range(2):
                    k = kts[i + j]
                    o = b.ap[:, j * 256 + tb * 128:j * 256 + tb * 128 + 128]
                    s = src[:, tb, k * 128:k * 128 + 128]
                    r = ready[2 + k // 4] if by_half else ready
                    t = pe.do(lambda e, o=o, s=s: e.transpose(o, s, ident), b.free, r, s_ident,
                              sig=(j == 1 and tb == 1))
            k, d = kts[i], d0 + i
            if gcol is None:
                tok = split_evac([dst.ap[0][:, d:d + 2, :]], [dst.ap[1][:, d:d + 2, :]],
                                 [b.ap.rearrange("p (a b) -> p a b", a=2)], [None], t, dst.free, *waits)
            else:
                tok = split_evac([dst.ap[0][:, d + j, :] for j in range(2)], [dst.ap[1][:, d + j, :] for j in range(2)],
                                 [b.ap[:, j * 256:j * 256 + 256] for j in range(2)],
                                 [gain[:, gcol + k + j:gcol + k + j + 1] for j in range(2)], t, dst.free, *waits)
            give(b, tok)
            dst.ready[d] = dst.ready[d + 1] = tok
        return tok

    pool.do(lambda e: e.memset(half[:, 0:32], -0.5))
    pool.do(lambda e: e.memset(half[:, 32:33], 0.5))
    dma(act, gain[:, :], A["gains"], "s_g")
    XT = 14080
    xT0 = av(XT, 2048, 8)
    for i, (a, b) in enumerate(((0, 2), (2, 8))):
        dma(act, xT0[:, a:b, :], A["xT"][a * 128:b * 128, :].rearrange("(t p) n -> p t n", p=128), f"s_t{i}")
    s_ident = (S["s_id"], 16)
    s_const = (S["s_c"], 32)
    x3 = v3(xs, 2)

    scr = {}

    def scratch(off):
        for name, n in (("S", 2), ("P", 3), ("T", 2)):
            scr[name] = [Buf(av(off + 512 * i, 512, None if name == "T" else 2)) for i in range(n)]
            off += 512 * n
        return off

    def attention(units, kmax, q_of, k_of, v_of, score, hd, vready, finish, ready, deep=False):
        n = len(units)
        ob = {}
        sums = {}

        def stage1(i):
            qb, hs = units[i]
            nk = kmax[qb]
            if qb not in sums:
                sums[qb] = stats(8)
            b = banks.popleft()
            for j, h in enumerate(hs):
                o = b.ap[:, j * 256:j * 256 + nk]
                t = pe.do(lambda e, o=o, h=h: e.matmul(o, q_of(h, qb), k_of(h, nk), start=True, stop=True),
                          b.free, ready, sig=j == 1)
            Sb, Pb = scr["S"][i % 2], scr["P"][i % 3]
            src, par, t2, freed = score(qb, hs, b.ap.rearrange("p (a b) -> p a b", a=2)[:, :, 0:nk],
                                        Sb.ap[:, :, 0:nk], (t, Sb.free))
            for j, h in enumerate(hs):
                scl, nm = par[j]
                po, si, ac = Pb.ap[:, j, 0:nk], src[:, j, :], sums[qb][:, h:h + 1]
                t3 = act.do(lambda e, po=po, si=si, ac=ac, scl=scl, nm=nm: e.activation(
                    po, si, ACT.Exp, bias=nm, scale=scl, accum_out=ac), t2, Pb.free)
            if freed is None:
                give(b, t3)
            else:
                give(b, freed)
                Sb.free = [t3]
            Pb.ready = t3

        def stage2(i):
            qb, hs = units[i]
            nk = kmax[qb]
            Pb, Tb = scr["P"][i % 3], scr["T"][i % 2]
            b = banks.popleft()
            nb = nk // 128
            for j in range(2):
                for kb in range(nb):
                    o = b.ap[:, (j * nb + kb) * 128:(j * nb + kb) * 128 + 128]
                    s = Pb.ap[:, j, kb * 128:kb * 128 + 128]
                    t = pe.do(lambda e, o=o, s=s: e.transpose(o, s, ident), b.free, Pb.ready, s_ident,
                              sig=(j == 1 and kb == nb - 1))
            Pb.free = [t]
            w = 2 * nk
            if i % 2:
                t = act.do(lambda e: e.activation(Tb.ap[:, 0:w], b.ap[:, 0:w], ACT.Copy), t, Tb.free)
            else:
                t = dve.do(lambda e: e.tensor_copy(Tb.ap[:, 0:w], b.ap[:, 0:w]), t, Tb.free)
            give(b, t)
            Tb.ready = t

        def stage3(i):
            qb, hs = units[i]
            nb = kmax[qb] // 128
            Tb = scr["T"][i % 2]
            if qb not in ob:
                ob[qb] = banks.popleft()
            b = ob[qb]
            for j, h in enumerate(hs):
                for kb in range(nb):
                    o = b.ap[:, h * hd:h * hd + hd]
                    s = Tb.ap[:, (j * nb + kb) * 128:(j * nb + kb) * 128 + 128]
                    t = pe.do(lambda e, o=o, s=s, kb=kb, h=h: e.matmul(o, s, v_of(h, kb), start=kb == 0, stop=kb == nb - 1),
                              b.free, Tb.ready, vready, sig=(j == 1 and kb == nb - 1))
            Tb.free = [t]
            b.ready = t
            if i == n - 1 or units[i + 1][0] != qb:
                finish(qb, b, sums[qb])

        if deep:
            for i in range(n + 3):
                if 0 <= i - 2 < n:
                    stage2(i - 2)
                if 0 <= i - 3 < n:
                    stage3(i - 3)
                if i < n:
                    stage1(i)
                yield
            return
        for i in range(n + 2):
            if i < n:
                stage1(i)
                yield
            if 0 <= i - 1 < n:
                stage2(i - 1)
            if 0 <= i - 2 < n:
                stage3(i - 2)
            yield

    PAIRS = [(0, 2), (1, 3), (4, 6), (5, 7)]
    U8 = [(qb, hs) for qb in range(2) for hs in PAIRS]
    U4 = [(qb, hs) for qb in range(2) for hs in ((0, 1), (2, 3))]

    def qT_of(qT):
        return lambda h, qb: qT[(h % 2) * 64:(h % 2) * 64 + 64, h // 2, qb * 128:qb * 128 + 128]

    def kT_of(kT):
        return lambda h, nk: kT[(h % 2) * 64:(h % 2) * 64 + 64, h // 2, 0:nk]

    def soft_common(biased):
        def score(qb, hs, bank, Sb, waits):
            nm = stats(2)
            tab = biased["tab"](qb, hs) if biased["tab"] else None
            c = biased["scale"]
            if tab is None:
                t = dve.do(lambda e: e.tensor_reduce(nm, bank, AXX, ALU.max, negate=True), waits[0])
                t = dve.do(lambda e: e.tensor_scalar(nm, nm, c, None, ALU.mult), t)
                return bank, [(c, nm[:, 0:1]), (c, nm[:, 1:2])], t, None
            t = dve.do(lambda e: e.scalar_tensor_tensor(Sb, bank, c, tab, ALU.mult, ALU.add),
                       *waits, biased["ready"])
            f = t
            t = dve.do(lambda e: e.tensor_reduce(nm, Sb, AXX, ALU.max, negate=True), t)
            return Sb, [(1.0, nm[:, 0:1]), (1.0, nm[:, 1:2])], t, f
        return score

    def norm_out(dst_of, nh=8, extra=None):
        toks = {}

        def finish(qb, b, sm):
            r = stats(8)
            t = act.last()
            if extra:
                t = extra(qb, sm, t)
            t = dve.do(lambda e: e.reciprocal(r[:, 0:nh], sm[:, 0:nh]), t)
            hd = 512 // nh
            o3 = b.ap.rearrange("p (h d) -> p h d", h=nh)
            d = dst_of(qb)
            d3 = d.rearrange("p (h d) -> p h d", h=nh)
            rb = bc(r[:, 0:nh].unsqueeze(2), 128, nh, hd)
            t = dve.do(lambda e: e.tensor_tensor(d3, o3, rb, ALU.mult), t, b.ready)
            give(b, t)
            toks[qb] = t
        return finish, toks

    def take(g, n):
        for _ in range(n):
            next(g)
            yield

    def skip(g, n):
        for _ in range(n):
            yield
        yield from g

    def drive(*gens):
        gens = list(gens)
        while gens:
            for g in list(gens):
                try:
                    next(g)
                except StopIteration:
                    gens.remove(g)

    AQT, AKT, BQT, BKT, AV, BV, BB, OS = 0, 1024, 1536, 2560, 3584, 3840, 4864, 8960
    o = scratch(11008)
    SQ = [Buf(av(o + 512 * i, 512)) for i in range(2)]
    QN = [Buf(av(o + 1024 + 512 * i, 512)) for i in range(2)]
    aqT, akT, bqT, bkT = av(AQT, 1024, 4), av(AKT, 512, 2), av(BQT, 1024, 4), av(BKT, 1024, 4)
    avv, bvv = av(AV, 256, 2), av(BV, 1024, 2)
    biasB = av(BB, 4096)
    osb = av(OS, 2048, 2)

    def load_x():
        for tb in range(2):
            dma(sp, xs[:, tb * 1024:tb * 1024 + 1024], A["x"][0, tb * 128:tb * 128 + 128, :], f"s_x{tb}")
        dma(sp, cst[:, 0:128], A["consts"][:, 0:128], "s_id")

    def load_consts():
        dma(sp, cst[:, 128:NCONST], A["consts"][:, 128:NCONST], "s_c")
        dma(sp, rows[:, :], bass.AP(A["rowvec"].tensor, 0, [[0, 128], [1, NROW]]), "s_c")

    def load_bias():
        for qr in range(4):
            dst = biasB[(qr % 2) * 64:(qr % 2) * 64 + 64, (qr // 2) * 2048:(qr // 2) * 2048 + 2048]
            src = A["rpb"].rearrange("q (h r) k -> q h (r k)", h=8)[:, :, (3 - qr) * 64:(7 - qr) * 64]
            dma(sp, dst.rearrange("p (h c) -> p h c", h=8), src, "s_b")

    after_dma.update({1: load_x, 3: load_consts, 6: load_bias})
    split_x(xT0, G_ATT, hT, [(S["s_t0"], 16)] + [(S["s_t1"], 16)] * 3, (S["s_g"], 16))
    invs, negs = cst[:, C_IS:C_IS + 8], cst[:, C_NS:C_NS + 8]
    skp = lgt[:, 0:8]


    pend = []

    def run_pend():
        fs = list(pend)
        pend.clear()
        for f in fs:
            f()

    cnt = [0]
    muls = []

    def run_muls():
        for f in muls:
            f()
        muls.clear()

    def run_both():
        run_pend()
        run_muls()

    def head_norm(b, tb, c0, nh, gcol, dst, rdy, dup=False, then=None):
        w = nh * 64
        i = cnt[0] % 2
        cnt[0] += 1
        sq, qn = SQ[i], QN[i]
        src = b.ap[:, c0:c0 + w]
        ss = stats(nh)
        t0 = act.do(lambda e, w=w: e.activation(sq.ap[:, 0:w], src, ACT.Square), b.ready, sq.free)
        t1 = dve.do(lambda e, w=w: e.tensor_reduce(ss, sq.ap[:, 0:w].rearrange("p (h d) -> p h d", d=64), AXX, ALU.add), t0)
        sq.free = [t1]
        sc = xsc[tb]
        t2 = pool.do(lambda e: e.tensor_scalar(ss, ss, sc["i64"], EPS, ALU.mult, ALU.add), t1, sc["t"])
        t2 = pool.do(lambda e: e.tensor_tensor(ss, ss, half[:, 0:nh], ALU.pow), t2)
        t2 = pool.do(lambda e: e.tensor_scalar(ss, ss, sc["r"], None, ALU.mult), t2)

        def scale(w=w):
            s3 = src.rearrange("p (h d) -> p h d", d=64)
            if dup:
                q4 = qn.ap[:, 0:2 * w].rearrange("p (h r d) -> p h r d", h=nh, r=2)
                for r in range(2):
                    t3 = dve.do(lambda e, r=r: e.tensor_tensor(q4[:, :, r, :], s3, bc(ss.unsqueeze(2), 128, nh, 64), ALU.mult),
                                t2, b.ready, qn.free)
                w *= 2
            else:
                q3 = qn.ap[:, 0:w].rearrange("p (h d) -> p h d", d=64)
                t3 = dve.do(lambda e: e.tensor_tensor(q3, s3, bc(ss.unsqueeze(2), 128, nh, 64), ALU.mult),
                            t2, b.ready, qn.free)
            nb = w // 128

            def later(t3=t3):
                tbk = banks.popleft()
                for j in range(nb):
                    t = pe.do(lambda e, j=j: e.transpose(tbk.ap[:, j * 128:j * 128 + 128], qn.ap[:, j * 128:j * 128 + 128], ident),
                              tbk.free, t3, s_ident, sig=j == nb - 1)
                qn.free = [t]
                d = dst[:, 0:nb, tb * 128:tb * 128 + 128]
                s = tbk.ap[:, 0:nb * 128].rearrange("p (a b) -> p a b", a=nb)
                t = act.do(lambda e: e.activation(d, s, ACT.Copy, scale=gain[:, gcol:gcol + 1]), t)
                give(tbk, t)
                rdy.append(t)
            pend.append(later)
            if then:
                t3 = then(t3)
            give(b, t3)
        muls.append(scale)

    def plain_evac(b, c0, w, d, which, sc, *waits):
        s = b.ap[:, c0:c0 + w]
        if which:
            return act.do(lambda e: e.activation(d, s, ACT.Copy, scale=sc["r"]), b.ready, sc["t"], *waits)
        return dve.do(lambda e: e.tensor_scalar(d, s, sc["r"], None, ALU.mult), b.ready, sc["t"], *waits)

    W = "w_in_e"

    rA, rB, rVA, rVB = [], [], [], []

    def g_heads(c0, gc, dst, rdy):
        bk = yield from gemm_ng(W, c0, 512, mid=run_both)
        run_pend()
        for tb in range(2):
            head_norm(bk[tb], tb, 0, 8, gc, dst, rdy)

    xsc = []
    bk = gemm_n(W, 0, 512, mid=lambda: xsc.extend(row_scales(x3, osb, [(S["s_x0"], 16)] * 2 + [(S["s_x1"], 16)] * 2)))
    for tb in range(2):
        head_norm(bk[tb], tb, 0, 8, G_QA, aqT, rA)
    bk = gemm_n(W, 512, 256, mid=run_muls)

    def ev(b, tb):
        def f(t):
            t = plain_evac(b, 128, 128, avv[:, tb, :], 0, xsc[tb], t)
            rVA.append(t)
            return t
        return f

    for tb in range(2):
        head_norm(bk[tb], tb, 0, 2, G_KA, akT, rA, dup=True, then=ev(bk[tb], tb))
    finish_gen(g_heads(768, G_QB, bqT, rB))
    t_skp = pool.do(lambda e: e.tensor_tensor(skp, rows[:, R_SINK:R_SINK + 8], invs, ALU.mult), s_const)

    def rest_b():
        yield from g_heads(1280, G_KB, bkT, rB)
        bk = yield from gemm_ng(W, 1792, 512, mid=run_muls)
        run_pend()
        for tb in range(2):
            t = plain_evac(bk[tb], 0, 512, bvv[:, tb, :], tb, xsc[tb])
            rVB.append(t)
            give(bk[tb], t)

    slope = [2.0 ** -(h + 1) for h in range(8)]
    negabs = v3(cst, 2, C_NA, 512)
    nmA = [stats(8), stats(8)]

    def scoreA(qb, hs, bank, Sb, waits):
        mx = stats(2)
        for j, h in enumerate(hs):
            t = dve.do(lambda e, j=j, h=h: e.scalar_tensor_tensor(
                Sb[:, j, :], bank[:, j, :], 0.125 / slope[h], negabs[:, qb, :], ALU.mult, ALU.add), *waits, s_const)
        f = t
        t = dve.do(lambda e: e.tensor_reduce(mx, Sb, AXX, ALU.max), t)
        hsl = slice(hs[0], hs[1] + 1, hs[1] - hs[0])
        nm = nmA[qb][:, hsl]
        t = dve.do(lambda e: e.tensor_tensor(mx, mx, skp[:, hsl], ALU.max), t, t_skp)
        t = dve.do(lambda e: e.tensor_tensor(nm, mx, negs[:, hsl], ALU.mult), t)
        return Sb, [(slope[h], nmA[qb][:, h:h + 1]) for h in hs], t, f

    def extraA(qb, sm, t):
        es = stats(8)
        t1 = dve.do(lambda e: e.tensor_tensor(es, rows[:, R_SINK:R_SINK + 8], nmA[qb], ALU.add), t)
        t1 = act.do(lambda e: e.activation(es, es, ACT.Exp), t1)
        return dve.do(lambda e: e.tensor_tensor(sm, sm, es, ALU.add), t1, t)

    finA, tokA = norm_out(lambda qb: osb[:, qb, 0:512], extra=extraA)
    finB, tokB = norm_out(lambda qb: osb[:, qb, 512:1024])
    bias5 = biasB.rearrange("p (q h k) -> p q h k", q=2, h=8)
    kAT = lambda h, nk: akT[(h % 2) * 64:(h % 2) * 64 + 64, h // 4, 0:nk]
    drive(skip(attention(U8, [256, 256], qT_of(aqT), kAT, lambda h, kb: avv[:, kb, (h // 4) * 64:(h // 4) * 64 + 64],
                    scoreA, 64, rVA, finA, rA, deep=True), 1), rest_b())
    cfgB = dict(scale=0.125, tab=lambda qb, hs: bias5[:, qb, hs[0]:hs[1] + 1:hs[1] - hs[0], :], ready=(S["s_b"], 64))

    def out_half(acc, name, src, g, ready):
        u = ur[urn[0] % 2]
        urn[0] += 1
        to_T(src, u, list(range(4 * g, 4 * g + 4)), 0, None, ready)
        yield
        for j in range(2):
            acc.extend([] if acc else acc_open())
            yield from gemm_accg(acc, name, (4 * g + 2 * j) * 128, u, 2 * j, g == 0 and j == 0, g == 1 and j == 1)

    acc = []
    o0 = out_half(acc, "w_out_e", osb, 0, list(tokA.values()))
    drive(attention(U8, [256, 256], qT_of(bqT), kT_of(bkT), lambda h, kb: bvv[:, kb, h * 64:h * 64 + 64],
                    soft_common(cfgB), 64, rVB, finB, rB, deep=True),
          skip(take(o0, 3), 1))
    for _ in range(1):
        next(o0)
    next(o0)
    o1 = out_half(acc, "w_out_e", osb, 1, list(tokB.values()))
    next(o1)
    drive(o0)
    drive(o1)
    xr = acc_close(acc)

    def mlp(layer, gcol, xr, during=None):
        boundary()
        hn = av(0, 2048, 2)
        RL = [Buf(av(2048 + 512 * i, 512)) for i in range(2)]
        SQ2 = [Buf(av(3072 + 512 * i, 512)) for i in range(2)]
        to_T(x3, hT, list(range(8)), 0, gcol, xr, by_half=True)
        inv = [(c["i"], c["ti"]) for c in row_scales(x3, hn, xr)]
        acc = acc_open()
        w1, w2 = f"w1_{layer}", f"w2_{layer}"
        slots = []
        for j in range(17):
            if j < 16:
                b, = gemm_t(w1, j * 256, 256)
                rl, sq = RL[j % 2], SQ2[j % 2]
                u, off = ur[(j // 2) % 2], 2 * (j % 2)
                t = act.do(lambda e, b=b, rl=rl: e.activation(rl.ap, b.ap, ACT.Relu), b.ready, rl.free)
                give(b, t)
                t = dve.do(lambda e, rl=rl, sq=sq: e.tensor_tensor(sq.ap, rl.ap, rl.ap, ALU.mult), t, sq.free)
                rl.free = [t]
                s3 = sq.ap.rearrange("p (a b) -> p a b", a=2)
                dh, dl = u.ap[0][:, off:off + 2, :], u.ap[1][:, off:off + 2, :]
                th = act.do(lambda e, dh=dh, s3=s3: e.activation(dh, s3, ACT.Copy), t, u.free)
                t = dve.do(lambda e, dl=dl, dh=dh, s3=s3: e.tensor_tensor(dl, s3, dh.bitcast(F32), ALU.subtract), th, u.free)
                sq.free = [t]
                if not isinstance(u.ready, dict):
                    u.ready = {}
                u.ready[off] = u.ready[off + 1] = t
                slots.append((u, off))
            if j >= 1:
                u, off = slots[j - 1]
                gemm_acc(acc, w2, (j - 1) * 256, u, off, j == 1, j == 16)
            if during:
                during(j)
        return acc_close(acc, inv)

    DT = 15104
    dtab = av(DT, 3072, 8)

    td = []

    def decays(j):
        if 12 <= j < 16:
            dd = dtab[:, 2 * (j - 12):2 * (j - 12) + 2, :]
            td.append(act.do(lambda e: e.activation(dd, dd, ACT.Exp), td[0]))
        if j != 1:
            return
        d = rows[:, R_DF:R_DF + 16]
        a = [lgt[:, 16 * i:16 * i + 16] for i in range(1, 8)]
        ad, e_, s_, s2, pl, lo, t1 = a
        p = pool
        t = p.do(lambda e: e.tensor_scalar(ad, d, -1.0, None, ALU.mult), s_const)
        t = dve.do(lambda e: e.tensor_tensor(ad, ad, d, ALU.min), t)
        t = act.do(lambda e: e.activation(e_, ad, ACT.Exp), t)
        t = p.do(lambda e: e.tensor_scalar(t1, e_, 2.0, None, ALU.add), t)
        t = dve.do(lambda e: e.reciprocal(t1, t1), t)
        t = p.do(lambda e: e.tensor_tensor(s_, e_, t1, ALU.mult), t)
        t = p.do(lambda e: e.tensor_tensor(s2, s_, s_, ALU.mult), t)
        t = p.do(lambda e: e.tensor_scalar(pl, s2, 1.0 / 19, 1.0 / 17, ALU.mult, ALU.add), t)
        for n in (15, 13, 11, 9, 7, 5, 3, 1):
            t = p.do(lambda e: e.tensor_tensor(pl, pl, s2, ALU.mult), t)
            t = p.do(lambda e, n=n: e.tensor_scalar(pl, pl, 1.0 / n, None, ALU.add), t)
        t = p.do(lambda e: e.tensor_tensor(pl, pl, s_, ALU.mult), t)
        t = p.do(lambda e: e.tensor_scalar(pl, pl, 2.0, None, ALU.mult), t)
        t = p.do(lambda e: e.tensor_scalar(lo, d, 0.0, None, ALU.min), t)
        t = p.do(lambda e: e.tensor_tensor(lo, lo, pl, ALU.subtract), t)
        uu, ll = cst[:, C_U:C_U + 384], cst[:, C_L:C_L + 384]
        tmp = av(4096, 3072, 8)
        for h in range(8):
            p.do(lambda e, h=h: e.tensor_scalar(dtab[:, h, :], uu, lo[:, h:h + 1], None, ALU.mult), t)
            t2 = p.do(lambda e, h=h: e.tensor_scalar(tmp[:, h, :], ll, lo[:, 8 + h:9 + h], None, ALU.mult), t)
        t2 = p.do(lambda e: e.tensor_tensor(dtab, dtab, tmp, ALU.add), t2)
        td.append(t2)

    xr = mlp(0, G_MLP0, xr, decays)
    t_dtab = td[-1]

    boundary()
    OQ, OK_, OV, OY, OX = 0, 2048, 4096, 8192, 12288
    oqT, okT = av(OQ, 2048, 8), av(OK_, 2048, 8)
    ov, oy = av(OV, 4096, 2), av(OY, 4096, 2)
    ATs = [Buf(av(OX + 512 * i, 512, 2)) for i in range(2)]
    GT = [Buf(av(OX + 1024 + 512 * i, 512)) for i in range(2)]
    to_T(x3, hT, list(range(8)), 0, G_RET, xr, by_half=True)
    xsc = row_scales(x3, av(OY, 2048, 2), xr)
    t_ones = pool.do(lambda e: e.memset(ones, 1.0))
    bcast = row_broadcast(xsc)
    W = "w_in_o"
    qtok = []
    for base, dst in ((0, oqT), (1024, okT)):
        for c in range(0, 4, 2):
            bks = gemm_t(W, base + c * 256, 256) + gemm_t(W, base + c * 256 + 256, 256)
            if not qtok:
                t_rb = bcast()
            for i, b in enumerate(bks):
                d = dst[:, 2 * (c + i):2 * (c + i) + 2, :]
                s = b.ap.rearrange("p (a b) -> p a b", a=2)
                t = dve.do(lambda e, d=d, s=s: e.tensor_tensor(d, s, bc(rbc.unsqueeze(1), 128, 2, 256), ALU.mult), b.ready, t_rb)
                give(b, t)
                qtok.append(t)
    vtok = []

    def g_v(c):
        bk = yield from gemm_ng(W, 2048 + 512 * c, 512)
        ts = []
        for tb in range(2):
            ts.append(plain_evac(bk[tb], 0, 512, ov[:, tb, 512 * c:512 * c + 512], tb, xsc[tb]))
            give(bk[tb], ts[tb])
        vtok.append(ts)

    ytok = {}

    def retention():
        kscale = float(128 ** -0.5)

        def sc(h):
            b = banks.popleft()
            for jb in range(2):
                o = b.ap[:, jb * 256:jb * 256 + 256]
                t = pe.do(lambda e, o=o, jb=jb, h=h: e.matmul(o, okT[:, h, jb * 128:jb * 128 + 128], oqT[:, h, :],
                                                             start=True, stop=True), b.free, qtok, sig=jb == 1)
            a = ATs[h % 2]
            for jb in range(2):
                dd = dtab[:, h, 128 - jb * 128:128 - jb * 128 + 256]
                t2 = dve.do(lambda e, jb=jb, a=a, b=b, dd=dd: e.scalar_tensor_tensor(
                    a.ap[:, jb, :], b.ap[:, jb * 256:jb * 256 + 256], kscale, dd, ALU.mult, ALU.mult), t, a.free, t_dtab)
            a.ready = t2
            give(b, t2)

        def pv(h):
            a = ATs[h % 2]
            b = banks.popleft()
            for ib in range(2):
                for jb in range(2):
                    o = b.ap[:, ib * 256:ib * 256 + 256]
                    t = pe.do(lambda e, o=o, ib=ib, jb=jb, h=h, a=a: e.matmul(
                        o, a.ap[:, jb, ib * 128:ib * 128 + 128], ov[:, jb, h * 256:h * 256 + 256],
                        start=jb == 0, stop=jb == 1), b.free, a.ready, vtok[h // 2], sig=(ib == 1 and jb == 1))
            a.free = [t]
            st6, mv = stats(12), stats(4)
            for ib in range(2):
                t1 = dve.do(lambda e, ib=ib, st6=st6, b=b: e.bn_stats(st6[:, ib * 6:ib * 6 + 6], b.ap[:, ib * 256:ib * 256 + 256]), t)
            for ib in range(2):
                t1 = dve.do(lambda e, ib=ib, st6=st6, mv=mv: e.bn_aggr(mv[:, 2 * ib:2 * ib + 2], st6[:, ib * 6:ib * 6 + 6]), t1)
            t1 = rstd(mv[:, 1:4:2], 2, 1.0, GN_EPS, t1)
            for ib in range(2):
                t1 = dve.do(lambda e, ib=ib, mv=mv, b=b, h=h: e.tensor_scalar(
                    oy[:, ib, h * 256:h * 256 + 256], b.ap[:, ib * 256:ib * 256 + 256],
                    mv[:, 2 * ib:2 * ib + 1], mv[:, 2 * ib + 1:2 * ib + 2], ALU.subtract, ALU.mult), t1)
            give(b, t1)
            ytok[h] = t1

        for h in range(9):
            if h < 8:
                sc(h)
            if h >= 1:
                pv(h - 1)
            yield

    gen = retention()
    for c in range(4):
        for i, _ in enumerate(g_v(c)):
            if c and i % 2 == 0:
                next(gen)
    acc = []
    utok = {}

    def u_T(k):
        to_T(oy, ur[k % 2], list(range(4 * k, 4 * k + 4)), 0, G_GN, [utok[(k, 0)], utok[(k, 1)]])

    def u_acc(k, j):
        acc.extend([] if acc else acc_open())
        gemm_acc(acc, "w_out_o", (4 * k + 2 * j) * 128, ur[k % 2], 2 * j, k == 0 and j == 0, k == 3 and j == 1)

    for c in range(4):
        bk = gemm_n(W, 4096 + 512 * c, 512, mid=(lambda: u_T(c - 1)) if c else None)
        for tb in range(2):
            g, b, sc = GT[tb], bk[tb], xsc[tb]
            t = act.do(lambda e, g=g, b=b, sc=sc: e.activation(g.ap, b.ap, ACT.Tanh, scale=sc["h"]), b.ready, g.free, sc["t"])
            t = dve.do(lambda e, g=g, b=b: e.scalar_tensor_tensor(g.ap, g.ap, 1.0, b.ap, ALU.add, ALU.mult), t)
            give(b, t)
            y = oy[:, tb, 512 * c:512 * c + 512]
            t = dve.do(lambda e, g=g, y=y, sc=sc: e.scalar_tensor_tensor(y, g.ap, sc["h"], y, ALU.mult, ALU.mult), t,
                       ytok[2 * c], ytok[2 * c + 1])
            g.free = [t]
            utok[(c, tb)] = t
        for _ in range(2):
            next(gen, None)
        if c:
            u_acc(c - 1, 0)
            if c == 3:
                u_T(3)
            u_acc(c - 1, 1)
    u_acc(3, 0)
    u_acc(3, 1)
    for _ in gen:
        pass
    xr = acc_close(acc)

    MQ, MK, MV, DQ, DK, DV, XQ, XK, XV, SG, DM, IQ, UU, TT = (
        0, 1024, 2048, 3072, 4096, 5120, 6144, 7168, 8192, 9216, 12288, 3072, 0, 2048)
    MT, MR, MJ = 6144, 9216, 13184
    memT, memr = av(MT, 2048, 8), av(MR, 2048, 2)
    msc = []

    class Halves:

        def __init__(self, i):
            self.i = i

        def __getitem__(self, key):
            return ur[key[1] // 4].ap[self.i][:, key[1] % 4, key[2]]

    mT = Buf((Halves(0), Halves(1)))
    mT.ready = {}

    def split_mem(half_):
        u = ur[half_]
        for k in range(4 * half_, 4 * half_ + 4):
            g = gain[:, G_MEM + k:G_MEM + k + 1]
            dh, dl = u.ap[0][:, k % 4, :], u.ap[1][:, k % 4, :]
            t = act.do(lambda e, k=k, dh=dh, g=g: e.activation(dh, memT[:, k, :], ACT.Copy, scale=g), (S["s_m"], 32), u.free)
            mT.ready[k] = dve.do(lambda e, k=k, dh=dh, dl=dl, g=g: e.scalar_tensor_tensor(
                dl, memT[:, k, :], g, dh.bitcast(F32), ALU.mult, ALU.subtract), t, u.free)

    mrb = []

    def mem_rows(j):
        if j == 1:
            w = [q.last() for q in (act, dve, pe, pool)]
            dma(sp, memT, A["memT"].rearrange("(t p) n -> p t n", p=128), "s_m", *w)
            dma(sp, memr, A["mem"].rearrange("a (t p) n -> p (a t) n", p=128), "s_m", *w)
        if j == 5:
            msc.extend(row_scales(memr, av(MJ, 2048, 2), [(S["s_m"], 32)] * 4))
        if j == 8:
            mrb.append(row_broadcast(msc, *(q.last() for q in (act, dve, pe))))
        if j == 11:
            mrb.append(mrb[0]())
        if j == 15:
            split_mem(0)

    xr = mlp(1, G_MLP1, xr, mem_rows)

    boundary()
    dqT, dkT, dv = av(DQ, 1024, 4), av(DK, 1024, 4), av(DV, 1024, 2)
    mqT, mkT, mvv = av(MQ, 1024, 4), av(MK, 1024, 4), av(MV, 1024, 2)
    iqT, ikT = av(IQ, 1024, 4), av(IQ + 1024, 256)
    xqT, xkT, xv = av(XQ, 1024, 4), av(XK, 1024, 4), av(XV, 1024, 2)
    sg = [av(SG + 1024 * i, 1024, 2) for i in range(3)]
    msk = av(DM, 512, 2)
    o = scratch(12800)
    R1 = [Buf(av(o + 512 * i, 512)) for i in range(2)]
    R2 = [Buf(av(o + 1024 + 512 * i, 512)) for i in range(2)]
    o += 2048
    iwt, ikraw = av(o, 16, 2), av(o + 16, 256)[0:72, :]
    RS = [[Buf(av(o + 272 + 256 * i + 128 * j, 128)) for j in range(2)] for i in range(2)]
    hnx = av(SG, 2048, 2)
    split_mem(1)
    t_rb = mrb[1]
    for c in range(2):
        b, = gemm_t("w_mem", c * 256, 256, xT=mT)
        t = dve.do(lambda e, b=b, c=c: e.tensor_tensor(xkT[:, 2 * c:2 * c + 2, :], b.ap.rearrange("p (a b) -> p a b", a=2),
                                                      bc(rbc.unsqueeze(1), 128, 2, 256), ALU.mult), b.ready, t_rb, mT.ready[7])
        give(b, t)
    rX, rVX = [t], []
    t_rbfree = t
    to_T(x3, hT, list(range(8)), 0, G_IN, xr, by_half=True)
    xsc = row_scales(x3, hnx, xr)
    bk = gemm_n("w_mem", 512, 512, xT=mT)
    for tb in range(2):
        t = plain_evac(bk[tb], 0, 512, xv[:, tb, :], tb, msc[tb], mT.ready[7])
        give(bk[tb], t)
        rVX.append(t)
    for u in ur:
        u.free = [bk[1].ready]
        u.ready = None

    cos, sin = v3(cst, 2, C_COS, 128), v3(cst, 2, C_SIN, 128)
    rc = [0]

    def rope(b, tb, c0, nh, dst, rdy, dup=False):
        if dup:
            r1, r2 = RS[tb]
        else:
            r1, r2 = R1[rc[0] % 2], R2[rc[0] % 2]
            rc[0] += 1
        w = nh * 64
        src = b.ap[:, c0:c0 + w].rearrange("p (h d) -> p h d", d=64)
        a = r1.ap[:, 0:w].rearrange("p (h d) -> p h d", d=64)
        c = r2.ap[:, 0:w].rearrange("p (h d) -> p h d", d=64)
        ct, s_t = cos[:, tb, :], sin[:, tb, :]
        sc = xsc[tb]
        t1 = dve.do(lambda e: e.scalar_tensor_tensor(a, src, sc["r"], bc(ct.unsqueeze(1), 128, nh, 64), ALU.mult, ALU.mult),
                    b.ready, r1.free, sc["t"])
        for q in range(2):
            t2 = dve.do(lambda e, q=q: e.scalar_tensor_tensor(
                c[:, :, q * 32:q * 32 + 32], src[:, :, 32 - q * 32:64 - q * 32], sc["r"],
                bc(s_t[:, q * 32:q * 32 + 32].unsqueeze(1), 128, nh, 32), ALU.mult, ALU.mult),
                        b.ready, r2.free)
        if dup:
            pool.do(lambda e: e.tensor_tensor(r2.ap[:, 64:128], r1.ap[:, 0:64], r2.ap[:, 0:64], ALU.add), t1, t2)
            t3 = pool.do(lambda e: e.tensor_tensor(r1.ap[:, 0:64], r1.ap[:, 0:64], r2.ap[:, 0:64], ALU.add), t1, t2)
            t3 = pool.do(lambda e: e.tensor_copy(r1.ap[:, 64:128], r2.ap[:, 64:128]), t3)
            w = 128
        else:
            t3 = pool.do(lambda e: e.tensor_tensor(r1.ap[:, 0:w], r1.ap[:, 0:w], r2.ap[:, 0:w], ALU.add), t1, t2)
        r2.free = [t3]
        nb = w // 128

        def later():
            tbk = banks.popleft()
            for j in range(nb):
                t = pe.do(lambda e, j=j: e.transpose(tbk.ap[:, j * 128:j * 128 + 128], r1.ap[:, j * 128:j * 128 + 128], ident),
                          tbk.free, t3, s_ident, sig=j == nb - 1)
            r1.free = [t]
            d = dst[:, 0:nb, tb * 128:tb * 128 + 128]
            s = tbk.ap[:, 0:nb * 128].rearrange("p (a b) -> p a b", a=nb)
            t = act.do(lambda e: e.activation(d, s, ACT.Copy), t)
            give(tbk, t)
            rdy.append(t)
        pend.append(later)
        return t2

    W = "w_in_2"

    def g_rope(c0, dst, rdy):
        bk = yield from gemm_ng(W, c0, 512)
        run_pend()
        for tb in range(2):
            give(bk[tb], rope(bk[tb], tb, 0, 8, dst, rdy))

    def g_plain(c0, dst, rdy):
        bk = yield from gemm_ng(W, c0, 512)
        run_pend()
        for tb in range(2):
            t = plain_evac(bk[tb], 0, 512, dst[:, tb, :], tb, xsc[tb])
            give(bk[tb], t)
            rdy.append(t)

    tsg = {}

    def g_silu(c0, i):
        bk = yield from gemm_ng(W, c0, 512)
        run_pend()
        for tb in range(2):
            b, d, sc = bk[tb], sg[i][:, tb, :], xsc[tb]
            t = act.do(lambda e, b=b, d=d, sc=sc: e.activation(d, b.ap, ACT.Tanh, scale=sc["h"]), b.ready, sc["t"])
            t = dve.do(lambda e, b=b, d=d: e.scalar_tensor_tensor(d, d, 1.0, b.ap, ALU.add, ALU.mult), t)
            give(b, t)
            t = dve.do(lambda e, d=d, sc=sc: e.tensor_scalar(d, d, sc["h"], None, ALU.mult), t)
        tsg[i] = t

    rI, rM, rD, rVM, rVD = [], [], [], [], []
    bcast = row_broadcast(xsc, t_rbfree)
    finish_gen(g_rope(4096, iqT, rI))
    ikw = {}

    def g_ik():
        b = banks.popleft()
        for x in range(2):
            w = next_half(W, 0, 8, 4608, 72, "k")
            for k in range(4):
                kk = 4 * x + k
                xh, xl = hT.ap[0][:, kk, :], hT.ap[1][:, kk, :]
                wh, wl = w["h"][:, k, :], w["l"][:, k, :]
                t = mm3(b.ap[0:72, 0:256], [(wh, xh), (wh, xl), (wl, xh)], kk == 0, kk == 7,
                        b.free, hT.part(kk), w["hi"], w["lo"], sig=k == 3)
            half_done(t)
        t = act.do(lambda e: e.activation(ikraw, b.ap[0:72, 0:256], ACT.Copy), t)
        give(b, t)

        def back():
            b = banks.popleft()
            for tb in range(2):
                tp = pe.do(lambda e, tb=tb, b=b: e.transpose(b.ap[:, tb * 72:tb * 72 + 72], ikraw[:, tb * 128:tb * 128 + 128],
                                                             ident[0:72, 0:72]), b.free, t, s_ident, sig=tb == 1)
            b.ready = tp
            for tb in range(2):
                rope(b, tb, tb * 72, 1, ikT.rearrange("p (a b) -> p a b", a=1), rI, dup=True)
                t2 = dve.do(lambda e, tb=tb, b=b: e.tensor_scalar(
                    iwt[:, tb, :], b.ap[:, tb * 72 + 64:tb * 72 + 72], xsc[tb]["r"], float(8 ** -0.5) * 0.125,
                    ALU.mult, ALU.mult), tp)
            give(b, t2)
            ikw["t"] = t2
        pend.append(back)

    g_ik()
    caus = cst[:, C_CA:C_CA + 256]
    mtok = {}

    def index():
        for qb in range(2):
            nk = 128 + 128 * qb
            m = msk[:, qb, 0:nk]
            ca = caus[:, 256 - nk:256]
            t = dve.do(lambda e, m=m, ca=ca: e.tensor_copy(m, ca), s_const)
            for i, hs in enumerate(PAIRS):
                b = banks.popleft()
                for j, h in enumerate(hs):
                    o = b.ap[:, j * 256:j * 256 + nk]
                    hf = (h % 2) * 64
                    tp = pe.do(lambda e, o=o, h=h, hf=hf, qb=qb, nk=nk: e.matmul(
                        o, iqT[hf:hf + 64, h // 2, qb * 128:qb * 128 + 128], ikT[hf:hf + 64, 0:nk],
                        start=True, stop=True), b.free, rI, sig=j == 1)
                Sb = scr["S"][i % 2]
                s = Sb.ap[:, :, 0:nk]
                bb = b.ap.rearrange("p (a b) -> p a b", a=2)[:, :, 0:nk]
                tr = act.do(lambda e, s=s, bb=bb: e.activation(s, bb, ACT.Relu), tp, Sb.free)
                give(b, tr)
                for j, h in enumerate(hs):
                    t = dve.do(lambda e, s=s, j=j, h=h, m=m, qb=qb: e.scalar_tensor_tensor(
                        m, s[:, j, :], iwt[:, qb, h:h + 1], m, ALU.mult, ALU.add), tr, t, ikw["t"])
                Sb.free = [t]
                if i % 2:
                    yield
            mtok[qb] = t
        ms = [(qb, msk[:, qb, 0:128 + 128 * qb], stats(8)) for qb in range(2)]
        for r in range(8):
            for qb, m, m8 in ms:
                mtok[qb] = dve.do(lambda e, m=m, m8=m8: e.max(m8, m), mtok[qb])
            yield
            for qb, m, m8 in ms:
                mtok[qb] = dve.do(lambda e, m=m, m8=m8: e.match_replace(m, m8, m, MARK), mtok[qb])
            yield
        for qb, m, m8 in ms:
            ca = caus[:, 128 - 128 * qb:256]
            t = dve.do(lambda e, m=m: e.tensor_scalar(m, m, -3.2e38, NEG, ALU.is_gt, ALU.mult), mtok[qb])
            mtok[qb] = dve.do(lambda e, m=m, ca=ca: e.tensor_tensor(m, m, ca, ALU.add), t)

    ix = index()

    def mlist(*fs):
        for f in fs:
            g = f()
            if g is not None:
                yield from g

    def scales():
        rb["t"] = bcast()

    rb = {}
    drive(mlist(lambda: g_rope(0, mqT, rM), scales, lambda: g_rope(512, mkT, rM), lambda: g_plain(1024, mvv, rVM),
                lambda: g_silu(1536, 0)), skip(take(ix, 4), 9))
    t_rb = rb["t"]

    def f_xq():
        for c in range(2):
            b, = yield from gemm_tg(W, 4680 + c * 256, 256)
            t = dve.do(lambda e, b=b, c=c: e.tensor_tensor(
                xqT[:, 2 * c:2 * c + 2, :], b.ap.rearrange("p (a b) -> p a b", a=2),
                bc(rbc.unsqueeze(1), 128, 2, 256), ALU.mult), b.ready, t_rb)
            give(b, t)
            rX.append(t)

    def gated_out(i):
        toks = {}
        def finish(qb, b, sm):
            nh = 4 if i == 2 else 8
            r = stats(8)
            t = dve.do(lambda e: e.reciprocal(r[:, 0:nh], sm[:, 0:nh]), act.last())
            d = sg[i][:, qb, :]
            hd = 512 // nh
            t1 = dve.do(lambda e: e.tensor_tensor(d, b.ap, d, ALU.mult), b.ready, tsg[i])
            give(b, t1)
            d3 = d.rearrange("p (h d) -> p h d", h=nh)
            toks[qb] = dve.do(lambda e: e.tensor_tensor(d3, d3, bc(r[:, 0:nh].unsqueeze(2), 128, nh, hd), ALU.mult), t, t1)
        return finish, toks

    uT, tT = av(UU, 2048, 8), av(TT, 1024, 4)
    hb = lgt[:, 8:32]
    t_hb = pool.do(lambda e: e.tensor_scalar(hb, gain[:, G_BM:G_BM + 24], 0.5, None, ALU.mult), s_const)
    state_u = dict(tfree=[])

    names = {0: "w_up_moba", 1: "w_up_dsa", 2: "w_up_cross"}
    finM, tokM = gated_out(0)
    finX, tokX = gated_out(2)
    cfgM = dict(scale=0.125, ready=s_const,
                tab=lambda qb, hs: bc(caus[:, 128 - 128 * qb:256].unsqueeze(1), 128, 2, 128 + 128 * qb))
    cfgX = dict(scale=float(128 ** -0.5), ready=None, tab=None)

    def merge(i, toks, first):
        u = ur[urn[0] % 2]
        urn[0] += 1
        state_u["now"] = []
        for g in range(2):
            for c in range(2):
                b, = yield from gemm_tg(W, 5704 + 1024 * i + 512 * g + 256 * c, 256)
                d = tT[:, 2 * c:2 * c + 2, :]
                t = dve.do(lambda e, b=b, d=d: e.tensor_tensor(
                    d, b.ap.rearrange("p (a b) -> p a b", a=2), bc(rbc.unsqueeze(1), 128, 2, 256), ALU.mult),
                    b.ready, t_rb, state_u["tfree"])
                give(b, t)
                for m in range(2):
                    k = 4 * g + 2 * c + m
                    d = tT[:, 2 * c + m, :]
                    tt_ = act.do(lambda e, d=d, k=k: e.activation(
                        d, d, ACT.Tanh, bias=hb[:, 8 * i + k:8 * i + k + 1], scale=0.5), t, t_hb)
                if g == 0 and c == 0:
                    to_T(sg[i], u, [0, 1, 2, 3], 0, None, [toks[0], toks[1]])
            bks = yield from gemm_tg(names[i], 512 * g, 512, nk=4, xT=u)
            for n, b in enumerate(bks):
                tt = tT[:, 2 * n:2 * n + 2, :]
                dd = uT[:, 4 * g + 2 * n:4 * g + 2 * n + 2, :]
                b3 = b.ap.rearrange("p (a b) -> p a b", a=2)
                dst = dd if first else tt
                t1 = dve.do(lambda e, tt=tt, b3=b3, dst=dst: e.scalar_tensor_tensor(dst, tt, 1.0, b3, ALU.add, ALU.mult),
                            b.ready, tt_)
                give(b, t1)
                if not first:
                    t1 = dve.do(lambda e, dd=dd, tt=tt: e.tensor_tensor(dd, dd, tt, ALU.add), t1)
            state_u["tfree"] = [t1]
            state_u[g] = t1
            state_u["now"] = state_u["now"] + [g]
            if g == 1:
                u.free = [bks[-1].ready]

    def all_of(*gs):
        for g in gs:
            yield from g

    drive(attention(U8, [128, 256], qT_of(mqT), kT_of(mkT), lambda h, kb: mvv[:, kb, h * 64:h * 64 + 64],
                    soft_common(cfgM), 64, rVM, finM, rM, deep=True),
          mlist(lambda: g_rope(2048, dqT, rD), lambda: g_rope(2560, dkT, rD), lambda: g_plain(3072, dv, rVD),
                lambda: g_silu(3584, 1)), ix)
    cfgD = dict(scale=0.125, ready=[mtok[0], mtok[1]],
                tab=lambda qb, hs: bc(msk[:, qb, 0:128 + 128 * qb].unsqueeze(1), 128, 2, 128 + 128 * qb))
    finD, tokD = gated_out(1)
    for q in (act, dve, pe, pool):
        q.wait(tokM[0], tokM[1])
    drive(attention(U8, [128, 256], qT_of(dqT), kT_of(dkT), lambda h, kb: dv[:, kb, h * 64:h * 64 + 64],
                    soft_common(cfgD), 64, rVD, finD, rD, deep=True),
          all_of(mlist(f_xq), merge(0, tokM, True)))
    drive(attention(U4, [256, 256], lambda h, qb: xqT[:, h, qb * 128:qb * 128 + 128], lambda h, nk: xkT[:, h, 0:nk],
                    lambda h, kb: xv[:, kb, h * 128:h * 128 + 128], soft_common(cfgX), 128, rVX, finX, rX),
          all_of(mlist(lambda: g_silu(5192, 2)), merge(1, tokD, False)))

    def split_u(g):
        u = ur[urn[0] % 2]
        urn[0] += 1
        u.ready = {}
        for i in range(2):
            src = uT[:, 4 * g + 2 * i:4 * g + 2 * i + 2, :]
            dh, dl = u.ap[0][:, 2 * i:2 * i + 2, :], u.ap[1][:, 2 * i:2 * i + 2, :]
            t = act.do(lambda e, dh=dh, src=src: e.activation(dh, src, ACT.Copy, scale=0.5), state_u[g], u.free)
            u.ready[2 * i] = u.ready[2 * i + 1] = dve.do(lambda e, dh=dh, dl=dl, src=src: e.scalar_tensor_tensor(
                dl, src, 0.5, dh.bitcast(F32), ALU.mult, ALU.subtract), t, u.free)
        return u

    mg = merge(2, tokX, False)
    next(mg)
    while 0 not in state_u["now"]:
        next(mg)
    u0 = split_u(0)
    drive(mg)
    u1 = split_u(1)
    acc = acc_open()
    t_attn = pe.last()
    for g, u in ((0, u0), (1, u1)):
        for j in range(2):
            gemm_acc(acc, "w_out_2", (4 * g + 2 * j) * 128, u, 2 * j, g == 0 and j == 0, g == 1 and j == 1)
    xr = acc_close(acc)
    fin = av(3072, 2048, 2)
    rs = []
    for tb in range(2):
        ss = stats(1)
        f, x = fin[:, tb, :], x3[:, tb, :]
        t = act.do(lambda e, f=f, x=x, ss=ss: e.activation(f, x, ACT.Square, accum_out=ss), xr[2 * tb + 1], t_attn)
        rs.append((ss, rstd(ss, 1, 1.0 / 1024, EPS, t)))
    for tb in range(2):
        ss, t = rs[tb]
        f, x = fin[:, tb, :], x3[:, tb, :]
        for i in range(2):
            c = slice(512 * i, 512 * i + 512)
            t1 = dve.do(lambda e, f=f, x=x, ss=ss, c=c: e.scalar_tensor_tensor(
                f[:, c], x[:, c], ss, rows[:, R_FIN + c.start:R_FIN + c.stop], ALU.mult, ALU.mult), t)
            dma((sp, act)[i], out[0, tb * 128:tb * 128 + 128, c], f[:, c], "s_out", t1)
    sp.wait((S["s_out"], dma_n["s_out"]))
    return used, dict(sp=sp, act=act, dve=dve, pe=pe, pool=pool)


def shape_constants():
    import numpy as np
    c = np.zeros((128, NCONST), np.float32)
    p = np.arange(128)
    c[:, C_ID:C_ID + 128] = np.eye(128)
    for qb in range(2):
        rel = np.abs(np.arange(256)[None, :] - (p[:, None] + 128 * qb))
        c[:, C_NA + 256 * qb:C_NA + 256 * qb + 256] = np.where(rel <= 128, -rel, NEG)
    c[:, C_CA + 128:C_CA + 256] = np.where(p[None, :] <= p[:, None], 0.0, LOW)
    inv = np.power(np.float32(10000.0), -np.arange(32, dtype=np.float32) * np.float32(2.0) / np.float32(64)).astype(np.float32)
    for tb in range(2):
        ang = ((p + 128 * tb).astype(np.float32)[:, None] * inv[None, :]).astype(np.float32).astype(np.float64)
        co, si = np.cos(ang), np.sin(ang)
        c[:, C_COS + 64 * tb:C_COS + 64 * tb + 64] = np.concatenate([co, co], 1)
        c[:, C_SIN + 64 * tb:C_SIN + 64 * tb + 64] = np.concatenate([-si, si], 1)
    d = np.arange(384)[None, :] - 128 - p[:, None]
    c[:, C_U:C_U + 384] = np.maximum(d, 0)
    c[:, C_L:C_L + 384] = np.maximum(-d, 0)
    h = np.arange(8)
    c[:, C_IS:C_IS + 8] = 2.0 ** (h + 1)
    c[:, C_NS:C_NS + 8] = -(2.0 ** -(h + 1.0))
    return c


def layout(inputs):
    import numpy as np
    a = {k: np.asarray(v) for k, v in inputs.items()}

    def cols(v):
        return v.reshape(-1, 128).T

    def twice(v):
        return np.concatenate([v, v])[:, None]

    gains = np.concatenate([
        cols(a["attn_norm_e"][0]), cols(a["mlp_norm"][0]), cols(a["ret_norm_o"][0]), cols(a["mlp_norm"][1]),
        cols(a["g_in_2"][0]), cols(a["g_mem_2"][0]), cols(a["ret_gn_o"][0]), cols(a["b_merge_2"][0]),
        twice(a["q_norm_a"][0]), twice(a["k_norm_a"][0]), twice(a["q_norm_b"][0]), twice(a["k_norm_b"][0])], 1)
    rowvec = np.concatenate([a["g_final_2"], a["sink_a"][0], a["decay_fwd_o"][0], a["decay_bwd_o"][0]])[None, :]
    rpb = np.full((64, 8, 7, 64), NEG, np.float32)
    for q in range(64):
        k0 = min(max(q - 8, 0), 48)
        rpb[q, :, :, k0:k0 + 16] = a["rpb_b"][0][:, 4:11, k0 - q + 15:k0 - q + 31]
    rpb = rpb.reshape(64, 56, 64)
    return dict(
        x=a["x"], xT=a["x"][0].T, mem=a["mem_2"], memT=a["mem_2"][0].T, gains=gains, rowvec=rowvec, rpb=rpb, consts=shape_constants(),
        w_in_e=a["w_in_e"][0], w_out_e=a["w_out_e"][0], w_in_o=a["w_in_o"][0], w_out_o=a["w_out_o"][0],
        w1_0=a["w_mlp_in"][0], w1_1=a["w_mlp_in"][1], w2_0=a["w_mlp_out"][0], w2_1=a["w_mlp_out"][1],
        w_in_2=a["w_in_2"][0], w_mem=a["w_mem_kv_2"][0], w_up_moba=a["w_up_moba_2"][0],
        w_up_dsa=a["w_up_dsa_2"][0], w_up_cross=a["w_up_cross_2"][0], w_out_2=a["w_out_2"][0])


def kernel(**inputs):
    import numpy as np
    import concourse.bacc as bacc
    from concourse.bass_utils import run_bass_kernel_spmd

    nc = bacc.Bacc("TRN2", target_bir_lowering=False, num_devices=1)
    arrays, args = {}, {}
    for name, a in layout(inputs).items():
        a = np.ascontiguousarray(a)
        arrays[f"in_{name}"] = a
        args[name] = nc.dram_tensor(f"in_{name}", a.shape, mybir.dt.from_np(a.dtype), kind="ExternalInput").ap()
    out = nc.dram_tensor("out", (1, 256, 1024), F32, kind="ExternalOutput").ap()
    program(nc, args, out)
    r = run_bass_kernel_spmd(nc, [arrays], core_ids=[0])
    return r.results[0]["out"]
```
